# Optimizing a Trainium2 kernel written in Bass

```python
import math
import jax
import jax.numpy as jnp
from jax import lax
import numpy as np

D_MODEL = 1024
BATCH = 1
SEQ = 512
DEPTH = 2

N_META = 16
ROPE_THETA = 500000.0
EPS = 1e-6
Q_BLOCK = 128
CHUNK = 128
NEG = -1e30

MLA_HEADS = 8
MLA_NOPE = 64
MLA_ROPE = 32
MLA_QK = MLA_NOPE + MLA_ROPE
MLA_V = 64
MLA_Q_RANK = 384
MLA_KV_RANK = 256

SSD_HEADS = 8
SSD_HEAD_DIM = 64
SSD_INNER = SSD_HEADS * SSD_HEAD_DIM
SSD_GROUPS = 2
SSD_STATE = 64
SSD_CONV = 5
SSD_CONV_CH = SSD_INNER + 2 * SSD_GROUPS * SSD_STATE

DIFF_HEADS = 4
DIFF_QK = 64
DIFF_V = 2 * DIFF_QK
DIFF_ROPE = DIFF_QK // 4

MLSTM_HEADS = 4
MLSTM_QK = 64
MLSTM_V = 128

D_MIX = MLA_HEADS * MLA_V + SSD_INNER + DIFF_HEADS * DIFF_V + MLSTM_HEADS * MLSTM_V
D_FF = -(-8 * D_MODEL // (3 * 256)) * 256

IN_SPLITS = (
    MLA_Q_RANK, MLA_KV_RANK, MLA_ROPE,
    SSD_INNER, SSD_CONV_CH, 2 * SSD_HEADS,
    2 * DIFF_HEADS * DIFF_QK, 2 * DIFF_HEADS * DIFF_QK, DIFF_HEADS * DIFF_V,
    MLSTM_HEADS * MLSTM_QK, MLSTM_HEADS * MLSTM_QK, MLSTM_HEADS * MLSTM_V,
    MLSTM_HEADS * MLSTM_V, 2 * MLSTM_HEADS, 2 * MLSTM_HEADS,
)
IN_COLS = sum(IN_SPLITS)

kernel_name = 'hybrid_mla_ssd_diff_mlstm_encoder'

def rms_norm(x, g):
    xf = x.astype(jnp.float32)
    y = xf * lax.rsqrt(jnp.mean(xf * xf, axis=-1, keepdims=True) + EPS)
    return (y * g.astype(jnp.float32)).astype(x.dtype)

def split_columns(u, sizes):
    out, start = [], 0
    for s in sizes:
        out.append(u[..., start:start + s])
        start += s
    return out

def rope_tables(n_pos, rot_dim):
    inv = 1.0 / (ROPE_THETA ** (jnp.arange(0, rot_dim, 2, dtype=jnp.float32) / rot_dim))
    ang = jnp.arange(n_pos, dtype=jnp.float32)[:, None] * inv[None, :]
    return jnp.cos(ang), jnp.sin(ang)

def apply_partial_rope(x, cos, sin):
    r = cos.shape[-1]
    c = cos[None, :, None, :].astype(x.dtype)
    s = sin[None, :, None, :].astype(x.dtype)
    x1, x2, rest = x[..., :r], x[..., r:2 * r], x[..., 2 * r:]
    return jnp.concatenate([x1 * c - x2 * s, x2 * c + x1 * s, rest], axis=-1)

def softmax_probs(qb, k, scale):
    s = jnp.einsum('bqhd,bkhd->bhqk', qb, k).astype(jnp.float32) * scale
    return jax.nn.softmax(s, axis=-1)

def sweep_query_blocks(attend, q):
    b, t, h, d = q.shape
    n_blk = (t - N_META) // Q_BLOCK
    out_meta = attend(q[:, :N_META])
    q_blocks = jnp.transpose(q[:, N_META:].reshape(b, n_blk, Q_BLOCK, h, d), (1, 0, 2, 3, 4))
    ob = lax.map(attend, q_blocks)
    out_real = jnp.transpose(ob, (1, 0, 2, 3, 4)).reshape((b, n_blk * Q_BLOCK) + ob.shape[3:])
    return jnp.concatenate([out_meta, out_real], axis=1)

def pad_front(u, n, value=0.0):
    return jnp.pad(u, [(0, 0), (n, 0)] + [(0, 0)] * (u.ndim - 2), constant_values=value)

def mla_mixer(c_q, c_kv, k_rope, q_norm_g, kv_norm_g, w_uq, w_ukv, q_head_g, k_head_g, out_g, cos, sin):
    b, t, _ = c_q.shape
    q = (rms_norm(c_q, q_norm_g) @ w_uq).reshape(b, t, MLA_HEADS, MLA_QK)
    kv = (rms_norm(c_kv, kv_norm_g) @ w_ukv).reshape(b, t, MLA_HEADS, MLA_NOPE + MLA_V)
    k_nope, v = kv[..., :MLA_NOPE], kv[..., MLA_NOPE:]
    k_r = jnp.broadcast_to(k_rope[:, :, None, :], (b, t, MLA_HEADS, MLA_ROPE))
    k = jnp.concatenate([k_r, k_nope], axis=-1)
    q = apply_partial_rope(rms_norm(q, q_head_g), cos, sin)
    k = apply_partial_rope(rms_norm(k, k_head_g), cos, sin)
    scale = MLA_QK ** -0.5

    def attend(qb):
        p = softmax_probs(qb, k, scale)
        return jnp.einsum('bhqk,bkhd->bqhd', p.astype(v.dtype), v)

    o = sweep_query_blocks(attend, q).reshape(b, t, MLA_HEADS * MLA_V)
    return rms_norm(o, out_g)

def depthwise_conv_centred(u, w, bias):
    y = lax.conv_general_dilated(
        u, w[:, None, :].astype(u.dtype), window_strides=(1,),
        padding=[(SSD_CONV // 2, SSD_CONV // 2)],
        dimension_numbers=('NWC', 'WIO', 'NWC'), feature_group_count=u.shape[-1])
    return y + bias.astype(u.dtype)

def segsum(a):
    l = a.shape[-1]
    xr = jnp.broadcast_to(a[..., :, None], a.shape + (l,))
    xr = jnp.where(jnp.tril(jnp.ones((l, l), dtype=bool), -1), xr, 0.0)
    out = jnp.cumsum(xr, axis=-2)
    return jnp.where(jnp.tril(jnp.ones((l, l), dtype=bool)), out, -jnp.inf)

def ssd_chunked(x, a, bm, cm):
    b, t, h, p = x.shape
    c = t // CHUNK
    x = x.reshape(b, c, CHUNK, h, p)
    bm = bm.reshape(b, c, CHUNK, h, -1)
    cm = cm.reshape(b, c, CHUNK, h, -1)
    a = jnp.transpose(a.reshape(b, c, CHUNK, h), (0, 3, 1, 2))
    a_cs = jnp.cumsum(a, axis=-1)
    scores = jnp.einsum('bclhn,bcshn->bhcls', cm, bm) * jnp.exp(segsum(a))
    y_diag = jnp.einsum('bhcls,bcshp->bclhp', scores, x)
    decay_states = jnp.transpose(jnp.exp(a_cs[..., -1:] - a_cs), (0, 2, 3, 1))[..., None]
    states = jnp.einsum('bclhn,bclhp->bchpn', bm * decay_states, x)
    states = jnp.concatenate([jnp.zeros_like(states[:, :1]), states], axis=1)
    decay_chunk = jnp.exp(segsum(jnp.pad(a_cs[..., -1], [(0, 0), (0, 0), (1, 0)])))
    states = jnp.einsum('bhzc,bchpn->bzhpn', decay_chunk, states)[:, :-1]
    state_decay = jnp.transpose(jnp.exp(a_cs), (0, 2, 3, 1))[..., None]
    y_off = jnp.einsum('bclhn,bchpn->bclhp', cm, states) * state_decay
    return (y_diag + y_off).reshape(b, t, h, p)

def ssd_direction(xs, dt, a, bm, cm, reverse):
    n_pad = CHUNK - N_META

    def prep(u):
        u = pad_front(u, n_pad)
        return u[:, ::-1] if reverse else u

    heads_per_group = SSD_HEADS // SSD_GROUPS
    y = ssd_chunked(prep(xs * dt[..., None]), prep(dt * a),
                    prep(jnp.repeat(bm, heads_per_group, axis=2)),
                    prep(jnp.repeat(cm, heads_per_group, axis=2)))
    y = y[:, ::-1] if reverse else y
    return y[:, n_pad:]

def ssd_mixer(z, xbc, dt_raw, conv_w, conv_b, dt_bias, a_log, d_skip, norm_g):
    b, t, _ = xbc.shape
    xbc = jax.nn.silu(depthwise_conv_centred(xbc, conv_w, conv_b))
    xs, bm, cm = split_columns(xbc, (SSD_INNER, SSD_GROUPS * SSD_STATE, SSD_GROUPS * SSD_STATE))
    xs = xs.reshape(b, t, SSD_HEADS, SSD_HEAD_DIM)
    bm = bm.reshape(b, t, SSD_GROUPS, SSD_STATE)
    cm = cm.reshape(b, t, SSD_GROUPS, SSD_STATE)
    dt = jax.nn.softplus(dt_raw.reshape(b, t, 2, SSD_HEADS).astype(jnp.float32) + dt_bias.astype(jnp.float32))
    a = -jnp.exp(a_log.astype(jnp.float32))
    y = (ssd_direction(xs, dt[:, :, 0], a[0], bm, cm, False)
         + ssd_direction(xs, dt[:, :, 1], a[1], bm, cm, True)
         + d_skip[None, None, :, None] * xs)
    y = y.reshape(b, t, SSD_INNER)
    return rms_norm(y * jax.nn.silu(z), norm_g)

def diff_mixer(q, k, v, q_head_g, k_head_g, lam, out_g, lambda_init, cos, sin):
    b, t, _ = q.shape
    q = apply_partial_rope(rms_norm(q.reshape(b, t, 2 * DIFF_HEADS, DIFF_QK), q_head_g), cos, sin)
    k = apply_partial_rope(rms_norm(k.reshape(b, t, 2 * DIFF_HEADS, DIFF_QK), k_head_g), cos, sin)
    v = v.reshape(b, t, DIFF_HEADS, DIFF_V)
    lam = lam.astype(jnp.float32)
    lam_full = jnp.exp(jnp.sum(lam[0] * lam[1])) - jnp.exp(jnp.sum(lam[2] * lam[3])) + lambda_init
    scale = DIFF_QK ** -0.5

    def attend(qb):
        p = softmax_probs(qb, k, scale).reshape(b, DIFF_HEADS, 2, qb.shape[1], t)
        amap = p[:, :, 0] - lam_full * p[:, :, 1]
        return jnp.einsum('bhqk,bkhd->bqhd', amap.astype(v.dtype), v)

    o = sweep_query_blocks(attend, q)
    o = rms_norm(o, out_g) * (1.0 - lambda_init)
    return o.reshape(b, t, DIFF_HEADS * DIFF_V)

def mlstm_chunk(carry, inputs):
    c_st, n_st, m_st = carry
    qc, kc, vc, ic, fc = inputs
    ic = jnp.swapaxes(ic, 1, 2)
    fc = jnp.swapaxes(fc, 1, 2)
    bcum = jnp.cumsum(fc, axis=-1)
    causal = jnp.tril(jnp.ones((CHUNK, CHUNK), dtype=bool))
    dmat = jnp.where(causal, bcum[..., :, None] - bcum[..., None, :] + ic[..., None, :], -jnp.inf)
    inter = bcum + m_st[..., None]
    m_row = jnp.maximum(jnp.max(dmat, axis=-1), inter)
    w_intra = jnp.exp(dmat - m_row[..., None])
    w_inter = jnp.exp(inter - m_row)
    s = jnp.einsum('blhd,bshd->bhls', qc, kc).astype(jnp.float32) * w_intra
    num = (jnp.einsum('bhls,bshv->blhv', s, vc)
           + jnp.swapaxes(w_inter, 1, 2)[..., None] * jnp.einsum('bhvd,blhd->blhv', c_st, qc))
    den = jnp.sum(s, axis=-1) + w_inter * jnp.einsum('bhd,blhd->bhl', n_st, qc)
    den = jnp.maximum(jnp.abs(den), jnp.exp(-m_row))
    h = num / jnp.swapaxes(den, 1, 2)[..., None]
    g_last = bcum[..., -1]
    d_last = g_last[..., None] - bcum + ic
    m_new = jnp.maximum(g_last + m_st, jnp.max(d_last, axis=-1))
    w_s = jnp.swapaxes(jnp.exp(d_last - m_new[..., None]), 1, 2)[..., None]
    w_prev = jnp.exp(g_last + m_st - m_new)
    c_new = w_prev[..., None, None] * c_st + jnp.einsum('bshv,bshd->bhvd', vc * w_s, kc)
    n_new = w_prev[..., None] * n_st + jnp.sum(kc * w_s, axis=1)
    return (c_new.astype(jnp.float32), n_new.astype(jnp.float32), m_new.astype(jnp.float32)), h.astype(jnp.float32)

def mlstm_direction(q, k, v, i_log, f_log, reverse):
    n_pad = CHUNK - N_META

    def prep(u, value=0.0):
        u = pad_front(u, n_pad, value)
        return u[:, ::-1] if reverse else u

    qp, kp, vp = prep(q), prep(k), prep(v)
    ip, fp = prep(i_log, NEG), prep(f_log)
    b, t = qp.shape[:2]
    c = t // CHUNK

    def to_chunks(u):
        return jnp.moveaxis(u.reshape((b, c, CHUNK) + u.shape[2:]), 1, 0)

    init = (jnp.zeros((b, MLSTM_HEADS, MLSTM_V, MLSTM_QK), jnp.float32),
            jnp.zeros((b, MLSTM_HEADS, MLSTM_QK), jnp.float32),
            jnp.full((b, MLSTM_HEADS), NEG, jnp.float32))
    _, h = lax.scan(mlstm_chunk, init, (to_chunks(qp), to_chunks(kp), to_chunks(vp), to_chunks(ip), to_chunks(fp)))
    h = jnp.moveaxis(h, 0, 1).reshape(b, t, MLSTM_HEADS, MLSTM_V)
    h = h[:, ::-1] if reverse else h
    return h[:, n_pad:]

def mlstm_mixer(q, k, v, o_raw, i_raw, f_raw, i_bias, f_bias, out_g):
    b, t, _ = q.shape
    q = q.reshape(b, t, MLSTM_HEADS, MLSTM_QK) * (MLSTM_QK ** -0.5)
    k = k.reshape(b, t, MLSTM_HEADS, MLSTM_QK)
    v = v.reshape(b, t, MLSTM_HEADS, MLSTM_V)
    i_log = i_raw.reshape(b, t, 2, MLSTM_HEADS).astype(jnp.float32) + i_bias.astype(jnp.float32)
    f_log = jax.nn.log_sigmoid(f_raw.reshape(b, t, 2, MLSTM_HEADS).astype(jnp.float32) + f_bias.astype(jnp.float32))
    h = (mlstm_direction(q, k, v, i_log[:, :, 0], f_log[:, :, 0], False)
         + mlstm_direction(q, k, v, i_log[:, :, 1], f_log[:, :, 1], True))
    h = rms_norm(h, out_g).reshape(b, t, MLSTM_HEADS * MLSTM_V)
    return jax.nn.sigmoid(o_raw) * h

def setup_inputs(seed: int = 0) -> dict:
    key = jax.random.key(seed)
    ks = iter(jax.random.split(key, 32))
    L = DEPTH

    def nrm(shape, scale):
        return scale * jax.random.normal(next(ks), shape, jnp.float32)

    def gain(shape):
        return 1.0 + 0.02 * jax.random.normal(next(ks), shape, jnp.float32)

    x = nrm((BATCH, SEQ, D_MODEL), 1.0)
    meta_tokens = nrm((N_META, D_MODEL), 1.0)
    attn_norm_g = gain((L, D_MODEL))
    w_in = nrm((L, D_MODEL, IN_COLS), D_MODEL ** -0.5)
    mla_q_norm_g = gain((L, MLA_Q_RANK))
    mla_kv_norm_g = gain((L, MLA_KV_RANK))
    mla_w_uq = nrm((L, MLA_Q_RANK, MLA_HEADS * MLA_QK), MLA_Q_RANK ** -0.5)
    mla_w_ukv = nrm((L, MLA_KV_RANK, MLA_HEADS * (MLA_NOPE + MLA_V)), MLA_KV_RANK ** -0.5)
    mla_q_head_g = gain((L, MLA_QK))
    mla_k_head_g = gain((L, MLA_QK))
    mla_out_g = gain((L, MLA_HEADS * MLA_V))
    ssd_conv_w = nrm((L, SSD_CONV, SSD_CONV_CH), SSD_CONV ** -0.5)
    ssd_conv_b = nrm((L, SSD_CONV_CH), 0.02)
    dt0 = jnp.exp(jax.random.uniform(next(ks), (L, 2, SSD_HEADS), jnp.float32, math.log(1e-3), math.log(1e-1)))
    ssd_dt_bias = dt0 + jnp.log(-jnp.expm1(-dt0))
    ssd_a_log = jnp.log(jax.random.uniform(next(ks), (L, 2, SSD_HEADS), jnp.float32, 1.0, 16.0))
    ssd_d = gain((L, SSD_HEADS))
    ssd_norm_g = gain((L, SSD_INNER))
    diff_q_head_g = gain((L, DIFF_QK))
    diff_k_head_g = gain((L, DIFF_QK))
    diff_lambda = nrm((L, 4, DIFF_QK), 0.1)
    diff_out_g = gain((L, DIFF_V))
    mlstm_i_bias = nrm((L, 2, MLSTM_HEADS), 0.1)
    mlstm_f_bias = 3.0 + nrm((L, 2, MLSTM_HEADS), 0.5)
    mlstm_out_g = gain((L, MLSTM_V))
    w_out = nrm((L, D_MIX, D_MODEL), D_MIX ** -0.5)
    ffn_norm_g = gain((L, D_MODEL))
    w_ffn_in = nrm((L, D_MODEL, 2 * D_FF), D_MODEL ** -0.5)
    w_ffn_out = nrm((L, D_FF, D_MODEL), D_FF ** -0.5)
    return {'x': x, 'meta_tokens': meta_tokens, 'attn_norm_g': attn_norm_g, 'w_in': w_in,
            'mla_q_norm_g': mla_q_norm_g, 'mla_kv_norm_g': mla_kv_norm_g, 'mla_w_uq': mla_w_uq,
            'mla_w_ukv': mla_w_ukv, 'mla_q_head_g': mla_q_head_g, 'mla_k_head_g': mla_k_head_g,
            'mla_out_g': mla_out_g, 'ssd_conv_w': ssd_conv_w, 'ssd_conv_b': ssd_conv_b,
            'ssd_dt_bias': ssd_dt_bias, 'ssd_a_log': ssd_a_log, 'ssd_d': ssd_d, 'ssd_norm_g': ssd_norm_g,
            'diff_q_head_g': diff_q_head_g, 'diff_k_head_g': diff_k_head_g, 'diff_lambda': diff_lambda,
            'diff_out_g': diff_out_g, 'mlstm_i_bias': mlstm_i_bias, 'mlstm_f_bias': mlstm_f_bias,
            'mlstm_out_g': mlstm_out_g, 'w_out': w_out, 'ffn_norm_g': ffn_norm_g,
            'w_ffn_in': w_ffn_in, 'w_ffn_out': w_ffn_out}

def reference(x, meta_tokens, attn_norm_g, w_in, mla_q_norm_g, mla_kv_norm_g, mla_w_uq, mla_w_ukv,
              mla_q_head_g, mla_k_head_g, mla_out_g, ssd_conv_w, ssd_conv_b, ssd_dt_bias, ssd_a_log,
              ssd_d, ssd_norm_g, diff_q_head_g, diff_k_head_g, diff_lambda, diff_out_g,
              mlstm_i_bias, mlstm_f_bias, mlstm_out_g, w_out, ffn_norm_g, w_ffn_in, w_ffn_out):
    b = x.shape[0]
    meta = jnp.broadcast_to(meta_tokens[None].astype(x.dtype), (b, N_META, D_MODEL))
    h = jnp.concatenate([meta, x], axis=1)
    t = h.shape[1]
    cos_d, sin_d = rope_tables(t, DIFF_ROPE)
    cos_m, sin_m = rope_tables(t, MLA_ROPE)
    for l in range(DEPTH):
        lambda_init = 0.8 - 0.6 * math.exp(-0.3 * l)
        hn = rms_norm(h, attn_norm_g[l])
        proj = hn @ w_in[l]
        (c_q, c_kv, k_rope, ssd_z, ssd_xbc, ssd_dt, d_q, d_k, d_v,
         m_q, m_k, m_v, m_o, m_i, m_f) = split_columns(proj, IN_SPLITS)
        y_a = mla_mixer(c_q, c_kv, k_rope, mla_q_norm_g[l], mla_kv_norm_g[l], mla_w_uq[l], mla_w_ukv[l],
                        mla_q_head_g[l], mla_k_head_g[l], mla_out_g[l], cos_m, sin_m)
        y_b = ssd_mixer(ssd_z, ssd_xbc, ssd_dt, ssd_conv_w[l], ssd_conv_b[l], ssd_dt_bias[l],
                        ssd_a_log[l], ssd_d[l], ssd_norm_g[l])
        y_c = diff_mixer(d_q, d_k, d_v, diff_q_head_g[l], diff_k_head_g[l], diff_lambda[l],
                         diff_out_g[l], lambda_init, cos_d, sin_d)
        y_d = mlstm_mixer(m_q, m_k, m_v, m_o, m_i, m_f, mlstm_i_bias[l], mlstm_f_bias[l], mlstm_out_g[l])
        mixed = jnp.concatenate([y_a, y_b, y_c, y_d], axis=-1)
        h = h + mixed @ w_out[l]
        hn = rms_norm(h, ffn_norm_g[l])
        gate, up = jnp.split(hn @ w_ffn_in[l], 2, axis=-1)
        h = h + (jax.nn.silu(gate) * up) @ w_ffn_out[l]
    return h[:, N_META:].astype(x.dtype)


_drawn_inputs = setup_inputs


def setup_inputs(seed=0):
    import zlib

    import numpy as np

    out = dict(_drawn_inputs(seed))
    spreads = {}
    factors = {'mla_q_norm_g': 5.51,
     'mla_kv_norm_g': 3.461,
     'mla_q_head_g': 5.41,
     'mla_k_head_g': 5.754,
     'mla_out_g': 4.528,
     'ssd_conv_b': 3.108,
     'ssd_d': 8.0,
     'ssd_norm_g': 5.108,
     'diff_q_head_g': 7.365,
     'diff_k_head_g': 7.886,
     'diff_lambda': 2.809,
     'diff_out_g': 6.072,
     'mlstm_i_bias': 8.0,
     'mlstm_out_g': 8.0,
     'ffn_norm_g': 3.221}
    for name, (base, spread) in spreads.items():
        noise = np.random.default_rng([zlib.crc32(name.encode()), seed]).standard_normal(out[name].shape)
        drawn = base * np.exp(spread * noise) if base else spread * noise
        out[name] = jnp.asarray(drawn.astype(out[name].dtype))
    for name, factor in factors.items():
        out[name] = (out[name] * factor).astype(out[name].dtype)
    return out
```

```python
from contextlib import ExitStack

import numpy as np
import concourse.bass as bass
from concourse import mybir

FP32 = mybir.dt.float32
ALU = mybir.AluOpType
ACT = mybir.ActivationFunctionType
AX = mybir.AxisListType

DEPTH, D_MODEL, N_META, SEQ = 2, 1024, 16, 512
EPS, NEG = 1e-6, -1e30
P = 128
T = N_META + SEQ
HALF = T // 2
KD = D_MODEL // P
TILES = [(i * P, min(P, T - i * P)) for i in range(-(-T // P))]
NT = len(TILES)
WIDE = NT * P

MLA_H, MLA_NOPE, MLA_ROPE, MLA_V = 8, 64, 32, 64
MLA_QK = MLA_NOPE + MLA_ROPE
Q_RANK, KV_RANK = 384, 256
SSD_H, SSD_P, SSD_G, SSD_N, TAPS = 8, 64, 2, 64, 5
DIFF_H, DIFF_QK, DIFF_V, DIFF_ROPE = 4, 64, 128, 16
ML_H, ML_QK, ML_V = 4, 64, 128
D_FF = 2816
KF = D_FF // P
KM = 16

XS, BM, CM, ZT, MISC, MO, CQ, CKV, DQ, DK, DV, MQ, MK, MV = 0, 4, 5, 6, 10, 11, 15, 18, 20, 24, 28, 32, 34, 36
N_IN = 40
S_UV, S_UQ, S_UK = N_IN, N_IN + 1, N_IN + 4
S_OUT = N_IN + 5
S_FIN = S_OUT + 2 * KD
S_FOUT = S_FIN + 2 * KF
N_SLOT = S_FOUT + 3 * KD
SLOT = KD * P
RING = 7
UQ_HEADS = 3
G_OUT, G_FIN, G_FOUT = N_IN, N_IN + KD, N_IN + KD + 2 * KF
N_GROUP = G_FOUT + KD

NDEC = 2 * SSD_H + 2 * ML_H
C_ML, C_DT, C_NM = 2 * SSD_H, NDEC, NDEC + 2 * SSD_H
NCOL = C_NM + 2 * ML_H


def layout(fields):
    at, out = 0, {}
    for name, n in fields:
        out[name] = (at, at + n)
        at += n
    return out, at


CONST, N_CONST = layout([("ones", P), ("ident", P), ("mask", 6 * P), ("ones_h", P), ("perm_d", P), ("perm_m", P), ("cos_d", T), ("sin_d", T),
                         ("cos_m", T), ("sin_m", T), ("rowsel", NDEC), ("lin_rs", NCOL), ("lin_i", NCOL), ("lin_sp", NCOL),
                         ("sign", 1)])
PARAM, N_PARAM = layout([("attn_g", KD), ("ffn_g", KD), ("q_g", 3), ("kv_g", 2), ("qh_g", 1), ("kh_g", 1), ("mla_out_g", 4),
                         ("conv_w", 6 * TAPS), ("conv_b", 6), ("ssd_g", 4), ("ssd_d", SSD_H), ("dq_g", 1), ("dk_g", 1),
                         ("diff_out_g", 1), ("ml_out_g", 1), ("bias", 1), ("a_log", 1), ("i_bias", 1), ("lam", 4 * DIFF_QK),
                         ("lambda_init", 2)])

STEPS_SSD, STEPS_ML, STEPS = 2 * SSD_H * NT, 2 * ML_H * NT, 2 * (SSD_H + ML_H) * NT
N_ATT_M = MLA_H * NT
N_ATT = N_ATT_M + 2 * DIFF_H * NT
SQ_A, SQ_B, SQ_S, SQ_M, SQ_F = 0, KD, KD + 13, KD + 17, KD + 17 + 2 * MLA_H
N_SQ = SQ_F + KD
RS_A, RS_B, RS_S, RS_M, RS_F = 0, 1, 11, 12, 12 + 2 * MLA_H
N_RS = RS_F + 1
TR_X, TR_OS, TR_MV, TR_OM, TR_DV, TR_OA, TR_OD = range(0, 7 * NT, NT)


class Signal:

    def __init__(self, sem, per):
        self.sem, self.per = sem, per

    def at(self, layer, k):
        return layer * self.per + k


def trunk(nc, x_t, w_stream, params, consts, out):
    ctx = ExitStack()
    with ctx:
        def sb(name, shape):
            return ctx.enter_context(nc.sbuf_tensor(name, shape, FP32))

        def signal(name, per):
            return Signal(ctx.enter_context(nc.semaphore(name)), per)

        h = sb("h", [P, KD, T])
        proj = sb("proj", [P, N_IN * T])
        mix = sb("mix", [P, KM * T])
        ring = sb("ring", [P, RING, SLOT])
        o_tok = sb("o_tok", [P, NT, 512])
        sq = sb("sq", [P, 2, T])
        rstd = sb("rstd", [P, T])
        rstd2 = sb("rstd2", [P, T])
        ebuf = sb("ebuf", [P, 2, T])
        mbuf = sb("mbuf", [P, 2, WIDE])
        qh = sb("qh", [P, 2, WIDE])
        kh = sb("kh", [P, 2, T])
        rows = sb("rows", [P, T])
        cols = sb("cols", [P, NT, NCOL])
        enm = sb("enm", [P, NT, 2 * ML_H])
        con = sb("con", [P, N_CONST])
        par = sb("par", [P, DEPTH, N_PARAM])
        sums = sb("sums", [P, 4])
        negmax = sb("negmax", [P, 2])
        rowmax = sb("rowmax", [P, 2])
        rsum = sb("rsum", [P, 2])
        ea = sb("ea", [P, 1])
        lam_p = sb("lam_p", [P, 2, DIFF_QK])
        lam_s = sb("lam_s", [P, 2])
        lam_e = sb("lam_e", [P, 2])
        neg_lam = sb("neg_lam", [P, 1])
        gain_d = sb("gain_d", [P, 1])
        eps = sb("eps", [P, 1])
        den = sb("den", [P, NT])
        den2 = sb("den2", [P, NT])
        hs = sb("hs", [P, 4 * NT])
        pb = ctx.enter_context(nc.psum_tensor("pb", [P, 8, 512], FP32))

        def C(name, rows_=slice(0, P)):
            return con[rows_, CONST[name][0]:CONST[name][1]]

        def par_at(layer, name, i=0, n=1, rows_=slice(0, P)):
            a = PARAM[name][0] + i
            return par[rows_, layer, a:a + n]

        def tile_of(buf, k, a=0, b=T, rows_=slice(0, P)):
            return buf[rows_, k * T + a:k * T + b]

        def halves(ap):
            return ap.rearrange("p (a b) -> p a b", b=HALF)

        def pair(p, rows_=slice(0, P)):
            return pb[rows_, 2 * p:2 * p + 2, 0:HALF]

        def span(p, width, rows_):
            return pair(p, rows_) if width == T else pb[rows_, 2 * p, 0:width]

        def like(ap, width):
            return halves(ap) if width == T else ap

        def token_major(buf, tile0):
            return buf[:, tile0 * T:tile0 * T + NT * 512].rearrange("p (i f) -> p i f", f=512)

        x_tok = token_major(mix, 8)
        v_ml = proj[:, 0:NT * ML_H * (ML_V + 1)].rearrange("p (i h v) -> p i h v", h=ML_H, v=ML_V + 1)
        o_ml = token_major(proj, 5)
        v_mla = token_major(proj, 0)
        v_dif = token_major(proj, 5)
        o_dif = token_major(proj, 32)

        def cb(g, j, a, b, rows_):
            return tile_of(mix, 4 * g + j, a, b, rows_) if j < 4 else tile_of(mix, 13 + g, a, b, rows_)

        def rng(d, j):
            return (TILES[j][0], T) if d == 0 else (0, TILES[j][0] + TILES[j][1])

        def mask(d, j):
            a = 0 if d == 0 else P + (NT - 1) * P - TILES[j][0]
            lo, hi = rng(d, j)
            c = CONST["mask"][0] + a
            return con[0:TILES[j][1], c:c + hi - lo]

        def unit(u):
            if u < 2 * SSD_H:
                return u // 2, u % 2, (u % 2) * SSD_H + u // 2
            v = u - 2 * SSD_H
            return v // 2, v % 2, 2 * SSD_H + (v % 2) * ML_H + v // 2

        def att(n):
            if n < N_ATT_M:
                hd, i = n // NT, n % NT
                return (qh[0:MLA_QK, hd % 2, i * P:(i + 1) * P], kh[0:MLA_QK, hd % 2, :],
                        lambda j: v_mla[0:TILES[j][1], j, hd * MLA_V:(hd + 1) * MLA_V], MLA_V, MLA_QK ** -0.5, i, hd)
            hd, i = (n - N_ATT_M) // NT, (n - N_ATT_M) % NT
            r = slice(64 * (hd % 2), 64 * (hd % 2) + 64)
            return (tile_of(proj, DQ + hd // 2, i * P, (i + 1) * P, r), tile_of(proj, DK + hd // 2, rows_=r),
                    lambda j: v_dif[0:TILES[j][1], j, (hd // 2) * DIFF_V:(hd // 2 + 1) * DIFF_V], DIFF_V, DIFF_QK ** -0.5, i, hd)

        TURN, TAIL_O = 4, 5
        JOBS = [([CQ, CQ + 1, CQ + 2], Q_RANK, "q_g"), ([CKV, CKV + 1], KV_RANK, "kv_g")]
        JOBS += [([DQ + t], DIFF_QK, "dq_g" if t < 4 else "dk_g") for t in range(8)]
        JOB_G = CKV + 3
        JOB_SQ = [0, 3, 5] + [6 + t for t in range(7)]

        LAST_OF_SLOT = {2 * min(UQ_HEADS * c + UQ_HEADS - 1, MLA_H - 1): S_UQ + c + 1 for c in range(3)}
        LAST_OF_SLOT[2 * MLA_H - 1] = S_UK + 1

        def projected(layer, e):
            if e in LAST_OF_SLOT:
                return w_used.sem, w_used.at(layer, LAST_OF_SLOT[e])
            return p_ps.sem, p_ps.at(layer, sum(x not in LAST_OF_SLOT for x in range(e + 1)))

        const_in = signal("const_in", 0)
        table_in = signal("table_in", 0)
        eps_ready = signal("eps_ready", 0)
        par_in = signal("par_in", 0)
        x_in = [signal(f"x_in{k}", 0) for k in range(KD)]
        cleared = signal("cleared", 0)
        loaded = [signal(f"loaded{s}", 0) for s in range(RING)]
        w_used = signal("w_used", N_SLOT)
        evac = signal("evac", N_GROUP)
        xg_ready = signal("xg_ready", 2 * KD)
        sq_ready = signal("sq_ready", N_SQ)
        sq_used = signal("sq_used", N_SQ)
        rs_ready = signal("rs_ready", N_RS)
        rs_used = signal("rs_used", len(JOBS) + 1 + 2 * MLA_H)
        conv_ready = signal("conv_ready", 6)
        conv_act = signal("conv_act", 6)
        z_act = signal("z_act", 4)
        o_tanh = signal("o_tanh", 4)
        o_sig = signal("o_sig", 4)
        dec_u = signal("dec_u", 1)
        dec_ln = signal("dec_ln", 1)
        rows_ready = signal("rows_ready", 1)
        cols_ps = signal("cols_ps", 1)
        cols_ready = signal("cols_ready", 1)
        enm_ready = signal("enm_ready", 1)
        rot_ready = signal("rot_ready", 8 + 2 * MLA_H)
        roped = signal("roped", 8 + 2 * MLA_H)
        qcos = signal("qcos", 8)
        tr_ready = signal("tr_ready", 7 * NT)
        tr_evac = signal("tr_evac", 7 * NT)
        cb_ps = signal("cb_ps", 2 * NT)
        cb_ready = signal("cb_ready", 2 * NT)
        rowb = signal("rowb", 2 * (SSD_H + ML_H))
        e_raw = signal("e_raw", STEPS)
        e_exp = signal("e_exp", STEPS)
        m_ready = signal("m_ready", STEPS)
        m_used = signal("m_used", STEPS)
        qk_ps = signal("qk_ps", STEPS_ML)
        y_evac = signal("y_evac", SSD_H)
        nd_evac = signal("nd_evac", 2 * ML_H)
        osq = signal("osq", 3 * NT)
        ored = signal("ored", 3 * NT)
        orstd = signal("orstd", 3)
        oscaled = signal("oscaled", 3 * NT)
        v_ps = signal("v_ps", NT - 1)
        v_ready = signal("v_ready", NT)
        p_ps = signal("p_ps", 2 * MLA_H - len(LAST_OF_SLOT))
        p_copy = signal("p_copy", 2 * MLA_H)
        s_ps = signal("s_ps", N_ATT)
        max_ready = signal("max_ready", N_ATT)
        p_ready = signal("p_ready", N_ATT)
        t_ps = signal("t_ps", N_ATT)
        tail_ps = signal("tail_ps", N_ATT)
        pt_main = signal("pt_main", N_ATT)
        pt_tail = signal("pt_tail", N_ATT)
        o_ps = signal("o_ps", N_ATT)
        o_evac = signal("o_evac", N_ATT)
        lam_sum = signal("lam_sum", 1)
        lam_exp = signal("lam_exp", 1)
        gsilu = signal("gsilu", KF)
        act_ready = signal("act_ready", KF)
        stored = signal("stored", 0)
        dve_chain = signal("dve_chain", 0)
        act_chain = signal("act_chain", 0)

        block = ctx.enter_context(nc.Block())

        @block.sync
        def _(sp):
            for k in range(KD):
                sp.dma_start(h[:, k, :], x_t[:, k, :]).then_inc(x_in[k].sem, 16)
                if k == 0:
                    sp.dma_start(par[:, :, :], params).then_inc(par_in.sem, 16)
                    sp.dma_start(con[:, 0:2 * P], consts[:, 0:2 * P]).then_inc(const_in.sem, 16)
            for n in range(DEPTH * N_SLOT):
                if n == RING:
                    sp.dma_start(con[:, 2 * P:N_CONST], consts[:, 2 * P:N_CONST]).then_inc(table_in.sem, 16)
                if n >= RING:
                    sp.wait_ge(w_used.sem, n - RING + 1)
                sp.dma_start(ring[:, n % RING, :], w_stream[n, :, :]).then_inc(loaded[n % RING].sem, 16)
            for k in range(KD):
                sp.wait_ge(evac.sem, evac.at(DEPTH - 1, G_FOUT + k + 1))
                sp.dma_start(out[:, k, :], h[:, k, N_META:T]).then_inc(stored.sem, 16)
            sp.wait_ge(stored.sem, 16 * KD)

        @block.gpsimd
        def _(pool):
            nc.gpsimd.memset(mix[:, :], 0.0).then_inc(cleared.sem, 1)
            nc.gpsimd.memset(mbuf[:, :, :], 0.0).then_inc(cleared.sem, 1)
            nc.gpsimd.memset(qh[:, :, :], 0.0).then_inc(cleared.sem, 1)
            nc.gpsimd.memset(cols[:, :, :], 0.0).then_inc(cleared.sem, 1)
            nc.gpsimd.memset(rows[:, :], 0.0).then_inc(cleared.sem, 1)
            nc.gpsimd.memset(o_tok[:, :, :], 0.0).then_inc(cleared.sem, 1)
            pool.wait_ge(table_in.sem, 16)
            for l in range(DEPTH):
                for f in range(4):
                    pool.wait_ge(o_tanh.sem, o_tanh.at(l, f + 1))
                    nc.gpsimd.tensor_scalar(tile_of(proj, MO + f), tile_of(proj, MO + f), 0.5, 0.5,
                                            ALU.mult, ALU.add).then_inc(o_sig.sem, 1)
                for t in range(8):
                    pool.wait_ge(rs_used.sem, rs_used.at(l, 2 + t + 1))
                    pool.wait_ge(rot_ready.sem, rot_ready.at(l, t + 1))
                    nc.gpsimd.tensor_tensor(tile_of(proj, DQ + t), tile_of(proj, DQ + t), C("cos_d"),
                                            ALU.mult).then_inc(qcos.sem, 1)

        @block.tensor
        def _(pe):
            def slot_ready(l, s):
                n = l * N_SLOT + s
                pe.wait_ge(loaded[n % RING].sem, 16 * (n // RING + 1))
                return ring[:, n % RING, :]

            def product(p, lhs_t, rhs, start, stop, rows_=slice(0, P)):
                for a in range(2):
                    last = nc.tensor.matmul(pb[rows_, 2 * p + a, 0:HALF], lhs_t, rhs[:, a * HALF:(a + 1) * HALF],
                                            start=start, stop=stop)
                return last

            def norm_sum(l, s0, n, p, rows_=slice(0, P), stops=True, starts=True, ones="ones"):
                for k in range(n):
                    pe.wait_ge(sq_ready.sem, sq_ready.at(l, s0 + k + 1))
                    product(p, C(ones, rows_), sq[rows_, (s0 + k) % 2, :], starts and k == 0, stops and k == n - 1).then_inc(sq_used.sem, 1)

            def dense(l, g, slots, rhs_tile, hook=None):
                p = 1 + g % 3
                pe.wait_ge(evac.sem, evac.at(l, max(g - 2, 0)))
                k_all = sum(n for _, n in slots)
                k = 0
                for s, n in slots:
                    w = slot_ready(l, s)
                    for c in range(n):
                        last = product(p, w[:, c * P:(c + 1) * P], rhs_tile(k), k == 0, k == k_all - 1)
                        if hook:
                            hook(k)
                        k += 1
                    last.then_inc(w_used.sem, 1)

            def row_bcast(l, u, p):
                if u < 2 * SSD_H:
                    pe.wait_ge(e_raw.sem, e_raw.at(l, max(u - 1, 0) * NT))
                else:
                    pe.wait_ge(e_raw.sem, e_raw.at(l, u * NT))
                r = C("rowsel")[:, unit(u)[2]:unit(u)[2] + 1].to_broadcast([P, P])
                product(p, r, rows, True, True).then_inc(rowb.sem, 1)

            def out_transposes(l, idx, src, i):
                b = 4 + idx % 2
                pe.wait_ge(tr_evac.sem, tr_evac.at(l, max(idx - 1, 0)))
                for f in range(4):
                    last = src(b, f, i)
                last.then_inc(tr_ready.sem, 1)

            def to_tokens(tile0):
                def one(b, f, i):
                    a, w = TILES[i]
                    return nc.tensor.transpose(pb[0:w, b, f * P:(f + 1) * P], tile_of(proj, tile0 + f, a, a + w), C("ident"))
                return one

            def to_features(buf):
                def one(b, f, i):
                    w = TILES[i][1]
                    return nc.tensor.transpose(pb[:, b, f * P:f * P + w], buf[0:w, i, f * P:(f + 1) * P],
                                               C("ident")[0:w, 0:w])
                return one

            pe.wait_ge(const_in.sem, 16)
            pe.wait_ge(cleared.sem, 6)
            for l in range(DEPTH):
                pe.wait_ge(evac.sem, evac.at(l, 0))
                norm_sum(l, SQ_A, KD, 0)

                def job_hook(g):
                    def hook(k):
                        q = g - JOB_G
                        if not 0 <= q < len(JOBS):
                            return
                        if k == 3:
                            pe.wait_ge(rs_ready.sem, rs_ready.at(l, RS_B + q))
                            pe.wait_ge(roped.sem, roped.at(l, max(q - 2, 0)))
                            norm_sum(l, SQ_B + JOB_SQ[q], len(JOBS[q][0]), 0, ones="ones" if q < 2 else "ones_h")
                        if k == 7 and q >= 2:
                            pe.wait_ge(rs_used.sem, rs_used.at(l, q + 1))
                            product(0, C("perm_d"), tile_of(proj, DQ + q - 2), True, True).then_inc(rot_ready.sem, 1)
                    return hook

                for k in range(KD):
                    pe.wait_ge(xg_ready.sem, xg_ready.at(l, k + 1))
                for g in range(N_IN):
                    dense(l, g, [(g, KD)], lambda k: tile_of(mix, k), job_hook(g))

                pe.wait_ge(evac.sem, evac.at(l, N_IN))
                pe.wait_ge(rows_ready.sem, rows_ready.at(l, 1))
                pe.wait_ge(roped.sem, roped.at(l, 8))
                for i, (a, w) in enumerate(TILES):
                    o = pb[0:w, 7, i * NCOL:(i + 1) * NCOL]
                    nc.tensor.matmul(o, rows[:, a:a + w], C("lin_rs"), start=True, stop=False)
                    nc.tensor.matmul(o, qh[0:NDEC, 0, a:a + w], C("lin_i", slice(0, NDEC)), start=False, stop=False)
                    last = nc.tensor.matmul(o, mbuf[0:NDEC, 1, a:a + w], C("lin_sp", slice(0, NDEC)), start=False, stop=True)
                last.then_inc(cols_ps.sem, 1)

                pe.wait_ge(conv_act.sem, conv_act.at(l, 6))
                for i in range(NT):
                    out_transposes(l, TR_X + i, to_tokens(XS), i)
                row_bcast(l, 0, 0)
                row_bcast(l, 1, 1)
                for g in range(SSD_G):
                    r = slice(64 * g, 64 * g + 64)
                    for j, (a, w) in enumerate(TILES):
                        pe.wait_ge(tr_evac.sem, tr_evac.at(l, TR_X + NT))
                        pe.wait_ge(cb_ready.sem, cb_ready.at(l, g * NT + j))
                        product(2, tile_of(proj, BM, a, a + w, r), tile_of(proj, CM, rows_=r), True, True,
                                slice(0, w)).then_inc(cb_ps.sem, 1)
                pe.wait_ge(cols_ready.sem, cols_ready.at(l, 1))
                for u in range(2 * SSD_H):
                    hd, d, _ = unit(u)
                    if d == 0:
                        pe.wait_ge(y_evac.sem, y_evac.at(l, max(hd - 1, 0)))
                    for j, (_, kw) in enumerate(TILES):
                        n = u * NT + j
                        pe.wait_ge(m_ready.sem, m_ready.at(l, n + 1))
                        blocks = range(j, NT) if d == 0 else range(j + 1)
                        lo = rng(d, j)[0]
                        for i in blocks:
                            last = nc.tensor.matmul(pb[:, 6 + hd % 2, i * SSD_P:(i + 1) * SSD_P],
                                                    mbuf[0:kw, n % 2, i * P - lo:i * P - lo + P],
                                                    x_tok[0:kw, j, hd * SSD_P:(hd + 1) * SSD_P],
                                                    start=(d == 0 and j == 0 and i == 0), stop=(d == 1 and j == NT - 1),
                                                    skip_group_check=True)
                        last.then_inc(m_used.sem, 1)
                    if u + 2 < 2 * SSD_H:
                        row_bcast(l, u + 2, u % 2)

                pe.wait_ge(y_evac.sem, y_evac.at(l, SSD_H))
                for i in range(NT):
                    out_transposes(l, TR_OS + i, to_features(o_tok), i)
                for i in range(NT):
                    out_transposes(l, TR_MV + i, to_tokens(MV), i)
                norm_sum(l, SQ_S, 4, 3)

                def qk(n):
                    u, j = 2 * SSD_H + n // NT, n % NT
                    hd, d, _ = unit(u)
                    a, w = TILES[j]
                    lo, hi = rng(d, j)
                    r = slice(64 * (hd % 2), 64 * (hd % 2) + 64)
                    k_t = tile_of(proj, MK + hd // 2, a, a + w, r)
                    q_t = tile_of(proj, MQ + hd // 2, rows_=r)
                    if hi - lo == T:
                        product(1, k_t, q_t, True, True, slice(0, w)).then_inc(qk_ps.sem, 1)
                    else:
                        nc.tensor.matmul(pb[0:w, 2, 0:hi - lo], k_t, q_t[:, lo:hi], start=True, stop=True).then_inc(qk_ps.sem, 1)

                row_bcast(l, 2 * SSD_H, 0)
                qk(0)
                pe.wait_ge(tr_evac.sem, tr_evac.at(l, TR_MV + NT))
                pe.wait_ge(rs_ready.sem, rs_ready.at(l, RS_S + 1))
                for n in range(STEPS_ML):
                    v, j = n // NT, n % NT
                    hd, d, _ = unit(2 * SSD_H + v)
                    if j == 0:
                        pe.wait_ge(nd_evac.sem, nd_evac.at(l, max(v - 1, 0)))
                    if j == NT - 1 and v + 1 < 2 * ML_H:
                        row_bcast(l, 2 * SSD_H + v + 1, 0)
                    pe.wait_ge(m_ready.sem, m_ready.at(l, STEPS_SSD + n + 1))
                    if n + 1 < STEPS_ML:
                        qk(n + 1)
                    kw = TILES[j][1]
                    lo = rng(d, j)[0]
                    for i in (range(j, NT) if d == 0 else range(j + 1)):
                        first = (j == 0 and i in (0, 3)) if d == 0 else (i, j) in ((0, 0), (3, 3))
                        c = (i % 3) * (ML_V + 1)
                        last = nc.tensor.matmul(pb[:, 4 + 2 * (v % 2) + i // 3, c:c + ML_V + 1],
                                                mbuf[0:kw, (STEPS_SSD + n) % 2, i * P - lo:i * P - lo + P],
                                                v_ml[0:kw, j, hd, :], start=first, stop=(j == NT - 1), skip_group_check=True)
                    last.then_inc(m_used.sem, 1)

                w = slot_ready(l, S_UV)
                pe.wait_ge(nd_evac.sem, nd_evac.at(l, 2 * ML_H))
                for i, (a, wd) in enumerate(TILES):
                    pe.wait_ge(v_ready.sem, v_ready.at(l, max(i - 1, 0)))
                    for c in range(2):
                        last = nc.tensor.matmul(pb[0:wd, 6 + i % 2, 0:512], tile_of(proj, CKV + c, a, a + wd),
                                                w[:, c * 512:(c + 1) * 512], start=(c == 0), stop=(c == 1))
                    if i < NT - 1:
                        last.then_inc(v_ps.sem, 1)
                    else:
                        last.then_inc(w_used.sem, 1)
                pe.wait_ge(v_ready.sem, v_ready.at(l, NT))

                def prep(stage, hd):
                    side, what = stage // 3, stage % 3
                    e = 2 * hd + side
                    rws = slice(0, MLA_QK)
                    if what == 0:
                        pe.wait_ge(roped.sem, roped.at(l, 8 + e))
                        pe.wait_ge(rs_ready.sem, rs_ready.at(l, RS_M + e))
                        if side == 0:
                            s = S_UQ + hd // UQ_HEADS
                            w, m, n, t0 = slot_ready(l, s), MLA_QK, 3, CQ
                            o = (hd % UQ_HEADS) * 3 * MLA_QK
                        else:
                            w, m, n, t0 = slot_ready(l, S_UK), MLA_NOPE, 2, CKV
                            o = hd * 2 * MLA_NOPE
                        for c in range(n):
                            last = product(3, w[:, o + c * m:o + (c + 1) * m], tile_of(proj, t0 + c), c == 0, c == n - 1,
                                           slice(0, m))
                        if e in LAST_OF_SLOT:
                            last.then_inc(w_used.sem, 1)
                        else:
                            last.then_inc(p_ps.sem, 1)
                    elif what == 1:
                        pe.wait_ge(p_copy.sem, p_copy.at(l, e + 1))
                        norm_sum(l, SQ_M + e, 1, 3, rws)
                    else:
                        pe.wait_ge(rs_used.sem, rs_used.at(l, 11 + e + 1))
                        product(3, C("perm_m", rws)[:, 0:MLA_QK], (qh, kh)[side][rws, hd % 2, 0:T], True, True,
                                rws).then_inc(rot_ready.sem, 1)

                def scores(n):
                    q, k, _, _, _, i, hd = att(n)
                    pe.wait_ge(p_ready.sem, p_ready.at(l, max(n - 1, 0)))
                    if n < N_ATT_M and i == 0:
                        pe.wait_ge(roped.sem, roped.at(l, 8 + 2 * hd + 2))
                    product(n % 2, q, k, True, True).then_inc(s_ps.sem, 1)

                def turn(n):
                    pe.wait_ge(p_ready.sem, p_ready.at(l, n + 1))
                    pe.wait_ge(o_evac.sem, o_evac.at(l, max(n - 1, 0)))
                    pe.wait_ge(pt_tail.sem, pt_tail.at(l, n))
                    a, w = TILES[-1]
                    nc.tensor.transpose(pb[0:w, TAIL_O, 0:P], ebuf[:, n % 2, a:a + w], C("ident")).then_inc(tail_ps.sem, 1)
                    pe.wait_ge(pt_main.sem, pt_main.at(l, n))
                    for j, (a, w) in enumerate(TILES[:-1]):
                        last = nc.tensor.transpose(pb[:, TURN, j * P:(j + 1) * P], ebuf[:, n % 2, a:a + w], C("ident"))
                    last.then_inc(t_ps.sem, 1)

                def values(n):
                    _, _, v, dv, _, _, _ = att(n)
                    pe.wait_ge(pt_main.sem, pt_main.at(l, n + 1))
                    pe.wait_ge(pt_tail.sem, pt_tail.at(l, min(n + 2, N_ATT_M if n < N_ATT_M else N_ATT)))
                    pe.wait_ge(o_evac.sem, o_evac.at(l, n))
                    for j, (_, w) in enumerate(TILES):
                        last = nc.tensor.matmul(pb[:, TAIL_O, P:P + dv], mbuf[0:w, n % 2, j * P:(j + 1) * P],
                                                v(j), start=(j == 0), stop=(j == NT - 1))
                    last.then_inc(o_ps.sem, 1)

                for s in range(6):
                    prep(s, 0)
                for i in range(NT):
                    pe.wait_ge(oscaled.sem, oscaled.at(l, i + 1))
                    out_transposes(l, TR_OM + i, to_features(o_ml), i)
                pe.wait_ge(tr_evac.sem, tr_evac.at(l, TR_OM + NT))
                scores(0)
                for n in range(N_ATT_M):
                    hd, i = n // NT, n % NT
                    if n + 1 < N_ATT_M:
                        scores(n + 1)
                    if hd + 1 < MLA_H and i in (0, 1, 2, 3):
                        prep((0, 1, 3, 4)[i], hd + 1)
                    turn(n)
                    if n >= 1:
                        values(n - 1)
                    if hd + 1 < MLA_H and i in (1, 3):
                        prep((None, 2, None, 5)[i], hd + 1)
                values(N_ATT_M - 1)

                pe.wait_ge(o_evac.sem, o_evac.at(l, N_ATT_M))
                for i in range(NT):
                    out_transposes(l, TR_DV + i, to_tokens(DV), i)
                for i in range(NT):
                    pe.wait_ge(oscaled.sem, oscaled.at(l, NT + i + 1))
                    out_transposes(l, TR_OA + i, to_features(o_tok), i)
                pe.wait_ge(tr_evac.sem, tr_evac.at(l, TR_OA + NT))
                scores(N_ATT_M)
                for n in range(N_ATT_M, N_ATT):
                    if n + 1 < N_ATT:
                        scores(n + 1)
                    turn(n)
                    if n > N_ATT_M:
                        values(n - 1)
                values(N_ATT - 1)
                pe.wait_ge(o_evac.sem, o_evac.at(l, N_ATT))
                for i in range(NT):
                    pe.wait_ge(oscaled.sem, oscaled.at(l, 2 * NT + i + 1))
                    out_transposes(l, TR_OD + i, to_features(o_dif), i)

                pe.wait_ge(tr_evac.sem, tr_evac.at(l, TR_OD + NT))
                pe.wait_ge(rs_used.sem, rs_used.at(l, 11))
                pe.wait_ge(p_ready.sem, p_ready.at(l, N_ATT))
                for g in range(KD):
                    dense(l, G_OUT + g, [(S_OUT + 2 * g, KD), (S_OUT + 2 * g + 1, KD)], lambda k: tile_of(mix, k))
                    if g >= 1:
                        norm_sum(l, SQ_F + g - 1, 1, 0, starts=(g == 1), stops=False)
                norm_sum(l, SQ_F + KD - 1, 1, 0, starts=False)

                for k in range(KD):
                    pe.wait_ge(xg_ready.sem, xg_ready.at(l, KD + k + 1))
                for g in range(2 * KF):
                    dense(l, G_FIN + g, [(S_FIN + g, KD)], lambda k: tile_of(proj, 32 + k))
                pe.wait_ge(act_ready.sem, act_ready.at(l, KF))
                for g in range(KD):
                    s = S_FOUT + 3 * g
                    dense(l, G_FOUT + g, [(s, KD), (s + 1, KD), (s + 2, KF - 2 * KD)], lambda k: tile_of(proj, k))

        @block.scalar
        def _(act):
            chained = [0]

            def link(ins):
                chained[0] += 1
                ins.then_inc(act_chain.sem, 1)
                act.wait_ge(act_chain.sem, chained[0])

            def square(l, s, src, rows_=slice(0, P)):
                act.wait_ge(sq_used.sem, sq_used.at(l, max(s - 1, 0)))
                nc.scalar.activation(halves(sq[rows_, s % 2, :]), src, ACT.Square).then_inc(sq_ready.sem, 1)

            def rsqrt(l, s, p, n, dst, rows_=slice(0, P)):
                act.wait_ge(sq_used.sem, sq_used.at(l, s))
                link(nc.scalar.activation(halves(dst[rows_, :]), pair(p, rows_), ACT.Ln, scale=1.0 / n, bias=eps[rows_, :]))
                nc.scalar.activation(dst[rows_, :], dst[rows_, :], ACT.Exp, scale=-0.5).then_inc(rs_ready.sem, 1)

            def exps(l, n):
                u, j = n // NT, n % NT
                lo, hi = rng(unit(u)[1], j)
                e = ebuf[0:TILES[j][1], n % 2, 0:hi - lo]
                act.wait_ge(e_raw.sem, e_raw.at(l, n + 1))
                nc.scalar.activation(e, e, ACT.Exp).then_inc(e_exp.sem, 1)

            def out_squares(l, base, buf, width_rows=None):
                for i in range(NT):
                    if i >= 2:
                        act.wait_ge(ored.sem, ored.at(l, base + i - 1))
                    nc.scalar.activation(ebuf[:, i % 2, 0:512], buf[:, i, :], ACT.Square).then_inc(osq.sem, 1)

            def out_rstd(l, which, groups):
                act.wait_ge(ored.sem, ored.at(l, (which + 1) * NT))
                link(nc.scalar.activation(hs[:, 0:groups * NT], hs[:, 0:groups * NT], ACT.Ln, scale=groups / 512.0, bias=eps[:, :]))
                nc.scalar.activation(hs[:, 0:groups * NT], hs[:, 0:groups * NT], ACT.Exp, scale=-0.5).then_inc(orstd.sem, 1)

            def softmax(l, n):
                scale = att(n)[4]
                act.wait_ge(max_ready.sem, max_ready.at(l, n + 1))
                act.wait_ge(t_ps.sem, t_ps.at(l, max(n - 1, 0)))
                act.wait_ge(o_evac.sem, o_evac.at(l, max(n - 3, 0)))
                nc.scalar.activation(halves(ebuf[:, n % 2, :]), pair(n % 2), ACT.Exp, scale=scale, bias=negmax[:, n % 2:n % 2 + 1],
                                     accum_out=sums[:, n % 4:n % 4 + 1]).then_inc(p_ready.sem, 1)

            def turned(l, n):
                act.wait_ge(t_ps.sem, t_ps.at(l, n + 1))
                act.wait_ge(o_ps.sem, o_ps.at(l, max(n - 1, 0)))
                nc.scalar.activation(mbuf[:, n % 2, 0:512], pb[:, TURN, 0:512], ACT.Copy).then_inc(pt_main.sem, 1)

            act.wait_ge(par_in.sem, 16)
            act.wait_ge(eps_ready.sem, 1)
            for l in range(DEPTH):
                nc.scalar.preload_act_table_set("natural_log_exp_and_others")
                for k in range(KD):
                    if l == 0:
                        act.wait_ge(x_in[k].sem, 16)
                    else:
                        act.wait_ge(evac.sem, evac.at(l - 1, G_FOUT + k + 1))
                    square(l, SQ_A + k, halves(h[:, k, :]))
                rsqrt(l, SQ_A + KD, 0, D_MODEL, rstd)

                nc.scalar.preload_act_table_set("silu_and_others")
                for f in range(6):
                    act.wait_ge(conv_ready.sem, conv_ready.at(l, f + 1))
                    nc.scalar.activation(tile_of(proj, f), kh[:, f % 2, :], ACT.Silu).then_inc(conv_act.sem, 1)
                for g in range(ZT, MO + 4):
                    if g == MISC:
                        continue
                    act.wait_ge(evac.sem, evac.at(l, g + 1))
                    if g < MISC:
                        nc.scalar.activation(tile_of(proj, g), tile_of(proj, g), ACT.Silu).then_inc(z_act.sem, 1)
                    else:
                        nc.scalar.activation(tile_of(proj, g), tile_of(proj, g), ACT.Tanh, scale=0.5).then_inc(o_tanh.sem, 1)

                nc.scalar.preload_act_table_set("natural_log_exp_and_others")
                d24 = slice(0, NDEC)
                act.wait_ge(dec_u.sem, dec_u.at(l, 1))
                link(nc.scalar.activation(ebuf[d24, 1, :], ebuf[d24, 0, :], ACT.Abs))
                link(nc.scalar.activation(ebuf[d24, 1, :], ebuf[d24, 1, :], ACT.Exp, scale=-1.0))
                link(nc.scalar.activation(ea[d24, :], par_at(l, "a_log", rows_=d24), ACT.Exp))
                nc.scalar.activation(ebuf[d24, 1, :], ebuf[d24, 1, :], ACT.Ln, bias=1.0).then_inc(dec_ln.sem, 1)
                act.wait_ge(lam_sum.sem, lam_sum.at(l, 1))
                nc.scalar.activation(lam_e[:, :], lam_s[:, :], ACT.Exp).then_inc(lam_exp.sem, 1)

                def job(q):
                    act.wait_ge(rs_used.sem, rs_used.at(l, q))
                    rsqrt(l, SQ_B + JOB_SQ[q] + len(JOBS[q][0]), 0, JOBS[q][1], rstd2)

                SQUARED = [CQ, CQ + 1, CQ + 2, CKV, CKV + 1] + [DQ + t for t in range(8)]

                def tile_square(s):
                    act.wait_ge(evac.sem, evac.at(l, SQUARED[s] + 1))
                    square(l, SQ_B + s, halves(tile_of(proj, SQUARED[s])))

                for s in range(5):
                    tile_square(s)
                job(0)
                tile_square(5)
                tile_square(6)
                for q in range(1, len(JOBS)):
                    job(q)
                    if q + 6 < len(SQUARED):
                        tile_square(q + 6)

                for n in range(STEPS_SSD):
                    exps(l, n)
                act.wait_ge(cols_ready.sem, cols_ready.at(l, 1))
                nc.scalar.activation(enm[:, :, :], cols[:, :, C_NM:NCOL], ACT.Exp).then_inc(enm_ready.sem, 1)
                act.wait_ge(tr_evac.sem, tr_evac.at(l, TR_OS + NT))
                for f in range(4):
                    square(l, SQ_S + f, halves(tile_of(mix, 4 + f)))
                act.wait_ge(rs_used.sem, rs_used.at(l, 10))
                rsqrt(l, SQ_S + 4, 3, 512, rstd2)
                for n in range(STEPS_SSD, STEPS):
                    exps(l, n)
                act.wait_ge(nd_evac.sem, nd_evac.at(l, 2 * ML_H))
                out_squares(l, 0, o_ml)
                out_rstd(l, 0, ML_H)

                rws = slice(0, MLA_QK)

                def prep(stage, hd):
                    side, what = stage // 3, stage % 3
                    e = 2 * hd + side
                    if what == 0:
                        act.wait_ge(p_copy.sem, p_copy.at(l, e + 1))
                        act.wait_ge(sq_used.sem, sq_used.at(l, SQ_M + e - 1))
                        nc.scalar.activation(sq[rws, (SQ_M + e) % 2, :], (qh, kh)[side][rws, hd % 2, 0:T],
                                             ACT.Square).then_inc(sq_ready.sem, 1)
                    elif what == 1:
                        act.wait_ge(rs_used.sem, rs_used.at(l, 11 + e))
                        rsqrt(l, SQ_M + e + 1, 3, MLA_QK, rstd2, rws)

                for s in (0, 1, 3, 4):
                    prep(s, 0)
                softmax(l, 0)
                for n in range(N_ATT_M):
                    hd, i = n // NT, n % NT
                    if n + 1 < N_ATT_M:
                        softmax(l, n + 1)
                    if hd + 1 < MLA_H and i in (0, 1, 2, 3):
                        prep((0, 1, 3, 4)[i], hd + 1)
                    turned(l, n)
                act.wait_ge(o_evac.sem, o_evac.at(l, N_ATT_M))
                out_squares(l, NT, o_tok)
                out_rstd(l, 1, 1)
                softmax(l, N_ATT_M)
                for n in range(N_ATT_M, N_ATT):
                    if n + 1 < N_ATT:
                        softmax(l, n + 1)
                    turned(l, n)
                act.wait_ge(o_evac.sem, o_evac.at(l, N_ATT))
                out_squares(l, 2 * NT, o_dif)
                out_rstd(l, 2, DIFF_H)

                for k in range(KD):
                    act.wait_ge(evac.sem, evac.at(l, G_OUT + k + 1))
                    square(l, SQ_F + k, halves(h[:, k, :]))
                rsqrt(l, SQ_F + KD, 0, D_MODEL, rstd)
                nc.scalar.preload_act_table_set("silu_and_others")
                for j in range(KF):
                    act.wait_ge(evac.sem, evac.at(l, G_FIN + 2 * j + 1))
                    nc.scalar.activation(ebuf[:, j % 2, :], ebuf[:, j % 2, :], ACT.Silu).then_inc(gsilu.sem, 1)

        @block.vector
        def _(dve):
            chained = [0]

            def link(ins):
                chained[0] += 1
                ins.then_inc(dve_chain.sem, 1)
                dve.wait_ge(dve_chain.sem, chained[0])

            def gains(l, base, name, dst):
                for k in range(KD):
                    if base == 0:
                        if l == 0:
                            dve.wait_ge(x_in[k].sem, 16)
                        else:
                            dve.wait_ge(evac.sem, evac.at(l - 1, G_FOUT + k + 1))
                    else:
                        dve.wait_ge(evac.sem, evac.at(l, G_OUT + k + 1))
                    nc.vector.tensor_scalar(dst(k), h[:, k, :], par_at(l, name, k), None, ALU.mult).then_inc(xg_ready.sem, 1)

            def scale_out(l, g, dst):
                dve.wait_ge(w_used.sem, w_used.at(l, g + 1 if g < N_IN else g - G_FIN + S_FIN + 1))
                nc.vector.tensor_tensor(halves(dst), pair(1 + g % 3), halves(rstd[:, :]), ALU.mult).then_inc(evac.sem, 1)

            def conv(l, f):
                if f >= 2:
                    dve.wait_ge(conv_act.sem, conv_act.at(l, f - 1))
                mid = TAPS // 2
                acc, src = kh[:, f % 2, :], tile_of(proj, f)
                link(nc.vector.tensor_scalar(acc, src, par_at(l, "conv_w", f * TAPS + mid), par_at(l, "conv_b", f), ALU.mult, ALU.add))
                shifts = [s for s in range(-mid, mid + 1) if s]
                for s in shifts:
                    a, b = max(0, -s), T - max(0, s)
                    ins = nc.vector.scalar_tensor_tensor(out=acc[:, a:b], in0=src[:, a + s:b + s],
                                                         scalar=par_at(l, "conv_w", f * TAPS + mid + s), in1=acc[:, a:b],
                                                         op0=ALU.mult, op1=ALU.add)
                    if s == shifts[-1]:
                        ins.then_inc(conv_ready.sem, 1)
                    else:
                        link(ins)

            def normed(l, which, src, gain, rows_=slice(0, P), count=True):
                ins = nc.vector.scalar_tensor_tensor(out=src, in0=src, scalar=gain, in1=rstd2[rows_, :], op0=ALU.mult, op1=ALU.mult)
                return ins.then_inc(rs_used.sem, 1) if count else ins

            def from_transposes(l, idx, dst, i, f_major=False, op=None):
                dve.wait_ge(tr_ready.sem, tr_ready.at(l, idx + 1))
                w = TILES[i][1]
                b = 4 + idx % 2
                src = pb[:, b, :].rearrange("p (f t) -> p f t", f=4)[:, :, 0:w] if f_major else pb[0:w, b, 0:512]
                op(dst, src).then_inc(tr_evac.sem, 1)

            def copy(dst, src):
                return nc.vector.tensor_copy(dst, src)

            def feature_block(buf, tile0, i):
                a, w = TILES[i]
                return buf[:, tile0 * T:(tile0 + 4) * T].rearrange("p (f t) -> p f t", t=T)[:, :, a:a + w]

            def exponents(l, n):
                u, j = n // NT, n % NT
                _, d, r = unit(u)
                lo, hi = rng(d, j)
                w = TILES[j][1]
                rw = slice(0, w)
                p = u % 2 if u < 2 * SSD_H else 0
                if j == 0:
                    dve.wait_ge(rowb.sem, rowb.at(l, u + 1))
                dve.wait_ge(m_ready.sem, m_ready.at(l, max(n - 1, 0)))
                e = ebuf[rw, n % 2, :]
                m = mask(d, j)
                parts = [(lo, hi)] if hi <= HALF or lo >= HALF else [(lo, HALF), (HALF, hi)]
                if (lo, hi) == (0, T):
                    ins = nc.vector.scalar_tensor_tensor(out=halves(e[:, 0:T]), in0=pair(p, rw), scalar=cols[rw, j, r:r + 1],
                                                         in1=halves(m), op0=ALU.add, op1=ALU.min)
                else:
                    for a, b in parts:
                        ins = nc.vector.scalar_tensor_tensor(out=e[:, a - lo:b - lo],
                                                             in0=pb[rw, 2 * p + a // HALF, a % HALF:a % HALF + b - a],
                                                             scalar=cols[rw, j, r:r + 1], in1=m[:, a - lo:b - lo],
                                                             op0=ALU.add, op1=ALU.min)
                ins.then_inc(e_raw.sem, 1)

            def weights(l, n):
                u, j = n // NT, n % NT
                hd, d, r = unit(u)
                lo, hi = rng(d, j)
                rw = slice(0, TILES[j][1])
                e, m = ebuf[rw, n % 2, 0:hi - lo], mbuf[rw, n % 2, 0:hi - lo]
                dve.wait_ge(e_exp.sem, e_exp.at(l, n + 1))
                dve.wait_ge(m_used.sem, m_used.at(l, max(n - 1, 0)))
                if u < 2 * SSD_H:
                    nc.vector.scalar_tensor_tensor(out=m, in0=e, scalar=cols[rw, j, C_DT + r:C_DT + r + 1],
                                                   in1=cb(hd // (SSD_H // SSD_G), j, lo, hi, rw), op0=ALU.mult,
                                                   op1=ALU.mult).then_inc(m_ready.sem, 1)
                else:
                    dve.wait_ge(qk_ps.sem, qk_ps.at(l, n - STEPS_SSD + 1))
                    nc.vector.scalar_tensor_tensor(out=like(m, hi - lo), in0=like(e, hi - lo), scalar=ML_QK ** -0.5,
                                                   in1=span(1, hi - lo, rw), op0=ALU.mult, op1=ALU.mult).then_inc(m_ready.sem, 1)

            def ssd_head(l, hd):
                dve.wait_ge(m_used.sem, m_used.at(l, (hd + 1) * 2 * NT))
                c = slice(hd * SSD_P, (hd + 1) * SSD_P)
                nc.vector.scalar_tensor_tensor(out=o_tok[:, :, c], in0=x_tok[:, :, c], scalar=par_at(l, "ssd_d", hd),
                                               in1=pb[:, 6 + hd % 2, 0:NT * SSD_P].rearrange("p (i v) -> p i v", v=SSD_P),
                                               op0=ALU.mult, op1=ALU.add).then_inc(y_evac.sem, 1)

            def ml_unit(l, v):
                hd, d, _ = unit(2 * SSD_H + v)
                dve.wait_ge(m_used.sem, m_used.at(l, STEPS_SSD + (v + 1) * NT))
                b = 4 + 2 * (v % 2)
                nc.vector.tensor_copy(den[:, 0:3], pb[:, b, ML_V:3 * (ML_V + 1):ML_V + 1])
                link(nc.vector.tensor_copy(den[:, 3:5], pb[:, b + 1, ML_V:2 * (ML_V + 1):ML_V + 1]))
                link(nc.vector.scalar_tensor_tensor(out=den2[:, :], in0=den[:, :], scalar=-1.0, in1=den[:, :], op0=ALU.mult, op1=ALU.max))
                link(nc.vector.tensor_tensor(den[:, :], den2[:, :], enm[:, :, d * ML_H + hd], ALU.max))
                link(nc.vector.reciprocal(den2[:, :], den[:, :]))
                for i in range(NT):
                    num = pb[:, b + i // 3, (i % 3) * (ML_V + 1):(i % 3) * (ML_V + 1) + ML_V]
                    o = o_ml[:, i, hd * ML_V:(hd + 1) * ML_V]
                    if d == 0:
                        ins = nc.vector.tensor_scalar(o, num, den2[:, i:i + 1], None, ALU.mult)
                    else:
                        ins = nc.vector.scalar_tensor_tensor(out=o, in0=num, scalar=den2[:, i:i + 1], in1=o, op0=ALU.mult, op1=ALU.add)
                ins.then_inc(nd_evac.sem, 1)
                dve.wait_ge(nd_evac.sem, nd_evac.at(l, v + 1))

            def out_sums(l, which, groups):
                for i in range(NT):
                    dve.wait_ge(osq.sem, osq.at(l, which * NT + i + 1))
                    nc.vector.reduce_sum(hs[:, i * groups:(i + 1) * groups],
                                         ebuf[:, i % 2, 0:512].rearrange("p (g v) -> p g v", g=groups), axis=AX.X).then_inc(ored.sem, 1)

            def out_scales(l, which, groups, buf):
                dve.wait_ge(orstd.sem, orstd.at(l, which + 1))
                for i in range(NT):
                    o = buf[:, i, :].rearrange("p (g v) -> p g v", g=groups)
                    if groups == 1:
                        nc.vector.tensor_scalar(buf[:, i, :], buf[:, i, :], hs[:, i:i + 1], None, ALU.mult).then_inc(oscaled.sem, 1)
                    else:
                        nc.vector.tensor_tensor(o, o, hs[:, i * groups:(i + 1) * groups].unsqueeze(2).to_broadcast([P, groups, 512 // groups]),
                                                ALU.mult).then_inc(oscaled.sem, 1)

            def row_max(l, n):
                scale = att(n)[4]
                dve.wait_ge(s_ps.sem, s_ps.at(l, n + 1))
                dve.wait_ge(p_ready.sem, p_ready.at(l, max(n - 1, 0)))
                link(nc.vector.tensor_reduce(rowmax[:, n % 2:n % 2 + 1], pair(n % 2), AX.XY, ALU.max))
                nc.vector.tensor_scalar(negmax[:, n % 2:n % 2 + 1], rowmax[:, n % 2:n % 2 + 1], -scale, None,
                                        ALU.mult).then_inc(max_ready.sem, 1)

            def turned_tail(l, n):
                dve.wait_ge(tail_ps.sem, tail_ps.at(l, n + 1))
                dve.wait_ge(o_ps.sem, o_ps.at(l, max(n - 1, 0)))
                w = TILES[-1][1]
                nc.vector.tensor_copy(mbuf[0:w, n % 2, 512:WIDE], pb[0:w, TAIL_O, 0:P]).then_inc(pt_tail.sem, 1)

            def att_out(l, n):
                _, _, _, dv, _, i, hd = att(n)
                r = rsum[:, n % 2:n % 2 + 1]
                dve.wait_ge(p_ready.sem, p_ready.at(l, n + 1))
                link(nc.vector.reciprocal(r, sums[:, n % 4:n % 4 + 1]))
                src = pb[:, TAIL_O, P:P + dv]
                if n < N_ATT_M:
                    dve.wait_ge(o_ps.sem, o_ps.at(l, n + 1))
                    nc.vector.tensor_scalar(o_tok[:, i, hd * dv:(hd + 1) * dv], src, r, None, ALU.mult).then_inc(o_evac.sem, 1)
                else:
                    o = o_dif[:, i, (hd // 2) * dv:(hd // 2 + 1) * dv]
                    if hd % 2 == 0:
                        dve.wait_ge(o_ps.sem, o_ps.at(l, n + 1))
                        nc.vector.tensor_scalar(o, src, r, None, ALU.mult).then_inc(o_evac.sem, 1)
                    else:
                        link(nc.vector.tensor_tensor(r, r, neg_lam[:, :], ALU.mult))
                        dve.wait_ge(o_evac.sem, o_evac.at(l, n - NT + 1))
                        dve.wait_ge(o_ps.sem, o_ps.at(l, n + 1))
                        nc.vector.scalar_tensor_tensor(out=o, in0=src, scalar=r, in1=o, op0=ALU.mult, op1=ALU.add).then_inc(o_evac.sem, 1)

            nc.vector.memset(eps[:, :], EPS).then_inc(eps_ready.sem, 1)
            dve.wait_ge(par_in.sem, 16)
            dve.wait_ge(cleared.sem, 6)
            for l in range(DEPTH):
                if l:
                    dve.wait_ge(w_used.sem, w_used.at(l - 1, S_FIN))
                gains(l, 0, "attn_g", lambda k: tile_of(mix, k))
                dve.wait_ge(rs_ready.sem, rs_ready.at(l, RS_A + 1))
                d24 = slice(0, NDEC)
                for g in range(N_IN):
                    q = g - JOB_G
                    if 0 <= q < len(JOBS):
                        dve.wait_ge(rs_ready.sem, rs_ready.at(l, RS_B + q + 1))
                        ts = JOBS[q][0]
                        for c, t in enumerate(ts):
                            normed(l, q, tile_of(proj, t), par_at(l, JOBS[q][2], c if q < 2 else 0), count=(c == len(ts) - 1))
                    scale_out(l, g, tile_of(proj, g))
                    if 2 <= q < len(JOBS):
                        t = q - 2
                        dve.wait_ge(rot_ready.sem, rot_ready.at(l, t + 1))
                        dve.wait_ge(table_in.sem, 16)
                        link(nc.vector.tensor_tensor(halves(mbuf[:, 0, 0:T]), pair(0), halves(C("sin_d")), ALU.mult))
                        dve.wait_ge(qcos.sem, qcos.at(l, t + 1))
                        nc.vector.tensor_tensor(tile_of(proj, DQ + t), tile_of(proj, DQ + t), mbuf[:, 0, 0:T], ALU.add).then_inc(roped.sem, 1)
                    if g < 6:
                        dve.wait_ge(evac.sem, evac.at(l, g + 1))
                        conv(l, g)
                    if g == MISC + 1:
                        dve.wait_ge(table_in.sem, 16)
                        dve.wait_ge(evac.sem, evac.at(l, MISC + 1))
                        nc.vector.tensor_scalar(ebuf[d24, 0, :], tile_of(proj, MISC, rows_=d24), par_at(l, "bias", rows_=d24),
                                                C("sign", d24), ALU.add, ALU.mult).then_inc(dec_u.sem, 1)
                        lam = par_at(l, "lam", 0, 4 * DIFF_QK).rearrange("p (a b) -> p a b", b=DIFF_QK)
                        link(nc.vector.tensor_tensor(lam_p[:, :, :], lam[:, 0:4:2, :], lam[:, 1:4:2, :], ALU.mult))
                        nc.vector.reduce_sum(lam_s[:, :], lam_p[:, :, :], axis=AX.X).then_inc(lam_sum.sem, 1)
                    if g == MO + 5:
                        dve.wait_ge(conv_act.sem, conv_act.at(l, 6))
                        dve.wait_ge(dec_ln.sem, dec_ln.at(l, 1))
                        u, ln = ebuf[d24, 0, :], ebuf[d24, 1, :]
                        dec, sp, ig = kh[d24, 0, :], mbuf[d24, 1, 0:T], qh[d24, 0, 0:T]
                        link(nc.vector.scalar_tensor_tensor(out=sp, in0=u, scalar=0.0, in1=ln, op0=ALU.max, op1=ALU.add))
                        link(nc.vector.tensor_scalar(dec, sp, ea[d24, :], -1.0, ALU.mult, ALU.mult))
                        link(nc.vector.tensor_copy(ig, tile_of(proj, MISC, rows_=slice(32, 32 + NDEC))))
                        link(nc.vector.tensor_scalar(ig, ig, par_at(l, "i_bias", rows_=d24), None, ALU.add))
                        link(nc.vector.memset(ebuf[d24, 0, :], 0.0))
                        zero = ebuf[d24, 0, :]
                        link(nc.vector.tensor_tensor_scan(rows[0:NDEC, :], dec, zero, 0.0, ALU.add, ALU.add))
                        link(nc.vector.tensor_tensor_scan(rows[32:32 + NDEC, ::-1], dec[:, ::-1], zero, 0.0, ALU.add, ALU.add))
                        link(nc.vector.tensor_tensor_scan(rows[64:64 + NDEC, :], dec, ig, NEG, ALU.add, ALU.max))
                        nc.vector.tensor_tensor_scan(rows[96:96 + NDEC, ::-1], dec[:, ::-1], ig[:, ::-1], NEG, ALU.add,
                                                     ALU.max).then_inc(rows_ready.sem, 1)
                        dve.wait_ge(rows_ready.sem, rows_ready.at(l, 1))
                        dve.wait_ge(lam_exp.sem, lam_exp.at(l, 1))
                        link(nc.vector.scalar_tensor_tensor(out=neg_lam[:, :], in0=lam_e[:, 0:1], scalar=-1.0, in1=lam_e[:, 1:2],
                                                            op0=ALU.mult, op1=ALU.add))
                        link(nc.vector.tensor_tensor(neg_lam[:, :], neg_lam[:, :], par_at(l, "lambda_init", 0), ALU.subtract))
                        link(nc.vector.tensor_tensor(gain_d[:, :], par_at(l, "diff_out_g"), par_at(l, "lambda_init", 1), ALU.mult))

                dve.wait_ge(cols_ps.sem, cols_ps.at(l, 1))
                nc.vector.tensor_copy(cols[:, 0:NT - 1, :], pb[:, 7, 0:(NT - 1) * NCOL].rearrange("p (i c) -> p i c", c=NCOL))
                nc.vector.tensor_copy(cols[0:TILES[-1][1], NT - 1, :], pb[0:TILES[-1][1], 7, (NT - 1) * NCOL:NT * NCOL]).then_inc(cols_ready.sem, 1)
                dve.wait_ge(cols_ready.sem, cols_ready.at(l, 1))
                for i in range(NT):
                    from_transposes(l, TR_X + i, x_tok[0:TILES[i][1], i, :], i, op=copy)
                for g in range(SSD_G):
                    for j, (_, w) in enumerate(TILES):
                        dve.wait_ge(cb_ps.sem, cb_ps.at(l, g * NT + j + 1))
                        nc.vector.tensor_copy(halves(cb(g, j, 0, T, slice(0, w))), pair(2, slice(0, w))).then_inc(cb_ready.sem, 1)
                dve.wait_ge(cb_ready.sem, cb_ready.at(l, 2 * NT))
                exponents(l, 0)
                for n in range(STEPS_SSD):
                    if n + 1 < STEPS_SSD:
                        exponents(l, n + 1)
                    weights(l, n)
                    if n % (2 * NT) == 2 and n > 2 * NT:
                        ssd_head(l, n // (2 * NT) - 1)
                ssd_head(l, SSD_H - 1)
                dve.wait_ge(z_act.sem, z_act.at(l, 4))
                dve.wait_ge(m_ready.sem, m_ready.at(l, STEPS_SSD))
                for i in range(NT):
                    def gated(dst, src, i=i):
                        return nc.vector.tensor_tensor(dst, src, feature_block(proj, ZT, i), ALU.mult)
                    from_transposes(l, TR_OS + i, feature_block(mix, 4, i), i, True, gated)
                nc.vector.memset(v_ml[:, :, :, ML_V], 1.0)
                for i in range(NT):
                    def by_head(dst, src):
                        return nc.vector.tensor_copy(dst, src.rearrange("p (h v) -> p h v", v=ML_V))
                    from_transposes(l, TR_MV + i, v_ml[0:TILES[i][1], i, :, 0:ML_V], i, op=by_head)
                dve.wait_ge(rs_ready.sem, rs_ready.at(l, RS_S + 1))
                for f in range(4):
                    ins = nc.vector.scalar_tensor_tensor(out=tile_of(mix, 4 + f), in0=tile_of(mix, 4 + f), scalar=par_at(l, "ssd_g", f),
                                                         in1=rstd2[:, :], op0=ALU.mult, op1=ALU.mult)
                ins.then_inc(rs_used.sem, 1)

                dve.wait_ge(enm_ready.sem, enm_ready.at(l, 1))
                exponents(l, STEPS_SSD)
                for n in range(STEPS_SSD, STEPS):
                    if n + 1 < STEPS:
                        exponents(l, n + 1)
                    weights(l, n)
                    v = (n - STEPS_SSD) // NT
                    if (n - STEPS_SSD) % NT == 1 and v >= 1:
                        ml_unit(l, v - 1)
                ml_unit(l, 2 * ML_H - 1)
                out_sums(l, 0, ML_H)
                for i, (_, w) in enumerate(TILES):
                    if i < NT - 1:
                        dve.wait_ge(v_ps.sem, v_ps.at(l, i + 1))
                    else:
                        dve.wait_ge(w_used.sem, w_used.at(l, S_UV + 1))
                    nc.vector.tensor_copy(v_mla[0:w, i, :], pb[0:w, 6 + i % 2, :]).then_inc(v_ready.sem, 1)
                out_scales(l, 0, ML_H, o_ml)

                rws, kr = slice(0, MLA_QK), slice(MLA_NOPE, MLA_QK)

                def prep(stage, hd):
                    side, what = stage // 3, stage % 3
                    e = 2 * hd + side
                    buf = (qh, kh)[side]
                    if what == 0:
                        dve.wait_ge(s_ps.sem, s_ps.at(l, max(hd - 1, 0) * NT))
                        dve.wait_ge(*projected(l, e))
                        if side == 1:
                            nc.vector.tensor_copy(buf[kr, hd % 2, 0:T], tile_of(proj, MISC, rows_=kr))
                        m = slice(0, MLA_QK if side == 0 else MLA_NOPE)
                        nc.vector.tensor_copy(halves(buf[m, hd % 2, 0:T]), pair(3, m)).then_inc(p_copy.sem, 1)
                        dve.wait_ge(p_copy.sem, p_copy.at(l, e + 1))
                    elif what == 1:
                        dve.wait_ge(rs_ready.sem, rs_ready.at(l, RS_M + e + 1))
                        normed(l, 0, buf[rws, hd % 2, 0:T], par_at(l, ("qh_g", "kh_g")[side], rows_=rws), rws)
                    else:
                        dve.wait_ge(rot_ready.sem, rot_ready.at(l, 8 + e + 1))
                        t0, src = rstd[kr, :], buf[kr, hd % 2, 0:T]
                        link(nc.vector.tensor_tensor(halves(t0), pair(3, kr), halves(C("sin_m", kr)), ALU.mult))
                        link(nc.vector.tensor_tensor(src, src, C("cos_m", kr), ALU.mult))
                        nc.vector.tensor_tensor(src, src, t0, ALU.add).then_inc(roped.sem, 1)

                for s in range(6):
                    prep(s, 0)
                dve.wait_ge(o_sig.sem, o_sig.at(l, 4))
                for i in range(NT):
                    def gate(dst, src, i=i):
                        return nc.vector.scalar_tensor_tensor(out=dst, in0=src, scalar=par_at(l, "ml_out_g"),
                                                              in1=feature_block(proj, MO, i), op0=ALU.mult, op1=ALU.mult)
                    from_transposes(l, TR_OM + i, feature_block(mix, 12, i), i, True, gate)
                row_max(l, 0)
                for n in range(N_ATT_M):
                    hd, i = n // NT, n % NT
                    if n + 1 < N_ATT_M:
                        row_max(l, n + 1)
                    if hd + 1 < MLA_H and i in (0, 1, 2, 3):
                        prep((0, 1, 3, 4)[i], hd + 1)
                    turned_tail(l, n)
                    if n >= 1:
                        att_out(l, n - 1)
                    if hd + 1 < MLA_H and i in (1, 3):
                        prep((None, 2, None, 5)[i], hd + 1)
                att_out(l, N_ATT_M - 1)
                for i in range(NT):
                    from_transposes(l, TR_DV + i, v_dif[0:TILES[i][1], i, :], i, op=copy)
                out_sums(l, 1, 1)
                out_scales(l, 1, 1, o_tok)
                for i in range(NT):
                    def by_gain(dst, src, i=i):
                        return nc.vector.tensor_tensor(dst, src, par_at(l, "mla_out_g", 0, 4).unsqueeze(2).to_broadcast([P, 4, TILES[i][1]]), ALU.mult)
                    from_transposes(l, TR_OA + i, feature_block(mix, 0, i), i, True, by_gain)

                row_max(l, N_ATT_M)
                for n in range(N_ATT_M, N_ATT):
                    if n + 1 < N_ATT:
                        row_max(l, n + 1)
                    turned_tail(l, n)
                    if n > N_ATT_M:
                        att_out(l, n - 1)
                att_out(l, N_ATT - 1)
                out_sums(l, 2, DIFF_H)
                out_scales(l, 2, DIFF_H, o_dif)
                for i in range(NT):
                    def scaled(dst, src):
                        return nc.vector.tensor_scalar(dst, src, gain_d[:, :], None, ALU.mult)
                    from_transposes(l, TR_OD + i, feature_block(mix, 8, i), i, True, scaled)

                def residual(l, g, slot):
                    dve.wait_ge(w_used.sem, w_used.at(l, slot))
                    k = (g - G_OUT) if g < G_FIN else g - G_FOUT
                    nc.vector.tensor_tensor(halves(h[:, k, :]), halves(h[:, k, :]), pair(1 + g % 3), ALU.add).then_inc(evac.sem, 1)

                for g in range(KD):
                    residual(l, G_OUT + g, S_OUT + 2 * g + 2)
                gains(l, 1, "ffn_g", lambda k: tile_of(proj, 32 + k))

                dve.wait_ge(rs_ready.sem, rs_ready.at(l, RS_F + 1))
                for j in range(KF):
                    if j >= 2:
                        dve.wait_ge(act_ready.sem, act_ready.at(l, j - 1))
                    scale_out(l, G_FIN + 2 * j, ebuf[:, j % 2, :])
                    scale_out(l, G_FIN + 2 * j + 1, mbuf[:, j % 2, 0:T])
                    dve.wait_ge(gsilu.sem, gsilu.at(l, j + 1))
                    dve.wait_ge(evac.sem, evac.at(l, G_FIN + 2 * j + 2))
                    nc.vector.tensor_tensor(tile_of(proj, j), ebuf[:, j % 2, :], mbuf[:, j % 2, 0:T], ALU.mult).then_inc(act_ready.sem, 1)
                for g in range(KD):
                    residual(l, G_FOUT + g, S_FOUT + 3 * g + 3)


def _columns():
    cq, ckv, kr, z = 0, 384, 640, 672
    xbc, dt, dq = 1184, 1952, 1968
    dk, dv, mq, mk, mv, mo, mi, mf = 2480, 2992, 3504, 3760, 4016, 4528, 5040, 5048
    run = lambda a, n: list(range(a, a + n))
    misc = run(dt, 16) + run(mf, 8) + [-1] * 8 + [-1] * 16 + run(mi, 8) + [-1] * 8 + run(kr, 32) + [-1] * 32
    return np.array(run(xbc, 768) + run(z, 512) + misc + run(mo, 512) + run(cq, 384) + run(ckv, 256) + run(dq, 512)
                    + run(dk, 512) + run(dv, 512) + run(mq, 256) + run(mk, 256) + run(mv, 512))


_HEAD = np.array(list(range(MLA_ROPE, MLA_QK)) + list(range(MLA_ROPE)))


def _weights(w_in, w_uq, w_ukv, w_out, w_fi, w_fo):
    f = np.float32
    ws = np.zeros((DEPTH, N_SLOT, P, SLOT), f)
    cols = _columns()
    for l in range(DEPTH):
        wi = np.concatenate([w_in[l], np.zeros((D_MODEL, 1), f)], 1)[:, cols]
        tiles = lambda w, kt: w.reshape(kt, P, -1, P).transpose(2, 1, 0, 3)
        ws[l, 0:N_IN] = tiles(wi, KD).reshape(N_IN, P, SLOT)
        kv = w_ukv[l].reshape(2, P, MLA_H, MLA_NOPE + MLA_V)
        ws[l, S_UV] = kv[..., MLA_NOPE:].transpose(1, 0, 2, 3).reshape(P, SLOT)
        uq = w_uq[l].reshape(3, P, MLA_H, MLA_QK)[..., _HEAD].transpose(2, 1, 0, 3).reshape(MLA_H, P, 3 * MLA_QK)
        for hd in range(MLA_H):
            o = (hd % UQ_HEADS) * 3 * MLA_QK
            ws[l, S_UQ + hd // UQ_HEADS, :, o:o + 3 * MLA_QK] = uq[hd]
        ws[l, S_UK] = kv[..., :MLA_NOPE].transpose(1, 2, 0, 3).reshape(P, SLOT)
        ws[l, S_OUT:S_FIN] = tiles(w_out[l], KM).reshape(KD, P, 2, SLOT).transpose(0, 2, 1, 3).reshape(2 * KD, P, SLOT)
        fi = tiles(w_fi[l], KD).reshape(2, KF, P, SLOT)
        ws[l, S_FIN:S_FOUT] = fi.transpose(1, 0, 2, 3).reshape(2 * KF, P, SLOT)
        fo = tiles(w_fo[l], KF).reshape(KD, P, KF * P)
        pad = np.zeros((KD, P, 3 * SLOT), f)
        pad[:, :, :KF * P] = fo
        ws[l, S_FOUT:] = pad.reshape(KD, P, 3, SLOT).transpose(0, 2, 1, 3).reshape(3 * KD, P, SLOT)
    return ws.reshape(DEPTH * N_SLOT, P, SLOT)


def _params(a):
    f = np.float32
    out = np.zeros((P, DEPTH, N_PARAM), f)

    def put(name, v, rows_=P):
        s, e = PARAM[name]
        for l in range(DEPTH):
            out[0:rows_, l, s:e] = v(l)

    tiled = lambda x, n: x.reshape(n, P).T
    put("attn_g", lambda l: tiled(a["attn_norm_g"][l], KD))
    put("ffn_g", lambda l: tiled(a["ffn_norm_g"][l], KD))
    put("q_g", lambda l: tiled(a["mla_q_norm_g"][l], 3))
    put("kv_g", lambda l: tiled(a["mla_kv_norm_g"][l], 2))
    put("qh_g", lambda l: a["mla_q_head_g"][l][_HEAD][:, None], MLA_QK)
    put("kh_g", lambda l: a["mla_k_head_g"][l][_HEAD][:, None], MLA_QK)
    put("mla_out_g", lambda l: tiled(a["mla_out_g"][l], 4))
    put("conv_w", lambda l: a["ssd_conv_w"][l].reshape(TAPS, 6, P).transpose(2, 1, 0).reshape(P, 6 * TAPS))
    put("conv_b", lambda l: tiled(a["ssd_conv_b"][l], 6))
    put("ssd_g", lambda l: tiled(a["ssd_norm_g"][l], 4))
    put("ssd_d", lambda l: np.broadcast_to(a["ssd_d"][l][None], (P, SSD_H)))
    put("dq_g", lambda l: np.concatenate([a["diff_q_head_g"][l]] * 2)[:, None])
    put("dk_g", lambda l: np.concatenate([a["diff_k_head_g"][l]] * 2)[:, None])
    put("diff_out_g", lambda l: a["diff_out_g"][l][:, None])
    put("ml_out_g", lambda l: a["mlstm_out_g"][l][:, None])
    z8, z16 = np.zeros(8, f), np.zeros(16, f)
    put("bias", lambda l: np.concatenate([a["ssd_dt_bias"][l].ravel(), a["mlstm_f_bias"][l].ravel()])[:, None], NDEC)
    put("a_log", lambda l: np.concatenate([a["ssd_a_log"][l].ravel(), z8])[:, None], NDEC)
    put("i_bias", lambda l: np.concatenate([z16, a["mlstm_i_bias"][l].ravel()])[:, None], NDEC)
    put("lam", lambda l: np.broadcast_to(a["diff_lambda"][l].reshape(1, -1), (P, 4 * DIFF_QK)))
    init = [0.8 - 0.6 * float(np.exp(-0.3 * l)) for l in range(DEPTH)]
    put("lambda_init", lambda l: np.array([[init[l], 1.0 - init[l]]], f))
    return out


def _rope(rot, starts):
    f = np.float32
    r = rot // 2
    inv = (1.0 / (f(500000.0) ** (np.arange(0, rot, 2, dtype=f) / f(rot)))).astype(f)
    ang = (np.arange(T, dtype=f)[:, None] * inv[None, :]).astype(f)
    c, s = np.cos(ang).astype(f).T, np.sin(ang).astype(f).T
    cos, sin, perm = np.ones((P, T), f), np.zeros((P, T), f), np.zeros((P, P), f)
    for a in starts:
        cos[a:a + r], cos[a + r:a + rot] = c, c
        sin[a:a + r], sin[a + r:a + rot] = s, s
        for k in range(r):
            perm[a + r + k, a + k] = -1.0
            perm[a + k, a + r + k] = 1.0
    return cos, sin, perm


def _constants():
    f = np.float32
    out = np.zeros((P, N_CONST), f)

    def put(name, v):
        s, e = CONST[name]
        out[0:v.shape[0], s:e] = v

    put("ones", np.ones((P, P), f))
    put("ident", np.eye(P, dtype=f))
    put("ones_h", np.kron(np.eye(2, dtype=f), np.ones((64, 64), f)))
    key, query = np.arange(P)[:, None], np.arange(P)[None, :]
    put("mask", np.concatenate([np.where(query >= key, 0, NEG), np.zeros((P, 4 * P)), np.where(query <= key, 0, NEG)], 1).astype(f))
    cos, sin, perm = _rope(DIFF_ROPE, (0, 64))
    put("cos_d", cos), put("sin_d", sin), put("perm_d", perm)
    cos, sin, perm = _rope(MLA_ROPE, (MLA_NOPE,))
    put("cos_m", cos), put("sin_m", sin), put("perm_m", perm)
    FW, BW, MF, MB = 0, 32, 64, 96
    sel, rs, ig, sp = (np.zeros((P, n), f) for n in (NDEC, NCOL, NCOL, NCOL))
    for r in range(NDEC):
        back = r // SSD_H if r < C_ML else (r - C_ML) // ML_H
        sel[(BW if back else FW) + r, r] = 1.0
        rs[(BW if back else FW) + r, r] = -1.0
        if r >= C_ML:
            sel[(MB if back else MF) + r, r] = -1.0
            ig[r, r] = 1.0
            rs[(MB if back else MF) + r, C_NM + r - C_ML] = -1.0
        else:
            sp[r, C_DT + r] = 1.0
    put("rowsel", sel), put("lin_rs", rs), put("lin_i", ig), put("lin_sp", sp)
    put("sign", np.array([[1.0]] * C_ML + [[-1.0]] * (NDEC - C_ML), f))
    return out


def kernel(**inputs):
    import concourse.bacc as _bacc
    from concourse.bass_utils import run_bass_kernel_spmd as _run

    a = {k: np.asarray(v) for k, v in inputs.items()}
    tokens = np.concatenate([a["meta_tokens"], a["x"][0]], 0)
    arrays = {
        "x_t": np.ascontiguousarray(tokens.T.reshape(KD, P, T).transpose(1, 0, 2)),
        "w_stream": _weights(a["w_in"], a["mla_w_uq"], a["mla_w_ukv"], a["w_out"], a["w_ffn_in"], a["w_ffn_out"]),
        "params": _params(a),
        "consts": _constants(),
    }
    nc = _bacc.Bacc("TRN2", target_bir_lowering=False, num_devices=1, dynamic_dma_scratch_size=1024)
    args = [nc.dram_tensor(n, v.shape, FP32, kind="ExternalInput").ap() for n, v in arrays.items()]
    out = nc.dram_tensor("out_t", (P, KD, SEQ), FP32, kind="ExternalOutput").ap()
    trunk(nc, *args, out)
    r = _run(nc, [arrays], core_ids=[0])
    got = np.asarray(r.results[0]["out_t"])
    return np.ascontiguousarray(got.transpose(2, 1, 0).reshape(1, SEQ, D_MODEL))
```

```python
from contextlib import ExitStack

import numpy as np
import concourse.bass as bass
from concourse import mybir

FP32 = mybir.dt.float32
FP32R = mybir.dt.float32r
ALU = mybir.AluOpType
ACT = mybir.ActivationFunctionType
AX = mybir.AxisListType

DEPTH, D_MODEL, N_META, SEQ = 2, 1024, 16, 512
EPS, NEG = 1e-6, -1e30
P = 128
T = N_META + SEQ
HALF = T // 2
KD = D_MODEL // P
TILES = [(i * P, min(P, T - i * P)) for i in range(-(-T // P))]
NT = len(TILES)
WIDE = NT * P

MLA_H, MLA_NOPE, MLA_ROPE, MLA_V = 8, 64, 32, 64
MLA_QK = MLA_NOPE + MLA_ROPE
Q_RANK, KV_RANK = 384, 256
SSD_H, SSD_P, SSD_G, SSD_N, TAPS = 8, 64, 2, 64, 5
DIFF_H, DIFF_QK, DIFF_V, DIFF_ROPE = 4, 64, 128, 16
ML_H, ML_QK, ML_V = 4, 64, 128
D_FF = 2816
KF = D_FF // P
KM = 16

XS, BM, CM, MISC, ZT, MO, DQ, DK, MQ, MK, MV, CQ, CKV, DV = 0, 4, 5, 6, 7, 11, 15, 19, 23, 25, 27, 31, 34, 36
N_IN = 40
G_SSD, G_ML = 15, 31
SLOT = KD * P
S_OUT1, S_OUT2 = N_IN, N_IN + KD
S_FIN = N_IN + 2 * KD
S_FOUT = S_FIN + 2 * KF
N_SLOT = S_FOUT + 3 * KD
RAW = 2
PARTS = 2
N_RAW = N_SLOT + 1
UQ_HEADS = 3
G_OUT1, G_OUT2, G_FIN, G_FOUT = N_IN, N_IN + KD, N_IN + 2 * KD, N_IN + 2 * KD + 2 * KF
N_GROUP = G_FOUT + KD
CHUNKS_SSD = ((0, 0), (0, 2), (2, 4), (4, 6), (6, 8))
CHUNKS_ML = ((0, 0), (0, 2), (2, 4), (4, 5), (5, 8))
CHUNKS_DIFF = ((0, 2), (2, 4), (4, 6), (6, 7), (7, 8))
LATE_CHUNKS = ((0, 0), (0, 0), (0, 3), (3, 6), (6, 8))

NDEC = 2 * SSD_H + 2 * ML_H
C_ML, C_DT, C_NM = 2 * SSD_H, NDEC, NDEC + 2 * SSD_H
NCOL = C_NM + 2 * ML_H


def layout(fields):
    at, out = 0, {}
    for name, n in fields:
        out[name] = (at, at + n)
        at += n
    return out, at


CONST, N_CONST = layout([("ones", P), ("ident", P), ("mask", 6 * P), ("ones_h", P), ("perm_d", P), ("perm_m", P), ("cos_d", T), ("sin_d", T),
                         ("cos_m", T), ("sin_m", T), ("rowsel", NDEC), ("lin_rs", NCOL), ("lin_i", NCOL), ("lin_sp", NCOL),
                         ("sign", 1)])
PARAM, N_PARAM = layout([("attn_g", KD), ("ffn_g", KD), ("q_g", 3), ("kv_g", 2), ("qh_g", 1), ("kh_g", 1), ("mla_out_g", 4),
                         ("conv_w", 6 * TAPS), ("conv_b", 6), ("ssd_g", 4), ("ssd_d", SSD_H), ("dq_g", 1), ("dk_g", 1),
                         ("diff_out_g", 1), ("ml_out_g", 1), ("bias", 1), ("a_log", 1), ("i_bias", 1), ("lam", 4 * DIFF_QK),
                         ("lambda_init", 2)])

STEPS_SSD, STEPS_ML, STEPS = 2 * SSD_H * NT, 2 * ML_H * NT, 2 * (SSD_H + ML_H) * NT
N_ATT_M = MLA_H * NT
N_ATT = N_ATT_M + 2 * DIFF_H * NT
SQ_A, SQ_D, SQ_S, SQ_C, SQ_M, SQ_F = 0, KD, KD + 8, KD + 12, KD + 17, KD + 17 + 2 * MLA_H
N_SQ = SQ_F + KD
RS_A, RS_D, RS_S, RS_C, RS_M, RS_F = 0, 1, 9, 10, 12, 12 + 2 * MLA_H
N_RS = RS_F + 1
JOB_UNITS = {4: (SQ_C, 3, RS_C), 6: (SQ_C + 3, 2, RS_C + 1)}
TR_X, TR_OS, TR_MV, TR_OM, TR_DV, TR_OA, TR_OD = range(0, 7 * NT, NT)


class Signal:

    def __init__(self, sem, per):
        self.sem, self.per = sem, per

    def at(self, layer, k):
        return layer * self.per + k


def trunk(nc, x_t, w_stream, w_heads, params, consts, out):
    ctx = ExitStack()
    with ctx:
        def sb(name, shape, dtype=FP32):
            return ctx.enter_context(nc.sbuf_tensor(name, shape, dtype))

        def overlaid(name, shape, dtype, at):
            return nc.alloc_sbuf_tensor_at(name, shape, dtype, offset=at)

        def signal(name, per):
            return Signal(ctx.enter_context(nc.semaphore(name)), per)

        h = sb("h", [P, KD, T])
        proj_at = nc.sbuf_base
        proj = sb("proj", [P, N_IN * T])
        proj_r = overlaid("proj_r", [P, N_IN * T], FP32R, proj_at)
        mix = sb("mix", [P, KM * T], FP32R)
        raw = sb("raw", [P, RAW, SLOT])
        parts_at = nc.sbuf_base
        parts = sb("parts", [P, PARTS, 2, SLOT], FP32R)
        w_head = overlaid("w_head", [P, 4, SLOT], FP32, parts_at)
        o_at = nc.sbuf_base
        o_tok = sb("o_tok", [P, NT, 512])
        o_tok_r = overlaid("o_tok_r", [P, 4 * T], FP32R, o_at)
        v_tok = sb("v_tok", [P, NT * ML_H * (ML_V + 1)])
        sq = sb("sq", [P, 2, T])
        rstd = sb("rstd", [P, T])
        rstd2 = sb("rstd2", [P, T])
        ebuf = sb("ebuf", [P, 2, T])
        mbuf = sb("mbuf", [P, 2, WIDE])
        qh = sb("qh", [P, 2, WIDE])
        kh = sb("kh", [P, 2, T])
        rows = qh[:, 0, 0:T]
        cols = sb("cols", [P, NT, NCOL])
        enm = sb("enm", [P, NT, 2 * ML_H])
        con = sb("con", [P, N_CONST])
        par = sb("par", [P, DEPTH, N_PARAM])
        sums = sb("sums", [P, 4])
        negmax = sb("negmax", [P, 2])
        rowmax = sb("rowmax", [P, 2])
        rsum = sb("rsum", [P, 2])
        ea = sb("ea", [P, 1])
        lam_p = sb("lam_p", [P, 2, DIFF_QK])
        lam_s = sb("lam_s", [P, 2])
        lam_e = sb("lam_e", [P, 2])
        neg_lam = sb("neg_lam", [P, 1])
        gain_d = sb("gain_d", [P, 1])
        eps = sb("eps", [P, 1])
        den = sb("den", [P, NT])
        den2 = sb("den2", [P, NT])
        hs = sb("hs", [P, 4 * NT])
        pb = ctx.enter_context(nc.psum_tensor("pb", [P, 8, 512], FP32))

        def C(name, rows_=slice(0, P)):
            return con[rows_, CONST[name][0]:CONST[name][1]]

        def par_at(layer, name, i=0, n=1, rows_=slice(0, P)):
            a = PARAM[name][0] + i
            return par[rows_, layer, a:a + n]

        def tile_of(buf, k, a=0, b=T, rows_=slice(0, P)):
            return buf[rows_, k * T + a:k * T + b]

        def halves(ap):
            return ap.rearrange("p (a b) -> p a b", b=HALF)

        def pair(p, rows_=slice(0, P)):
            return pb[rows_, 2 * p:2 * p + 2, 0:HALF]

        def span(p, width, rows_):
            return pair(p, rows_) if width == T else pb[rows_, 2 * p, 0:width]

        def like(ap, width):
            return halves(ap) if width == T else ap

        def token_major(buf, tile0):
            return buf[:, tile0 * T:tile0 * T + NT * 512].rearrange("p (i f) -> p i f", f=512)

        x_tok = v_tok[:, 0:NT * 512].rearrange("p (i f) -> p i f", f=512)
        v_ml = v_tok[:, :].rearrange("p (i h v) -> p i h v", h=ML_H, v=ML_V + 1)
        o_ml = o_dif = o_tok
        v_mla = v_dif = x_tok

        def cb(g, j, a, b, rows_):
            if j == NT - 1:
                return (qh[rows_, 1, a:b], kh[rows_, 1, a:b])[g]
            return tile_of(proj, (XS, DV)[g] + j, a, b, rows_)

        def xg_parts(k):
            return tile_of(mix, k), tile_of(mix, KD + k)

        def ffn_parts(k):
            return tile_of(proj_r, DQ + k), tile_of(proj_r, DQ + KD + k)

        MIXED = [ZT + f for f in range(4)] + [MO + f for f in range(4)] + [CQ + f for f in range(4)] + [DV + f for f in range(4)]

        def mixed_parts(k):
            return tile_of(mix, k), tile_of(proj_r, MIXED[k])

        def act_parts(k):
            lead = tile_of(proj_r, k if k < DQ else k + KM)
            rest = tile_of(mix, k) if k < KM else tile_of(proj_r, N_IN - 2 + k - KM) if k < KM + 2 else tile_of(o_tok_r, k - KM - 2)
            return lead, rest

        def rng(d, j):
            return (TILES[j][0], T) if d == 0 else (0, TILES[j][0] + TILES[j][1])

        def mask(d, j):
            a = 0 if d == 0 else P + (NT - 1) * P - TILES[j][0]
            lo, hi = rng(d, j)
            c = CONST["mask"][0] + a
            return con[0:TILES[j][1], c:c + hi - lo]

        def unit(u):
            if u < 2 * SSD_H:
                return u // 2, u % 2, (u % 2) * SSD_H + u // 2
            v = u - 2 * SSD_H
            return v // 2, v % 2, 2 * SSD_H + (v % 2) * ML_H + v // 2

        def att(n):
            if n < N_ATT_M:
                hd, i = n // NT, n % NT
                return (qh[0:MLA_QK, hd % 2, i * P:(i + 1) * P], kh[0:MLA_QK, hd % 2, :],
                        lambda j: v_mla[0:TILES[j][1], j, hd * MLA_V:(hd + 1) * MLA_V], MLA_V, MLA_QK ** -0.5, i, hd)
            hd, i = (n - N_ATT_M) // NT, (n - N_ATT_M) % NT
            r = slice(64 * (hd % 2), 64 * (hd % 2) + 64)
            return (tile_of(proj, DQ + hd // 2, i * P, (i + 1) * P, r), tile_of(proj, DK + hd // 2, rows_=r),
                    lambda j: v_dif[0:TILES[j][1], j, (hd // 2) * DIFF_V:(hd // 2 + 1) * DIFF_V], DIFF_V, DIFF_QK ** -0.5, i, hd)

        def prepare(prep, n, stages=range(6)):
            hd, i = n // NT, n % NT
            stage, ahead = ((2, 1), (4, 1), (5, 1), (0, 2), (1, 2))[i]
            if hd + ahead < MLA_H and stage in stages:
                prep(stage, hd + ahead)

        TURN, TAIL_O = 4, 5
        def bank_pair(g):
            if G_SSD <= g < G_ML:
                return 2
            if G_ML <= g < G_OUT2:
                return 3
            return 1 + g % 3

        def raw_slot(layer, s):
            return (layer * N_RAW + s + (s >= N_IN)) % RAW

        def slot_end(g):
            return g + 1 if g < G_FOUT else S_FOUT + 3 * (g - G_FOUT + 1)

        const_in = signal("const_in", 0)
        table_in = signal("table_in", 0)
        eps_ready = signal("eps_ready", 0)
        par_in = signal("par_in", 0)
        x_in = [signal(f"x_in{k}", 0) for k in range(KD)]
        cleared = signal("cleared", 0)
        loaded = [signal(f"loaded{s}", 0) for s in range(RAW)]
        head_in = [signal(f"head_in{s}", 1) for s in range(4)]
        lead_ready = signal("lead_ready", N_SLOT)
        split = signal("split", N_SLOT)
        mixed_lead = signal("mixed_lead", KD)
        mixed = signal("mixed", KM)
        w_used = signal("w_used", N_SLOT)
        evac = signal("evac", N_GROUP)
        xg_ready = signal("xg_ready", 2 * KD)
        sq_ready = signal("sq_ready", N_SQ)
        sq_used = signal("sq_used", N_SQ)
        rs_ready = signal("rs_ready", N_RS)
        rs_used = signal("rs_used", 8 + 1 + 2 + 2 * MLA_H)
        conv_ready = signal("conv_ready", 6)
        conv_act = signal("conv_act", 6)
        z_act = signal("z_act", 4)
        o_tanh = signal("o_tanh", 4)
        o_sig = signal("o_sig", 4)
        dec_u = signal("dec_u", 1)
        dec_ln = signal("dec_ln", 1)
        rows_ready = signal("rows_ready", 1)
        cols_ps = signal("cols_ps", 1)
        cols_ready = signal("cols_ready", 1)
        enm_ready = signal("enm_ready", 1)
        rot_ready = signal("rot_ready", 8 + 2 * MLA_H)
        rot_used = signal("rot_used", 2 * MLA_H)
        roped = signal("roped", 8 + 2 * MLA_H)
        qcos = signal("qcos", 8)
        tr_ready = signal("tr_ready", 7 * NT)
        tr_evac = signal("tr_evac", 7 * NT)
        cb_ps = signal("cb_ps", 2 * NT)
        cb_ready = signal("cb_ready", 2 * NT)
        rowb = signal("rowb", 2 * (SSD_H + ML_H))
        e_raw = signal("e_raw", STEPS)
        e_exp = signal("e_exp", STEPS)
        m_ready = signal("m_ready", STEPS)
        m_used = signal("m_used", STEPS)
        qk_ps = signal("qk_ps", STEPS_ML)
        y_evac = signal("y_evac", SSD_H)
        nd_evac = signal("nd_evac", 2 * ML_H)
        osq = signal("osq", 3 * NT)
        ored = signal("ored", 3 * NT)
        orstd = signal("orstd", 3)
        oscaled = signal("oscaled", 3 * NT)
        v_ps = signal("v_ps", NT)
        v_ready = signal("v_ready", NT)
        p_ps = signal("p_ps", 2 * MLA_H)
        p_copy = signal("p_copy", 2 * MLA_H)
        s_ps = signal("s_ps", N_ATT)
        max_ready = signal("max_ready", N_ATT)
        p_ready = signal("p_ready", N_ATT)
        t_ps = signal("t_ps", N_ATT)
        tail_ps = signal("tail_ps", N_ATT)
        pt_main = signal("pt_main", N_ATT)
        pt_tail = signal("pt_tail", N_ATT)
        o_ps = signal("o_ps", N_ATT)
        o_evac = signal("o_evac", N_ATT)
        lam_sum = signal("lam_sum", 1)
        lam_exp = signal("lam_exp", 1)
        gsilu = signal("gsilu", KF)
        act_ready = signal("act_ready", KF)
        stored = signal("stored", 0)
        dve_chain = signal("dve_chain", 0)
        act_chain = signal("act_chain", 0)

        block = ctx.enter_context(nc.Block())

        @block.sync
        def _(sp):
            for k in range(KD):
                sp.dma_start(h[:, k, :], x_t[:, k, :]).then_inc(x_in[k].sem, 16)
                if k == 0:
                    sp.dma_start(par[:, :, :], params).then_inc(par_in.sem, 16)
                    sp.dma_start(con[:, 0:2 * P], consts[:, 0:2 * P]).then_inc(const_in.sem, 16)
            def released(r):
                l, s = r // N_RAW, r % N_RAW
                return (v_ps.sem, v_ps.at(l, NT)) if s == N_IN else (split.sem, split.at(l, s + 1 if s < N_IN else s))

            for n in range(DEPTH * N_RAW):
                l, s = n // N_RAW, n % N_RAW
                if n == RAW:
                    sp.dma_start(con[:, 2 * P:N_CONST], consts[:, 2 * P:N_CONST]).then_inc(table_in.sem, 16)
                if n >= RAW:
                    sp.wait_ge(*released(n - RAW))
                sp.dma_start(raw[:, n % RAW, :], w_stream[n, :, :]).then_inc(loaded[n % RAW].sem, 16)
                if s == N_IN:
                    sp.wait_ge(w_used.sem, w_used.at(l, N_IN))
                    for c in range(4):
                        sp.dma_start(w_head[:, c, :], w_heads[4 * l + c, :, :]).then_inc(head_in[c].sem, 16)
            for k in range(KD):
                sp.wait_ge(evac.sem, evac.at(DEPTH - 1, G_FOUT + k + 1))
                sp.dma_start(out[:, k, :], h[:, k, N_META:T]).then_inc(stored.sem, 16)
            sp.wait_ge(stored.sem, 16 * KD)

        @block.gpsimd
        def _(pool):
            nc.gpsimd.memset(v_tok[:, :], 0.0).then_inc(cleared.sem, 1)
            nc.gpsimd.memset(mbuf[:, :, :], 0.0).then_inc(cleared.sem, 1)
            nc.gpsimd.memset(qh[:, :, :], 0.0).then_inc(cleared.sem, 1)
            nc.gpsimd.memset(cols[:, :, :], 0.0).then_inc(cleared.sem, 1)
            nc.gpsimd.memset(o_tok[:, :, :], 0.0).then_inc(cleared.sem, 1)
            pool.wait_ge(table_in.sem, 16)
            def rest(l, s):
                n = l * N_SLOT + s
                w = raw[:, raw_slot(l, s), :]
                pool.wait_ge(lead_ready.sem, n + 1)
                nc.gpsimd.tensor_tensor(parts[:, n % PARTS, 1, :], w, parts[:, n % PARTS, 0, :].bitcast(FP32),
                                        ALU.subtract).then_inc(split.sem, 1)

            for l in range(DEPTH):
                for s in range(N_SLOT):
                    rest(l, s)
                    if MO + 1 <= s < MO + 5:
                        f = s - MO - 1
                        pool.wait_ge(o_tanh.sem, o_tanh.at(l, f + 1))
                        nc.gpsimd.tensor_scalar(tile_of(proj, MO + f), tile_of(proj, MO + f), 0.5, 0.5,
                                                ALU.mult, ALU.add).then_inc(o_sig.sem, 1)
                    if s == N_IN - 1:
                        pool.wait_ge(w_used.sem, w_used.at(l, N_IN))
                        pool.wait_ge(rs_used.sem, rs_used.at(l, 9))
                        pool.wait_ge(tr_evac.sem, tr_evac.at(l, TR_OM + NT))
                        for k in range(KD):
                            lead, other = mixed_parts(k)
                            nc.gpsimd.tensor_copy(lead, tile_of(proj, MIXED[k])).then_inc(mixed_lead.sem, 1)
                            pool.wait_ge(mixed_lead.sem, mixed_lead.at(l, k + 1))
                            nc.gpsimd.tensor_tensor(other, tile_of(proj, MIXED[k]), lead.bitcast(FP32),
                                                    ALU.subtract).then_inc(mixed.sem, 1)
                    t = s - G_SSD - 4
                    if 0 <= t < 8:
                        pool.wait_ge(rs_used.sem, rs_used.at(l, t + 1))
                        pool.wait_ge(rot_ready.sem, rot_ready.at(l, t + 1))
                        nc.gpsimd.tensor_tensor(tile_of(proj, DQ + t), tile_of(proj, DQ + t), C("cos_d"),
                                                ALU.mult).then_inc(qcos.sem, 1)

        @block.tensor
        def _(pe):
            def product(p, lhs_t, rhs, start, stop, rows_=slice(0, P)):
                for a in range(2):
                    last = nc.tensor.matmul(pb[rows_, 2 * p + a, 0:HALF], lhs_t, rhs[:, a * HALF:(a + 1) * HALF],
                                            start=start, stop=stop)
                return last

            def norm_sum(l, s0, n, p, rows_=slice(0, P), stops=True, starts=True, ones="ones"):
                for k in range(n):
                    pe.wait_ge(sq_ready.sem, sq_ready.at(l, s0 + k + 1))
                    product(p, C(ones, rows_), sq[rows_, (s0 + k) % 2, :], starts and k == 0, stops and k == n - 1).then_inc(sq_used.sem, 1)

            def split_product(l, g, k0, k1, operand):
                p = bank_pair(g)
                k_all = KF if g >= G_FOUT else KD
                for k in range(k0, k1):
                    s = g + k // KD if g < G_FOUT else S_FOUT + 3 * (g - G_FOUT) + k // KD
                    n = l * N_SLOT + s
                    if k % KD == 0:
                        pe.wait_ge(split.sem, n + 1)
                    c = k % KD
                    w_lead = parts[:, n % PARTS, 0, c * P:(c + 1) * P]
                    w_rest = parts[:, n % PARTS, 1, c * P:(c + 1) * P]
                    lead, rest = operand(k)
                    product(p, w_lead, lead, k == 0, False)
                    product(p, w_lead, rest, False, False)
                    last = product(p, w_rest, lead, False, k == k_all - 1)
                    if c == KD - 1 or k == k_all - 1:
                        last.then_inc(w_used.sem, 1)

            def dense(l, g, operand):
                pe.wait_ge(evac.sem, evac.at(l, max(g - 2, 0)))
                split_product(l, g, 0, KF if g >= G_FOUT else KD, operand)

            def beside(l, g, j, operand, chunks):
                if chunks[j][0] == 0 and chunks[j][1] > 0:
                    pe.wait_ge(evac.sem, evac.at(l, g))
                split_product(l, g, *chunks[j], operand)

            def row_bcast(l, u, p):
                pe.wait_ge(e_raw.sem, e_raw.at(l, u * NT))
                r = C("rowsel")[:, unit(u)[2]:unit(u)[2] + 1].to_broadcast([P, P])
                product(p, r, rows, True, True).then_inc(rowb.sem, 1)

            def out_transposes(l, idx, src, i):
                b = 4 + idx % 2
                pe.wait_ge(tr_evac.sem, tr_evac.at(l, max(idx - 1, 0)))
                for f in range(4):
                    last = src(b, f, i)
                last.then_inc(tr_ready.sem, 1)

            def to_tokens(tile0):
                def one(b, f, i):
                    a, w = TILES[i]
                    return nc.tensor.transpose(pb[0:w, b, f * P:(f + 1) * P], tile_of(proj, tile0 + f, a, a + w), C("ident"))
                return one

            def to_features(buf):
                def one(b, f, i):
                    w = TILES[i][1]
                    return nc.tensor.transpose(pb[:, b, f * P:f * P + w], buf[0:w, i, f * P:(f + 1) * P],
                                               C("ident")[0:w, 0:w])
                return one

            pe.wait_ge(const_in.sem, 16)
            pe.wait_ge(cleared.sem, 5)
            for l in range(DEPTH):
                if l == 0:
                    norm_sum(l, SQ_A, KD, 0)

                for g in range(G_SSD):
                    if g == 0:
                        for k in range(KD):
                            pe.wait_ge(xg_ready.sem, xg_ready.at(l, k + 1))
                            pe.wait_ge(evac.sem, evac.at(l, 0))
                            split_product(l, 0, k, k + 1, xg_parts)
                    else:
                        dense(l, g, xg_parts)

                pe.wait_ge(evac.sem, evac.at(l, G_SSD))
                pe.wait_ge(rows_ready.sem, rows_ready.at(l, 1))
                for i, (a, w) in enumerate(TILES):
                    o = pb[0:w, 7, i * NCOL:(i + 1) * NCOL]
                    nc.tensor.matmul(o, rows[:, a:a + w], C("lin_rs"), start=True, stop=False)
                    nc.tensor.matmul(o, kh[0:NDEC, 1, a:a + w], C("lin_i", slice(0, NDEC)), start=False, stop=False)
                    last = nc.tensor.matmul(o, mbuf[0:NDEC, 1, a:a + w], C("lin_sp", slice(0, NDEC)), start=False, stop=True)
                last.then_inc(cols_ps.sem, 1)

                pe.wait_ge(conv_act.sem, conv_act.at(l, 6))
                for i in range(NT):
                    out_transposes(l, TR_X + i, to_tokens(XS), i)
                row_bcast(l, 0, 0)
                for g in range(SSD_G):
                    r = slice(64 * g, 64 * g + 64)
                    for j, (a, w) in enumerate(TILES):
                        pe.wait_ge(tr_evac.sem, tr_evac.at(l, TR_X + NT))
                        pe.wait_ge(cb_ready.sem, cb_ready.at(l, g * NT + j))
                        product(2, tile_of(proj, BM, a, a + w, r), tile_of(proj, CM, rows_=r), True, True,
                                slice(0, w)).then_inc(cb_ps.sem, 1)
                pe.wait_ge(cols_ready.sem, cols_ready.at(l, 1))
                pe.wait_ge(cb_ready.sem, cb_ready.at(l, 2 * NT))
                for u in range(2 * SSD_H):
                    hd, d, _ = unit(u)
                    if d == 0:
                        pe.wait_ge(y_evac.sem, y_evac.at(l, max(hd - 1, 0)))
                    for j, (_, kw) in enumerate(TILES):
                        n = u * NT + j
                        if j == NT - 1 and u + 1 < 2 * SSD_H:
                            row_bcast(l, u + 1, 0)
                        pe.wait_ge(m_ready.sem, m_ready.at(l, n + 1))
                        blocks = range(j, NT) if d == 0 else range(j + 1)
                        lo = rng(d, j)[0]
                        for i in blocks:
                            last = nc.tensor.matmul(pb[:, 6 + hd % 2, i * SSD_P:(i + 1) * SSD_P],
                                                    mbuf[0:kw, n % 2, i * P - lo:i * P - lo + P],
                                                    x_tok[0:kw, j, hd * SSD_P:(hd + 1) * SSD_P],
                                                    start=(d == 0 and j == 0 and i == 0), stop=(d == 1 and j == NT - 1),
                                                    skip_group_check=True)
                        last.then_inc(m_used.sem, 1)
                        beside(l, G_SSD + u, j, xg_parts, CHUNKS_SSD)
                        if j == 0 and 0 <= u - 4 < 8:
                            pe.wait_ge(rs_ready.sem, rs_ready.at(l, RS_D + min(u - 2, 8)))
                            pe.wait_ge(rs_used.sem, rs_used.at(l, u - 3))
                            product(1, C("perm_d"), tile_of(proj, DQ + u - 4), True, True).then_inc(rot_ready.sem, 1)
                        if j == 2 and 0 <= u - 2 < 8:
                            pe.wait_ge(roped.sem, roped.at(l, max(u - 3, 0)))
                            norm_sum(l, SQ_D + u - 2, 1, 1, ones="ones_h")

                pe.wait_ge(y_evac.sem, y_evac.at(l, SSD_H))
                pe.wait_ge(evac.sem, evac.at(l, G_ML))
                for i in range(NT):
                    out_transposes(l, TR_OS + i, to_features(o_tok), i)
                for i in range(NT):
                    out_transposes(l, TR_MV + i, to_tokens(MV), i)
                norm_sum(l, SQ_S, 4, 3)

                def qk(n):
                    u, j = 2 * SSD_H + n // NT, n % NT
                    hd, d, _ = unit(u)
                    a, w = TILES[j]
                    lo, hi = rng(d, j)
                    r = slice(64 * (hd % 2), 64 * (hd % 2) + 64)
                    k_t = tile_of(proj, MK + hd // 2, a, a + w, r)
                    q_t = tile_of(proj, MQ + hd // 2, rows_=r)
                    if hi - lo == T:
                        product(1, k_t, q_t, True, True, slice(0, w)).then_inc(qk_ps.sem, 1)
                    else:
                        nc.tensor.matmul(pb[0:w, 2, 0:hi - lo], k_t, q_t[:, lo:hi], start=True, stop=True).then_inc(qk_ps.sem, 1)

                row_bcast(l, 2 * SSD_H, 0)
                pe.wait_ge(roped.sem, roped.at(l, 8))
                qk(0)
                pe.wait_ge(tr_evac.sem, tr_evac.at(l, TR_MV + NT))
                pe.wait_ge(rs_ready.sem, rs_ready.at(l, RS_S + 1))
                pe.wait_ge(roped.sem, roped.at(l, 8))
                for n in range(STEPS_ML):
                    v, j = n // NT, n % NT
                    hd, d, _ = unit(2 * SSD_H + v)
                    if j == NT - 1 and v + 1 < 2 * ML_H:
                        row_bcast(l, 2 * SSD_H + v + 1, 0)
                    pe.wait_ge(m_ready.sem, m_ready.at(l, STEPS_SSD + n + 1))
                    if n + 1 < STEPS_ML:
                        qk(n + 1)
                    if j == 0:
                        pe.wait_ge(nd_evac.sem, nd_evac.at(l, v))
                    kw = TILES[j][1]
                    lo = rng(d, j)[0]
                    for i in (range(j, NT) if d == 0 else range(j + 1)):
                        first = (j == 0 and i in (0, 3)) if d == 0 else (i, j) in ((0, 0), (3, 3))
                        c = (i % 3) * (ML_V + 1)
                        last = nc.tensor.matmul(pb[:, 4 + i // 3, c:c + ML_V + 1],
                                                mbuf[0:kw, (STEPS_SSD + n) % 2, i * P - lo:i * P - lo + P],
                                                v_ml[0:kw, j, hd, :], start=first, stop=(j == NT - 1), skip_group_check=True)
                    last.then_inc(m_used.sem, 1)
                    if v in JOB_UNITS and j == 0:
                        pe.wait_ge(evac.sem, evac.at(l, G_ML + v))
                        norm_sum(l, *JOB_UNITS[v][0:2], 3)
                    if v in JOB_UNITS and j == 2:
                        pe.wait_ge(rs_ready.sem, rs_ready.at(l, JOB_UNITS[v][2] + 1))
                    beside(l, G_ML + v, j, xg_parts, LATE_CHUNKS if v in JOB_UNITS else CHUNKS_ML)
                for j in range(NT):
                    beside(l, N_IN - 1, j, xg_parts, CHUNKS_DIFF)

                n_uv = l * N_RAW + N_IN
                pe.wait_ge(loaded[n_uv % RAW].sem, 16 * (n_uv // RAW + 1))
                w = raw[:, n_uv % RAW, :]
                pe.wait_ge(nd_evac.sem, nd_evac.at(l, 2 * ML_H))
                pe.wait_ge(rs_used.sem, rs_used.at(l, 11))
                for i, (a, wd) in enumerate(TILES):
                    pe.wait_ge(v_ready.sem, v_ready.at(l, max(i - 1, 0)))
                    for c in range(2):
                        last = nc.tensor.matmul(pb[0:wd, 4 + i % 2, 0:512], tile_of(proj, CKV + c, a, a + wd),
                                                w[:, c * 512:(c + 1) * 512], start=(c == 0), stop=(c == 1))
                    last.then_inc(v_ps.sem, 1)
                pe.wait_ge(evac.sem, evac.at(l, N_IN))

                def prep(stage, hd):
                    side, what = stage // 3, stage % 3
                    e = 2 * hd + side
                    rws = slice(0, MLA_QK)
                    if what == 0:
                        pe.wait_ge(rot_used.sem, rot_used.at(l, e))
                        pe.wait_ge(rs_ready.sem, rs_ready.at(l, RS_M + e))
                        c_w = 0 if side else 1 + hd // UQ_HEADS
                        pe.wait_ge(head_in[c_w].sem, 16 * (l + 1))
                        if side == 0:
                            w, m, n, t0 = w_head[:, c_w, :], MLA_QK, 3, CQ
                            o = (hd % UQ_HEADS) * 3 * MLA_QK
                        else:
                            w, m, n, t0 = w_head[:, c_w, :], MLA_NOPE, 2, CKV
                            o = hd * 2 * MLA_NOPE
                        for c in range(n):
                            last = product(3, w[:, o + c * m:o + (c + 1) * m], tile_of(proj, t0 + c), c == 0, c == n - 1,
                                           slice(0, m))
                        last.then_inc(p_ps.sem, 1)
                    elif what == 1:
                        pe.wait_ge(p_copy.sem, p_copy.at(l, e + 1))
                        norm_sum(l, SQ_M + e, 1, 3, rws)
                    else:
                        pe.wait_ge(rs_used.sem, rs_used.at(l, 11 + e + 1))
                        product(3, C("perm_m", rws)[:, 0:MLA_QK], (qh, kh)[side][rws, hd % 2, 0:T], True, True,
                                rws).then_inc(rot_ready.sem, 1)

                def scores(n):
                    q, k, _, _, _, i, hd = att(n)
                    pe.wait_ge(p_ready.sem, p_ready.at(l, max(n - 1, 0)))
                    if n < N_ATT_M and i == 0:
                        pe.wait_ge(roped.sem, roped.at(l, 8 + 2 * hd + 2))
                    product(n % 2, q, k, True, True).then_inc(s_ps.sem, 1)

                def turn(n):
                    pe.wait_ge(p_ready.sem, p_ready.at(l, n + 1))
                    pe.wait_ge(o_evac.sem, o_evac.at(l, max(n - 1, 0)))
                    pe.wait_ge(pt_tail.sem, pt_tail.at(l, n))
                    a, w = TILES[-1]
                    nc.tensor.transpose(pb[0:w, TAIL_O, 0:P], ebuf[:, n % 2, a:a + w], C("ident")).then_inc(tail_ps.sem, 1)
                    pe.wait_ge(pt_main.sem, pt_main.at(l, n))
                    for j, (a, w) in enumerate(TILES[:-1]):
                        last = nc.tensor.transpose(pb[:, TURN, j * P:(j + 1) * P], ebuf[:, n % 2, a:a + w], C("ident"))
                    last.then_inc(t_ps.sem, 1)

                def values(n):
                    _, _, v, dv, _, _, _ = att(n)
                    pe.wait_ge(pt_main.sem, pt_main.at(l, n + 1))
                    pe.wait_ge(pt_tail.sem, pt_tail.at(l, min(n + 2, N_ATT_M if n < N_ATT_M else N_ATT)))
                    pe.wait_ge(o_evac.sem, o_evac.at(l, n))
                    for j, (_, w) in enumerate(TILES):
                        last = nc.tensor.matmul(pb[:, TAIL_O, P:P + dv], mbuf[0:w, n % 2, j * P:(j + 1) * P],
                                                v(j), start=(j == 0), stop=(j == NT - 1))
                    last.then_inc(o_ps.sem, 1)

                pe.wait_ge(v_ready.sem, v_ready.at(l, NT))
                for i in range(NT):
                    pe.wait_ge(oscaled.sem, oscaled.at(l, i + 1))
                    out_transposes(l, TR_OM + i, to_features(o_ml), i)
                for s in range(8):
                    prep(s % 6, s // 6)
                pe.wait_ge(tr_evac.sem, tr_evac.at(l, TR_OM + NT))
                scores(0)
                for n in range(N_ATT_M):
                    hd, i = n // NT, n % NT
                    if n + 1 < N_ATT_M:
                        scores(n + 1)
                    turn(n)
                    prepare(prep, n)
                    if n >= 1:
                        values(n - 1)
                    if i == 0 and hd + 1 < MLA_H:
                        prep(3, hd + 1)
                values(N_ATT_M - 1)

                pe.wait_ge(o_evac.sem, o_evac.at(l, N_ATT_M))
                for i in range(NT):
                    out_transposes(l, TR_DV + i, to_tokens(DV), i)
                for i in range(NT):
                    pe.wait_ge(oscaled.sem, oscaled.at(l, NT + i + 1))
                    out_transposes(l, TR_OA + i, to_features(o_tok), i)
                pe.wait_ge(tr_evac.sem, tr_evac.at(l, TR_OA + NT))
                scores(N_ATT_M)
                for n in range(N_ATT_M, N_ATT):
                    if n + 1 < N_ATT:
                        scores(n + 1)
                    turn(n)
                    if n == N_ATT_M:
                        pe.wait_ge(mixed.sem, mixed.at(l, KD))
                    beside(l, G_OUT1 + (n - N_ATT_M) // NT, n % NT, mixed_parts, CHUNKS_DIFF)
                    if n > N_ATT_M:
                        values(n - 1)
                values(N_ATT - 1)
                pe.wait_ge(o_evac.sem, o_evac.at(l, N_ATT))
                for i in range(NT):
                    pe.wait_ge(oscaled.sem, oscaled.at(l, 2 * NT + i + 1))
                    out_transposes(l, TR_OD + i, to_features(o_dif), i)

                pe.wait_ge(tr_evac.sem, tr_evac.at(l, TR_OD + NT))
                pe.wait_ge(p_ready.sem, p_ready.at(l, N_ATT))
                pe.wait_ge(evac.sem, evac.at(l, G_OUT2))
                for k in range(KD):
                    pe.wait_ge(mixed.sem, mixed.at(l, KD + k + 1))
                    split_product(l, G_OUT2, k, k + 1, lambda k: mixed_parts(KD + k))
                for g in range(1, KD):
                    dense(l, G_OUT2 + g, lambda k: mixed_parts(KD + k))
                    norm_sum(l, SQ_F + g - 1, 1, 0, starts=(g == 1), stops=False)

                for k in range(KD):
                    pe.wait_ge(xg_ready.sem, xg_ready.at(l, KD + k + 1))
                    if k == 0:
                        pe.wait_ge(evac.sem, evac.at(l, G_FIN - 2))
                    split_product(l, G_FIN, k, k + 1, ffn_parts)
                norm_sum(l, SQ_F + KD - 1, 1, 0, starts=False)
                for g in range(1, 2 * KF):
                    dense(l, G_FIN + g, ffn_parts)
                for k in range(KF):
                    if k == 0:
                        pe.wait_ge(evac.sem, evac.at(l, G_FOUT - 2))
                    pe.wait_ge(act_ready.sem, act_ready.at(l, k + 1))
                    split_product(l, G_FOUT, k, k + 1, act_parts)
                for g in range(1, KD):
                    dense(l, G_FOUT + g, act_parts)
                    if l + 1 < DEPTH:
                        norm_sum(l + 1, SQ_A + g - 1, 1, 0, starts=(g == 1), stops=False)
                if l + 1 < DEPTH:
                    norm_sum(l + 1, SQ_A + KD - 1, 1, 0, starts=False)

        @block.scalar
        def _(act):
            chained = [0]

            def link(ins):
                chained[0] += 1
                ins.then_inc(act_chain.sem, 1)
                act.wait_ge(act_chain.sem, chained[0])

            def square(l, s, src, rows_=slice(0, P)):
                act.wait_ge(sq_used.sem, sq_used.at(l, max(s - 1, 0)))
                nc.scalar.activation(halves(sq[rows_, s % 2, :]), src, ACT.Square).then_inc(sq_ready.sem, 1)

            def rsqrt(l, s, p, n, dst, rows_=slice(0, P)):
                act.wait_ge(sq_used.sem, sq_used.at(l, s))
                link(nc.scalar.activation(halves(dst[rows_, :]), pair(p, rows_), ACT.Ln, scale=1.0 / n, bias=eps[rows_, :]))
                nc.scalar.activation(dst[rows_, :], dst[rows_, :], ACT.Exp, scale=-0.5).then_inc(rs_ready.sem, 1)

            def exps(l, n):
                u, j = n // NT, n % NT
                lo, hi = rng(unit(u)[1], j)
                e = ebuf[0:TILES[j][1], n % 2, 0:hi - lo]
                act.wait_ge(e_raw.sem, e_raw.at(l, n + 1))
                nc.scalar.activation(e, e, ACT.Exp).then_inc(e_exp.sem, 1)

            def out_squares(l, base, buf, width_rows=None):
                for i in range(NT):
                    if i >= 2:
                        act.wait_ge(ored.sem, ored.at(l, base + i - 1))
                    nc.scalar.activation(ebuf[:, i % 2, 0:512], buf[:, i, :], ACT.Square).then_inc(osq.sem, 1)

            def out_rstd(l, which, groups):
                act.wait_ge(ored.sem, ored.at(l, (which + 1) * NT))
                link(nc.scalar.activation(hs[:, 0:groups * NT], hs[:, 0:groups * NT], ACT.Ln, scale=groups / 512.0, bias=eps[:, :]))
                nc.scalar.activation(hs[:, 0:groups * NT], hs[:, 0:groups * NT], ACT.Exp, scale=-0.5).then_inc(orstd.sem, 1)

            def softmax(l, n):
                scale = att(n)[4]
                act.wait_ge(max_ready.sem, max_ready.at(l, n + 1))
                act.wait_ge(t_ps.sem, t_ps.at(l, max(n - 1, 0)))
                act.wait_ge(o_evac.sem, o_evac.at(l, max(n - 3, 0)))
                nc.scalar.activation(halves(ebuf[:, n % 2, :]), pair(n % 2), ACT.Exp, scale=scale, bias=negmax[:, n % 2:n % 2 + 1],
                                     accum_out=sums[:, n % 4:n % 4 + 1]).then_inc(p_ready.sem, 1)

            def turned(l, n):
                act.wait_ge(t_ps.sem, t_ps.at(l, n + 1))
                act.wait_ge(o_ps.sem, o_ps.at(l, max(n - 1, 0)))
                nc.scalar.activation(mbuf[:, n % 2, 0:512], pb[:, TURN, 0:512], ACT.Copy).then_inc(pt_main.sem, 1)

            def lead(l, s):
                l, s = l + s // N_SLOT, s % N_SLOT
                if l == DEPTH:
                    return
                n, r = l * N_SLOT + s, l * N_RAW + s + (s >= N_IN)
                act.wait_ge(loaded[r % RAW].sem, 16 * (r // RAW + 1))
                if n >= PARTS:
                    act.wait_ge(w_used.sem, n - PARTS + 1)
                if s == N_IN:
                    act.wait_ge(p_ps.sem, p_ps.at(l, 2 * MLA_H))
                nc.scalar.activation(parts[:, n % PARTS, 0, :], raw[:, r % RAW, :], ACT.Copy).then_inc(lead_ready.sem, 1)

            def residual_square(l, s0, k, ready):
                act.wait_ge(evac.sem, ready)
                square(l, s0 + k, halves(h[:, k, :]))

            act.wait_ge(par_in.sem, 16)
            act.wait_ge(eps_ready.sem, 1)
            for l in range(DEPTH):
                if l == 0:
                    nc.scalar.preload_act_table_set("natural_log_exp_and_others")
                    for k in range(KD):
                        act.wait_ge(x_in[k].sem, 16)
                        square(l, SQ_A + k, halves(h[:, k, :]))
                    lead(l, 0)
                    lead(l, 1)
                rsqrt(l, SQ_A + KD, 0, D_MODEL, rstd)

                nc.scalar.preload_act_table_set("silu_and_others")
                for g in range(1, G_SSD + 1):
                    if g < G_SSD:
                        lead(l, g + 1)
                    if 0 <= g - 2 < 6:
                        f = g - 2
                        act.wait_ge(conv_ready.sem, conv_ready.at(l, f + 1))
                        nc.scalar.activation(tile_of(proj, f), kh[:, f % 2, :], ACT.Silu).then_inc(conv_act.sem, 1)
                    if g == ZT + 1:
                        nc.scalar.preload_act_table_set("natural_log_exp_and_others")
                        d24 = slice(0, NDEC)
                        act.wait_ge(dec_u.sem, dec_u.at(l, 1))
                        link(nc.scalar.activation(ebuf[d24, 1, :], ebuf[d24, 0, :], ACT.Abs))
                        link(nc.scalar.activation(ebuf[d24, 1, :], ebuf[d24, 1, :], ACT.Exp, scale=-1.0))
                        link(nc.scalar.activation(ea[d24, :], par_at(l, "a_log", rows_=d24), ACT.Exp))
                        nc.scalar.activation(ebuf[d24, 1, :], ebuf[d24, 1, :], ACT.Ln, bias=1.0).then_inc(dec_ln.sem, 1)
                        act.wait_ge(lam_sum.sem, lam_sum.at(l, 1))
                        nc.scalar.activation(lam_e[:, :], lam_s[:, :], ACT.Exp).then_inc(lam_exp.sem, 1)
                        nc.scalar.preload_act_table_set("silu_and_others")
                    if g > MISC + 1:
                        act.wait_ge(evac.sem, evac.at(l, g))
                        t = tile_of(proj, g - 1)
                        if g - 1 < MO:
                            nc.scalar.activation(t, t, ACT.Silu).then_inc(z_act.sem, 1)
                        else:
                            nc.scalar.activation(t, t, ACT.Tanh, scale=0.5).then_inc(o_tanh.sem, 1)
                nc.scalar.preload_act_table_set("natural_log_exp_and_others")

                for n in range(STEPS_SSD):
                    u, j = n // NT, n % NT
                    exps(l, n)
                    if j == 1:
                        lead(l, G_SSD + u + 1)
                    if j == 2 and 0 <= u - 1 < 8:
                        act.wait_ge(evac.sem, evac.at(l, DQ + u))
                        square(l, SQ_D + u - 1, halves(tile_of(proj, DQ + u - 1)))
                    if j == NT - 1 and 0 <= u - 2 < 8:
                        act.wait_ge(rs_used.sem, rs_used.at(l, u - 2))
                        rsqrt(l, SQ_D + u - 1, 1, DIFF_QK, rstd2)
                act.wait_ge(cols_ready.sem, cols_ready.at(l, 1))
                nc.scalar.activation(enm[:, :, :], cols[:, :, C_NM:NCOL], ACT.Exp).then_inc(enm_ready.sem, 1)
                act.wait_ge(tr_evac.sem, tr_evac.at(l, TR_OS + NT))
                for f in range(4):
                    square(l, SQ_S + f, halves(tile_of(proj, ZT + f)))
                act.wait_ge(rs_used.sem, rs_used.at(l, 8))
                rsqrt(l, SQ_S + 4, 3, 512, rstd2)
                def tile_square(s, g):
                    act.wait_ge(evac.sem, evac.at(l, g + 1))
                    square(l, SQ_C + s, halves(tile_of(proj, g)))

                for n in range(STEPS_SSD, STEPS):
                    v, j = (n - STEPS_SSD) // NT, n % NT
                    exps(l, n)
                    if (v, j) in ((3, 2), (3, 3), (4, 0)):
                        s = (v - 3) * 2 + max(j - 2, 0)
                        tile_square(s, CQ + s)
                    if (v, j) in ((5, 2), (5, 3)):
                        tile_square(3 + j - 2, CKV + j - 2)
                    if (v, j) == (4, 1):
                        act.wait_ge(rs_used.sem, rs_used.at(l, 9))
                        rsqrt(l, SQ_C + 3, 3, Q_RANK, rstd2)
                    if (v, j) == (6, 1):
                        act.wait_ge(rs_used.sem, rs_used.at(l, 10))
                        rsqrt(l, SQ_C + 5, 3, KV_RANK, rstd2)
                    if j == 1:
                        lead(l, G_ML + v + 1)
                act.wait_ge(nd_evac.sem, nd_evac.at(l, 2 * ML_H))
                out_squares(l, 0, o_ml)
                out_rstd(l, 0, ML_H)

                rws = slice(0, MLA_QK)

                def prep(stage, hd):
                    side, what = stage // 3, stage % 3
                    e = 2 * hd + side
                    if what == 0:
                        act.wait_ge(p_copy.sem, p_copy.at(l, e + 1))
                        act.wait_ge(sq_used.sem, sq_used.at(l, SQ_M + e - 1))
                        nc.scalar.activation(sq[rws, (SQ_M + e) % 2, :], (qh, kh)[side][rws, hd % 2, 0:T],
                                             ACT.Square).then_inc(sq_ready.sem, 1)
                    elif what == 1:
                        act.wait_ge(rs_used.sem, rs_used.at(l, 11 + e))
                        rsqrt(l, SQ_M + e + 1, 3, MLA_QK, rstd2, rws)

                for s in range(8):
                    prep(s % 6, s // 6)
                softmax(l, 0)
                for n in range(N_ATT_M):
                    hd, i = n // NT, n % NT
                    if n + 1 < N_ATT_M:
                        softmax(l, n + 1)
                    turned(l, n)
                    prepare(prep, n)
                    if i == 0 and hd + 1 < MLA_H:
                        prep(3, hd + 1)
                    if hd == MLA_H - 1 and i in (1, 2):
                        lead(l, S_OUT1 + i - 1)
                act.wait_ge(o_evac.sem, o_evac.at(l, N_ATT_M))
                out_squares(l, NT, o_tok)
                out_rstd(l, 1, 1)
                softmax(l, N_ATT_M)
                for n in range(N_ATT_M, N_ATT):
                    if n + 1 < N_ATT:
                        softmax(l, n + 1)
                    turned(l, n)
                    g, i = (n - N_ATT_M) // NT, n % NT
                    if g and i == 1:
                        lead(l, S_OUT1 + g + 1)
                lead(l, S_OUT2 + 1)
                act.wait_ge(o_evac.sem, o_evac.at(l, N_ATT))
                out_squares(l, 2 * NT, o_dif)
                out_rstd(l, 2, DIFF_H)

                for k in range(KD):
                    lead(l, S_OUT2 + k + 2)
                    residual_square(l, SQ_F, k, evac.at(l, G_OUT2 + k + 1))
                rsqrt(l, SQ_F + KD, 0, D_MODEL, rstd)
                nc.scalar.preload_act_table_set("silu_and_others")
                for j in range(KF):
                    lead(l, S_FIN + 2 * j + 2)
                    act.wait_ge(evac.sem, evac.at(l, G_FIN + 2 * j + 1))
                    nc.scalar.activation(ebuf[:, j % 2, :], ebuf[:, j % 2, :], ACT.Silu).then_inc(gsilu.sem, 1)
                    lead(l, S_FIN + 2 * j + 3)
                if l + 1 < DEPTH:
                    nc.scalar.preload_act_table_set("natural_log_exp_and_others")
                for s in range(S_FOUT + 2, N_SLOT + 2):
                    lead(l, s)
                    k = s - S_FOUT - 4
                    if k >= 0 and k % 3 == 0 and l + 1 < DEPTH:
                        residual_square(l + 1, SQ_A, k // 3, evac.at(l, G_FOUT + k // 3 + 1))

        @block.vector
        def _(dve):
            chained = [0]

            def link(ins):
                chained[0] += 1
                ins.then_inc(dve_chain.sem, 1)
                dve.wait_ge(dve_chain.sem, chained[0])

            def gains(l, k, name, dst):
                lead, rest = dst(k)
                g = par_at(l, name, k)
                link(nc.vector.tensor_scalar(lead, h[:, k, :], g, None, ALU.mult))
                nc.vector.scalar_tensor_tensor(out=rest, in0=h[:, k, :], scalar=g, in1=lead.bitcast(FP32), op0=ALU.mult,
                                               op1=ALU.subtract).then_inc(xg_ready.sem, 1)

            def mixed_split(l, k):
                lead, rest = mixed_parts(k)
                link(nc.vector.tensor_copy(lead, tile_of(proj, MIXED[k])))
                nc.vector.tensor_tensor(rest, tile_of(proj, MIXED[k]), lead.bitcast(FP32), ALU.subtract).then_inc(mixed.sem, 1)

            def scale_out(l, g, dst):
                dve.wait_ge(w_used.sem, w_used.at(l, slot_end(g)))
                nc.vector.tensor_tensor(halves(dst), pair(bank_pair(g)), halves(rstd[:, :]), ALU.mult).then_inc(evac.sem, 1)

            def residual(l, g, k):
                dve.wait_ge(w_used.sem, w_used.at(l, slot_end(g)))
                nc.vector.tensor_tensor(halves(h[:, k, :]), halves(h[:, k, :]), pair(bank_pair(g)), ALU.add).then_inc(evac.sem, 1)

            def conv(l, f):
                if f >= 2:
                    dve.wait_ge(conv_act.sem, conv_act.at(l, f - 1))
                mid = TAPS // 2
                acc, src = kh[:, f % 2, :], tile_of(proj, f)
                link(nc.vector.tensor_scalar(acc, src, par_at(l, "conv_w", f * TAPS + mid), par_at(l, "conv_b", f), ALU.mult, ALU.add))
                shifts = [s for s in range(-mid, mid + 1) if s]
                for s in shifts:
                    a, b = max(0, -s), T - max(0, s)
                    ins = nc.vector.scalar_tensor_tensor(out=acc[:, a:b], in0=src[:, a + s:b + s],
                                                         scalar=par_at(l, "conv_w", f * TAPS + mid + s), in1=acc[:, a:b],
                                                         op0=ALU.mult, op1=ALU.add)
                    if s == shifts[-1]:
                        ins.then_inc(conv_ready.sem, 1)
                    else:
                        link(ins)

            def normed(l, src, gain, rows_=slice(0, P), count=True):
                ins = nc.vector.scalar_tensor_tensor(out=src, in0=src, scalar=gain, in1=rstd2[rows_, :], op0=ALU.mult, op1=ALU.mult)
                return ins.then_inc(rs_used.sem, 1) if count else ins

            def from_transposes(l, idx, dst, i, f_major=False, op=None):
                dve.wait_ge(tr_ready.sem, tr_ready.at(l, idx + 1))
                w = TILES[i][1]
                b = 4 + idx % 2
                src = pb[:, b, :].rearrange("p (f t) -> p f t", f=4)[:, :, 0:w] if f_major else pb[0:w, b, 0:512]
                op(dst, src).then_inc(tr_evac.sem, 1)

            def copy(dst, src):
                return nc.vector.tensor_copy(dst, src)

            def feature_block(buf, tile0, i):
                a, w = TILES[i]
                return buf[:, tile0 * T:(tile0 + 4) * T].rearrange("p (f t) -> p f t", t=T)[:, :, a:a + w]

            def exponents(l, n):
                u, j = n // NT, n % NT
                _, d, r = unit(u)
                lo, hi = rng(d, j)
                w = TILES[j][1]
                rw = slice(0, w)
                if j == 0:
                    dve.wait_ge(rowb.sem, rowb.at(l, u + 1))
                dve.wait_ge(m_ready.sem, m_ready.at(l, max(n - 1, 0)))
                e = ebuf[rw, n % 2, :]
                m = mask(d, j)
                runs = [(lo, hi)] if hi <= HALF or lo >= HALF else [(lo, HALF), (HALF, hi)]
                if (lo, hi) == (0, T):
                    ins = nc.vector.scalar_tensor_tensor(out=halves(e[:, 0:T]), in0=pair(0, rw), scalar=cols[rw, j, r:r + 1],
                                                         in1=halves(m), op0=ALU.add, op1=ALU.min)
                else:
                    for a, b in runs:
                        ins = nc.vector.scalar_tensor_tensor(out=e[:, a - lo:b - lo],
                                                             in0=pb[rw, a // HALF, a % HALF:a % HALF + b - a],
                                                             scalar=cols[rw, j, r:r + 1], in1=m[:, a - lo:b - lo],
                                                             op0=ALU.add, op1=ALU.min)
                ins.then_inc(e_raw.sem, 1)

            def weights(l, n):
                u, j = n // NT, n % NT
                hd, d, r = unit(u)
                lo, hi = rng(d, j)
                rw = slice(0, TILES[j][1])
                e, m = ebuf[rw, n % 2, 0:hi - lo], mbuf[rw, n % 2, 0:hi - lo]
                dve.wait_ge(e_exp.sem, e_exp.at(l, n + 1))
                dve.wait_ge(m_used.sem, m_used.at(l, max(n - 1, 0)))
                if u < 2 * SSD_H:
                    nc.vector.scalar_tensor_tensor(out=m, in0=e, scalar=cols[rw, j, C_DT + r:C_DT + r + 1],
                                                   in1=cb(hd // (SSD_H // SSD_G), j, lo, hi, rw), op0=ALU.mult,
                                                   op1=ALU.mult).then_inc(m_ready.sem, 1)
                else:
                    dve.wait_ge(qk_ps.sem, qk_ps.at(l, n - STEPS_SSD + 1))
                    nc.vector.scalar_tensor_tensor(out=like(m, hi - lo), in0=like(e, hi - lo), scalar=ML_QK ** -0.5,
                                                   in1=span(1, hi - lo, rw), op0=ALU.mult, op1=ALU.mult).then_inc(m_ready.sem, 1)

            def ssd_head(l, hd):
                dve.wait_ge(m_used.sem, m_used.at(l, (hd + 1) * 2 * NT))
                c = slice(hd * SSD_P, (hd + 1) * SSD_P)
                nc.vector.scalar_tensor_tensor(out=o_tok[:, :, c], in0=x_tok[:, :, c], scalar=par_at(l, "ssd_d", hd),
                                               in1=pb[:, 6 + hd % 2, 0:NT * SSD_P].rearrange("p (i v) -> p i v", v=SSD_P),
                                               op0=ALU.mult, op1=ALU.add).then_inc(y_evac.sem, 1)

            def ml_unit(l, v):
                hd, d, _ = unit(2 * SSD_H + v)
                dve.wait_ge(m_used.sem, m_used.at(l, STEPS_SSD + (v + 1) * NT))
                b = 4
                nc.vector.tensor_copy(den[:, 0:3], pb[:, b, ML_V:3 * (ML_V + 1):ML_V + 1])
                link(nc.vector.tensor_copy(den[:, 3:5], pb[:, b + 1, ML_V:2 * (ML_V + 1):ML_V + 1]))
                link(nc.vector.scalar_tensor_tensor(out=den2[:, :], in0=den[:, :], scalar=-1.0, in1=den[:, :], op0=ALU.mult, op1=ALU.max))
                link(nc.vector.tensor_tensor(den[:, :], den2[:, :], enm[:, :, d * ML_H + hd], ALU.max))
                link(nc.vector.reciprocal(den2[:, :], den[:, :]))
                for i in range(NT):
                    num = pb[:, b + i // 3, (i % 3) * (ML_V + 1):(i % 3) * (ML_V + 1) + ML_V]
                    o = o_ml[:, i, hd * ML_V:(hd + 1) * ML_V]
                    if d == 0:
                        ins = nc.vector.tensor_scalar(o, num, den2[:, i:i + 1], None, ALU.mult)
                    else:
                        ins = nc.vector.scalar_tensor_tensor(out=o, in0=num, scalar=den2[:, i:i + 1], in1=o, op0=ALU.mult, op1=ALU.add)
                ins.then_inc(nd_evac.sem, 1)
                dve.wait_ge(nd_evac.sem, nd_evac.at(l, v + 1))

            def out_sums(l, which, groups):
                for i in range(NT):
                    dve.wait_ge(osq.sem, osq.at(l, which * NT + i + 1))
                    nc.vector.reduce_sum(hs[:, i * groups:(i + 1) * groups],
                                         ebuf[:, i % 2, 0:512].rearrange("p (g v) -> p g v", g=groups), axis=AX.X).then_inc(ored.sem, 1)

            def out_scales(l, which, groups, buf):
                dve.wait_ge(orstd.sem, orstd.at(l, which + 1))
                for i in range(NT):
                    o = buf[:, i, :].rearrange("p (g v) -> p g v", g=groups)
                    if groups == 1:
                        nc.vector.tensor_scalar(buf[:, i, :], buf[:, i, :], hs[:, i:i + 1], None, ALU.mult).then_inc(oscaled.sem, 1)
                    else:
                        nc.vector.tensor_tensor(o, o, hs[:, i * groups:(i + 1) * groups].unsqueeze(2).to_broadcast([P, groups, 512 // groups]),
                                                ALU.mult).then_inc(oscaled.sem, 1)

            def row_max(l, n):
                scale = att(n)[4]
                dve.wait_ge(s_ps.sem, s_ps.at(l, n + 1))
                dve.wait_ge(p_ready.sem, p_ready.at(l, max(n - 1, 0)))
                link(nc.vector.tensor_reduce(rowmax[:, n % 2:n % 2 + 1], pair(n % 2), AX.XY, ALU.max))
                nc.vector.tensor_scalar(negmax[:, n % 2:n % 2 + 1], rowmax[:, n % 2:n % 2 + 1], -scale, None,
                                        ALU.mult).then_inc(max_ready.sem, 1)

            def turned_tail(l, n):
                dve.wait_ge(tail_ps.sem, tail_ps.at(l, n + 1))
                dve.wait_ge(o_ps.sem, o_ps.at(l, max(n - 1, 0)))
                w = TILES[-1][1]
                nc.vector.tensor_copy(mbuf[0:w, n % 2, 512:WIDE], pb[0:w, TAIL_O, 0:P]).then_inc(pt_tail.sem, 1)

            def att_out(l, n):
                _, _, _, dv, _, i, hd = att(n)
                r = rsum[:, n % 2:n % 2 + 1]
                dve.wait_ge(p_ready.sem, p_ready.at(l, n + 1))
                link(nc.vector.reciprocal(r, sums[:, n % 4:n % 4 + 1]))
                src = pb[:, TAIL_O, P:P + dv]
                if n < N_ATT_M:
                    dve.wait_ge(o_ps.sem, o_ps.at(l, n + 1))
                    nc.vector.tensor_scalar(o_tok[:, i, hd * dv:(hd + 1) * dv], src, r, None, ALU.mult).then_inc(o_evac.sem, 1)
                else:
                    o = o_dif[:, i, (hd // 2) * dv:(hd // 2 + 1) * dv]
                    if hd % 2 == 0:
                        dve.wait_ge(o_ps.sem, o_ps.at(l, n + 1))
                        nc.vector.tensor_scalar(o, src, r, None, ALU.mult).then_inc(o_evac.sem, 1)
                    else:
                        link(nc.vector.tensor_tensor(r, r, neg_lam[:, :], ALU.mult))
                        dve.wait_ge(o_evac.sem, o_evac.at(l, n - NT + 1))
                        dve.wait_ge(o_ps.sem, o_ps.at(l, n + 1))
                        nc.vector.scalar_tensor_tensor(out=o, in0=src, scalar=r, in1=o, op0=ALU.mult, op1=ALU.add).then_inc(o_evac.sem, 1)

            nc.vector.memset(eps[:, :], EPS).then_inc(eps_ready.sem, 1)
            dve.wait_ge(par_in.sem, 16)
            dve.wait_ge(cleared.sem, 5)
            for l in range(DEPTH):
                if l:
                    dve.wait_ge(w_used.sem, w_used.at(l, 0))
                for k in range(KD):
                    if l == 0:
                        dve.wait_ge(x_in[k].sem, 16)
                    else:
                        dve.wait_ge(evac.sem, evac.at(l - 1, G_FOUT + k + 1))
                    gains(l, k, "attn_g", xg_parts)
                dve.wait_ge(rs_ready.sem, rs_ready.at(l, RS_A + 1))
                d24 = slice(0, NDEC)
                for g in range(G_SSD):
                    scale_out(l, g, tile_of(proj, g))
                    if g < 6:
                        dve.wait_ge(evac.sem, evac.at(l, g + 1))
                        conv(l, g)
                    if g == MISC:
                        dve.wait_ge(table_in.sem, 16)
                        dve.wait_ge(evac.sem, evac.at(l, MISC + 1))
                        nc.vector.tensor_scalar(ebuf[d24, 0, :], tile_of(proj, MISC, rows_=d24), par_at(l, "bias", rows_=d24),
                                                C("sign", d24), ALU.add, ALU.mult).then_inc(dec_u.sem, 1)
                        lam = par_at(l, "lam", 0, 4 * DIFF_QK).rearrange("p (a b) -> p a b", b=DIFF_QK)
                        link(nc.vector.tensor_tensor(lam_p[:, :, :], lam[:, 0:4:2, :], lam[:, 1:4:2, :], ALU.mult))
                        nc.vector.reduce_sum(lam_s[:, :], lam_p[:, :, :], axis=AX.X).then_inc(lam_sum.sem, 1)
                    if g == MISC + 3:
                        dve.wait_ge(conv_act.sem, conv_act.at(l, 6))
                        dve.wait_ge(dec_ln.sem, dec_ln.at(l, 1))
                        u, ln = ebuf[d24, 0, :], ebuf[d24, 1, :]
                        dec, sp, ig = kh[d24, 0, :], mbuf[d24, 1, 0:T], kh[d24, 1, :]
                        link(nc.vector.scalar_tensor_tensor(out=sp, in0=u, scalar=0.0, in1=ln, op0=ALU.max, op1=ALU.add))
                        link(nc.vector.tensor_scalar(dec, sp, ea[d24, :], -1.0, ALU.mult, ALU.mult))
                        link(nc.vector.tensor_copy(ig, tile_of(proj, MISC, rows_=slice(32, 32 + NDEC))))
                        link(nc.vector.tensor_scalar(ig, ig, par_at(l, "i_bias", rows_=d24), None, ALU.add))
                        link(nc.vector.memset(ebuf[d24, 0, :], 0.0))
                        zero = ebuf[d24, 0, :]
                        link(nc.vector.tensor_tensor_scan(rows[0:NDEC, :], dec, zero, 0.0, ALU.add, ALU.add))
                        link(nc.vector.tensor_tensor_scan(rows[32:32 + NDEC, ::-1], dec[:, ::-1], zero, 0.0, ALU.add, ALU.add))
                        link(nc.vector.tensor_tensor_scan(rows[64:64 + NDEC, :], dec, ig, NEG, ALU.add, ALU.max))
                        nc.vector.tensor_tensor_scan(rows[96:96 + NDEC, ::-1], dec[:, ::-1], ig[:, ::-1], NEG, ALU.add,
                                                     ALU.max).then_inc(rows_ready.sem, 1)
                        dve.wait_ge(rows_ready.sem, rows_ready.at(l, 1))
                        dve.wait_ge(lam_exp.sem, lam_exp.at(l, 1))
                        link(nc.vector.scalar_tensor_tensor(out=neg_lam[:, :], in0=lam_e[:, 0:1], scalar=-1.0, in1=lam_e[:, 1:2],
                                                            op0=ALU.mult, op1=ALU.add))
                        link(nc.vector.tensor_tensor(neg_lam[:, :], neg_lam[:, :], par_at(l, "lambda_init", 0), ALU.subtract))
                        link(nc.vector.tensor_tensor(gain_d[:, :], par_at(l, "diff_out_g"), par_at(l, "lambda_init", 1), ALU.mult))

                dve.wait_ge(cols_ps.sem, cols_ps.at(l, 1))
                nc.vector.tensor_copy(cols[:, 0:NT - 1, :], pb[:, 7, 0:(NT - 1) * NCOL].rearrange("p (i c) -> p i c", c=NCOL))
                nc.vector.tensor_copy(cols[0:TILES[-1][1], NT - 1, :], pb[0:TILES[-1][1], 7, (NT - 1) * NCOL:NT * NCOL]).then_inc(cols_ready.sem, 1)
                dve.wait_ge(cols_ready.sem, cols_ready.at(l, 1))
                for i in range(NT):
                    from_transposes(l, TR_X + i, x_tok[0:TILES[i][1], i, :], i, op=copy)
                for g in range(SSD_G):
                    for j, (_, w) in enumerate(TILES):
                        dve.wait_ge(cb_ps.sem, cb_ps.at(l, g * NT + j + 1))
                        nc.vector.tensor_copy(halves(cb(g, j, 0, T, slice(0, w))), pair(2, slice(0, w))).then_inc(cb_ready.sem, 1)
                dve.wait_ge(cb_ready.sem, cb_ready.at(l, 2 * NT))
                exponents(l, 0)
                sines = kh[:, 0, :]
                for n in range(STEPS_SSD):
                    u, j = n // NT, n % NT
                    if n + 1 < STEPS_SSD:
                        exponents(l, n + 1)
                    weights(l, n)
                    if j == 0 and u >= 1:
                        scale_out(l, DQ + u - 1, tile_of(proj, DQ + u - 1))
                    if j == 2 and u % 2 == 0 and u:
                        ssd_head(l, u // 2 - 1)
                    if j == 0 and 0 <= u - 3 < 8:
                        t = u - 3
                        dve.wait_ge(rs_ready.sem, rs_ready.at(l, RS_D + t + 1))
                        normed(l, tile_of(proj, DQ + t), par_at(l, "dq_g" if t < 4 else "dk_g"))
                    if j == 1 and 0 <= u - 4 < 8:
                        t = u - 4
                        dve.wait_ge(rot_ready.sem, rot_ready.at(l, t + 1))
                        link(nc.vector.tensor_tensor(halves(sines), pair(1), halves(C("sin_d")), ALU.mult))
                        dve.wait_ge(qcos.sem, qcos.at(l, t + 1))
                        nc.vector.tensor_tensor(tile_of(proj, DQ + t), tile_of(proj, DQ + t), sines, ALU.add).then_inc(roped.sem, 1)
                scale_out(l, G_ML - 1, tile_of(proj, G_ML - 1))
                ssd_head(l, SSD_H - 1)
                dve.wait_ge(z_act.sem, z_act.at(l, 4))
                dve.wait_ge(m_ready.sem, m_ready.at(l, STEPS_SSD))
                for i in range(NT):
                    def gated(dst, src):
                        return nc.vector.tensor_tensor(dst, src, dst, ALU.mult)
                    from_transposes(l, TR_OS + i, feature_block(proj, ZT, i), i, True, gated)
                nc.vector.memset(v_ml[:, :, :, ML_V], 1.0)
                for i in range(NT):
                    def by_head(dst, src):
                        return nc.vector.tensor_copy(dst, src.rearrange("p (h v) -> p h v", v=ML_V))
                    from_transposes(l, TR_MV + i, v_ml[0:TILES[i][1], i, :, 0:ML_V], i, op=by_head)
                dve.wait_ge(rs_ready.sem, rs_ready.at(l, RS_S + 1))
                for f in range(4):
                    ins = nc.vector.scalar_tensor_tensor(out=tile_of(proj, ZT + f), in0=tile_of(proj, ZT + f), scalar=par_at(l, "ssd_g", f),
                                                         in1=rstd2[:, :], op0=ALU.mult, op1=ALU.mult)
                ins.then_inc(rs_used.sem, 1)

                dve.wait_ge(enm_ready.sem, enm_ready.at(l, 1))
                exponents(l, STEPS_SSD)
                for n in range(STEPS_SSD, STEPS):
                    if n + 1 < STEPS:
                        exponents(l, n + 1)
                    weights(l, n)
                    v, j = (n - STEPS_SSD) // NT, n % NT
                    if j == NT - 1 and v < 2 * ML_H - 1:
                        ml_unit(l, v)
                    if j == 0 and v >= 1:
                        scale_out(l, G_ML + v - 1, tile_of(proj, G_ML + v - 1))
                    if v in JOB_UNITS and j == NT - 1:
                        s0, tiles, norm = JOB_UNITS[v]
                        dve.wait_ge(rs_ready.sem, rs_ready.at(l, norm + 1))
                        t0, gain = (CQ, "q_g") if norm == RS_C else (CKV, "kv_g")
                        for c in range(tiles):
                            normed(l, tile_of(proj, t0 + c), par_at(l, gain, c), count=(c == tiles - 1))
                ml_unit(l, 2 * ML_H - 1)
                scale_out(l, N_IN - 2, tile_of(proj, N_IN - 2))
                out_sums(l, 0, ML_H)
                scale_out(l, N_IN - 1, tile_of(proj, N_IN - 1))
                for i, (_, w) in enumerate(TILES):
                    dve.wait_ge(v_ps.sem, v_ps.at(l, i + 1))
                    nc.vector.tensor_copy(v_mla[0:w, i, :], pb[0:w, 4 + i % 2, :]).then_inc(v_ready.sem, 1)
                out_scales(l, 0, ML_H, o_ml)

                rws, kr = slice(0, MLA_QK), slice(MLA_NOPE, MLA_QK)

                def prep(stage, hd):
                    side, what = stage // 3, stage % 3
                    e = 2 * hd + side
                    buf = (qh, kh)[side]
                    if what == 0:
                        dve.wait_ge(s_ps.sem, s_ps.at(l, max(hd - 1, 0) * NT))
                        dve.wait_ge(p_ps.sem, p_ps.at(l, e + 1))
                        if side == 1:
                            nc.vector.tensor_copy(buf[kr, hd % 2, 0:T], tile_of(proj, MISC, rows_=kr))
                        m = slice(0, MLA_QK if side == 0 else MLA_NOPE)
                        nc.vector.tensor_copy(halves(buf[m, hd % 2, 0:T]), pair(3, m)).then_inc(p_copy.sem, 1)
                        dve.wait_ge(p_copy.sem, p_copy.at(l, e + 1))
                    elif what == 1:
                        dve.wait_ge(rs_ready.sem, rs_ready.at(l, RS_M + e + 1))
                        normed(l, buf[rws, hd % 2, 0:T], par_at(l, ("qh_g", "kh_g")[side], rows_=rws), rws)
                    else:
                        dve.wait_ge(rot_ready.sem, rot_ready.at(l, 8 + e + 1))
                        t0, src = rstd[kr, :], buf[kr, hd % 2, 0:T]
                        nc.vector.tensor_tensor(halves(t0), pair(3, kr), halves(C("sin_m", kr)), ALU.mult).then_inc(rot_used.sem, 1)
                        link(nc.vector.tensor_tensor(src, src, C("cos_m", kr), ALU.mult))
                        nc.vector.tensor_tensor(src, src, t0, ALU.add).then_inc(roped.sem, 1)

                dve.wait_ge(o_sig.sem, o_sig.at(l, 4))
                for i in range(NT):
                    def gate(dst, src):
                        return nc.vector.scalar_tensor_tensor(out=dst, in0=src, scalar=par_at(l, "ml_out_g"), in1=dst,
                                                              op0=ALU.mult, op1=ALU.mult)
                    from_transposes(l, TR_OM + i, feature_block(proj, MO, i), i, True, gate)
                for s in range(8):
                    prep(s % 6, s // 6)
                row_max(l, 0)
                for n in range(N_ATT_M):
                    hd, i = n // NT, n % NT
                    if n + 1 < N_ATT_M:
                        row_max(l, n + 1)
                    turned_tail(l, n)
                    prepare(prep, n, (0, 2, 5))
                    if n >= 1:
                        att_out(l, n - 1)
                    prepare(prep, n, (1, 4))
                    if i == 0 and hd + 1 < MLA_H:
                        prep(3, hd + 1)
                att_out(l, N_ATT_M - 1)
                for i in range(NT):
                    from_transposes(l, TR_DV + i, v_dif[0:TILES[i][1], i, :], i, op=copy)
                out_sums(l, 1, 1)
                out_scales(l, 1, 1, o_tok)
                for i in range(NT):
                    def by_gain(dst, src, i=i):
                        return nc.vector.tensor_tensor(dst, src, par_at(l, "mla_out_g", 0, 4).unsqueeze(2).to_broadcast([P, 4, TILES[i][1]]), ALU.mult)
                    from_transposes(l, TR_OA + i, feature_block(proj, CQ, i), i, True, by_gain)
                dve.wait_ge(tr_evac.sem, tr_evac.at(l, TR_OA + NT))
                for k in range(KD, KD + 4):
                    mixed_split(l, k)

                row_max(l, N_ATT_M)
                for n in range(N_ATT_M, N_ATT):
                    if n + 1 < N_ATT:
                        row_max(l, n + 1)
                    turned_tail(l, n)
                    if n > N_ATT_M:
                        att_out(l, n - 1)
                    if n % NT == NT - 1:
                        g = (n - N_ATT_M) // NT
                        residual(l, G_OUT1 + g, g)
                att_out(l, N_ATT - 1)
                out_sums(l, 2, DIFF_H)
                out_scales(l, 2, DIFF_H, o_dif)
                for i in range(NT):
                    def scaled(dst, src):
                        return nc.vector.tensor_scalar(dst, src, gain_d[:, :], None, ALU.mult)
                    from_transposes(l, TR_OD + i, feature_block(proj, DV, i), i, True, scaled)
                dve.wait_ge(tr_evac.sem, tr_evac.at(l, TR_OD + NT))
                for k in range(KD + 4, KM):
                    mixed_split(l, k)

                for k in range(KD):
                    residual(l, G_OUT2 + k, k)
                    dve.wait_ge(evac.sem, evac.at(l, G_OUT2 + k + 1))
                    gains(l, k, "ffn_g", ffn_parts)

                dve.wait_ge(rs_ready.sem, rs_ready.at(l, RS_F + 1))
                for j in range(KF):
                    if j >= 2:
                        dve.wait_ge(act_ready.sem, act_ready.at(l, j - 1))
                    scale_out(l, G_FIN + 2 * j, ebuf[:, j % 2, :])
                    scale_out(l, G_FIN + 2 * j + 1, mbuf[:, j % 2, 0:T])
                    dve.wait_ge(gsilu.sem, gsilu.at(l, j + 1))
                    dve.wait_ge(evac.sem, evac.at(l, G_FIN + 2 * j + 2))
                    prod = ebuf[:, j % 2, :]
                    link(nc.vector.tensor_tensor(prod, prod, mbuf[:, j % 2, 0:T], ALU.mult))
                    lead, rest = act_parts(j)
                    link(nc.vector.tensor_copy(lead, prod))
                    nc.vector.tensor_tensor(rest, prod, lead.bitcast(FP32), ALU.subtract).then_inc(act_ready.sem, 1)
                for k in range(KD):
                    residual(l, G_FOUT + k, k)


def _columns():
    cq, ckv, kr, z = 0, 384, 640, 672
    xbc, dt, dq = 1184, 1952, 1968
    dk, dv, mq, mk, mv, mo, mi, mf = 2480, 2992, 3504, 3760, 4016, 4528, 5040, 5048
    run = lambda a, n: list(range(a, a + n))
    misc = run(dt, 16) + run(mf, 8) + [-1] * 8 + [-1] * 16 + run(mi, 8) + [-1] * 8 + run(kr, 32) + [-1] * 32
    return np.array(run(xbc, 768) + misc + run(z, 512) + run(mo, 512) + run(dq, 512) + run(dk, 512) + run(mq, 256)
                    + run(mk, 256) + run(mv, 512) + run(cq, 384) + run(ckv, 256) + run(dv, 512))


_HEAD = np.array(list(range(MLA_ROPE, MLA_QK)) + list(range(MLA_ROPE)))


def _weights(w_in, w_uq, w_ukv, w_out, w_fi, w_fo):
    f = np.float32
    ws = np.zeros((DEPTH, N_RAW, P, SLOT), f)
    heads = np.zeros((DEPTH, 4, P, SLOT), f)
    cols = _columns()
    v_at = N_IN
    order = np.r_[4:8, 12:16, 0:4, 8:12]
    for l in range(DEPTH):
        wi = np.concatenate([w_in[l], np.zeros((D_MODEL, 1), f)], 1)[:, cols]
        tiles = lambda w, kt: w.reshape(kt, P, -1, P).transpose(2, 1, 0, 3)
        ws[l, 0:N_IN] = tiles(wi, KD).reshape(N_IN, P, SLOT)
        kv = w_ukv[l].reshape(2, P, MLA_H, MLA_NOPE + MLA_V)
        ws[l, v_at] = kv[..., MLA_NOPE:].transpose(1, 0, 2, 3).reshape(P, SLOT)
        heads[l, 0] = kv[..., :MLA_NOPE].transpose(1, 2, 0, 3).reshape(P, SLOT)
        uq = w_uq[l].reshape(3, P, MLA_H, MLA_QK)[..., _HEAD].transpose(2, 1, 0, 3).reshape(MLA_H, P, 3 * MLA_QK)
        for hd in range(MLA_H):
            o = (hd % UQ_HEADS) * 3 * MLA_QK
            heads[l, 1 + hd // UQ_HEADS, :, o:o + 3 * MLA_QK] = uq[hd]
        dense = ws[l, v_at + 1 - N_IN:]
        wo = tiles(w_out[l], KM)[:, :, order].reshape(KD, P, 2, SLOT)
        dense[S_OUT1:S_OUT2], dense[S_OUT2:S_FIN] = wo[:, :, 0], wo[:, :, 1]
        fi = tiles(w_fi[l], KD).reshape(2, KF, P, SLOT)
        dense[S_FIN:S_FOUT] = fi.transpose(1, 0, 2, 3).reshape(2 * KF, P, SLOT)
        fo = tiles(w_fo[l], KF).reshape(KD, P, KF * P)
        pad = np.zeros((KD, P, 3 * SLOT), f)
        pad[:, :, :KF * P] = fo
        dense[S_FOUT:] = pad.reshape(KD, P, 3, SLOT).transpose(0, 2, 1, 3).reshape(3 * KD, P, SLOT)
    return ws.reshape(DEPTH * N_RAW, P, SLOT), heads.reshape(DEPTH * 4, P, SLOT)


def _params(a):
    f = np.float32
    out = np.zeros((P, DEPTH, N_PARAM), f)

    def put(name, v, rows_=P):
        s, e = PARAM[name]
        for l in range(DEPTH):
            out[0:rows_, l, s:e] = v(l)

    tiled = lambda x, n: x.reshape(n, P).T
    put("attn_g", lambda l: tiled(a["attn_norm_g"][l], KD))
    put("ffn_g", lambda l: tiled(a["ffn_norm_g"][l], KD))
    put("q_g", lambda l: tiled(a["mla_q_norm_g"][l], 3))
    put("kv_g", lambda l: tiled(a["mla_kv_norm_g"][l], 2))
    put("qh_g", lambda l: a["mla_q_head_g"][l][_HEAD][:, None], MLA_QK)
    put("kh_g", lambda l: a["mla_k_head_g"][l][_HEAD][:, None], MLA_QK)
    put("mla_out_g", lambda l: tiled(a["mla_out_g"][l], 4))
    put("conv_w", lambda l: a["ssd_conv_w"][l].reshape(TAPS, 6, P).transpose(2, 1, 0).reshape(P, 6 * TAPS))
    put("conv_b", lambda l: tiled(a["ssd_conv_b"][l], 6))
    put("ssd_g", lambda l: tiled(a["ssd_norm_g"][l], 4))
    put("ssd_d", lambda l: np.broadcast_to(a["ssd_d"][l][None], (P, SSD_H)))
    put("dq_g", lambda l: np.concatenate([a["diff_q_head_g"][l]] * 2)[:, None])
    put("dk_g", lambda l: np.concatenate([a["diff_k_head_g"][l]] * 2)[:, None])
    put("diff_out_g", lambda l: a["diff_out_g"][l][:, None])
    put("ml_out_g", lambda l: a["mlstm_out_g"][l][:, None])
    z8, z16 = np.zeros(8, f), np.zeros(16, f)
    put("bias", lambda l: np.concatenate([a["ssd_dt_bias"][l].ravel(), a["mlstm_f_bias"][l].ravel()])[:, None], NDEC)
    put("a_log", lambda l: np.concatenate([a["ssd_a_log"][l].ravel(), z8])[:, None], NDEC)
    put("i_bias", lambda l: np.concatenate([z16, a["mlstm_i_bias"][l].ravel()])[:, None], NDEC)
    put("lam", lambda l: np.broadcast_to(a["diff_lambda"][l].reshape(1, -1), (P, 4 * DIFF_QK)))
    init = [0.8 - 0.6 * float(np.exp(-0.3 * l)) for l in range(DEPTH)]
    put("lambda_init", lambda l: np.array([[init[l], 1.0 - init[l]]], f))
    return out


def _rope(rot, starts):
    f = np.float32
    r = rot // 2
    inv = (1.0 / (f(500000.0) ** (np.arange(0, rot, 2, dtype=f) / f(rot)))).astype(f)
    ang = (np.arange(T, dtype=f)[:, None] * inv[None, :]).astype(f)
    c, s = np.cos(ang).astype(f).T, np.sin(ang).astype(f).T
    cos, sin, perm = np.ones((P, T), f), np.zeros((P, T), f), np.zeros((P, P), f)
    for a in starts:
        cos[a:a + r], cos[a + r:a + rot] = c, c
        sin[a:a + r], sin[a + r:a + rot] = s, s
        for k in range(r):
            perm[a + r + k, a + k] = -1.0
            perm[a + k, a + r + k] = 1.0
    return cos, sin, perm


def _constants():
    f = np.float32
    out = np.zeros((P, N_CONST), f)

    def put(name, v):
        s, e = CONST[name]
        out[0:v.shape[0], s:e] = v

    put("ones", np.ones((P, P), f))
    put("ident", np.eye(P, dtype=f))
    put("ones_h", np.kron(np.eye(2, dtype=f), np.ones((64, 64), f)))
    key, query = np.arange(P)[:, None], np.arange(P)[None, :]
    put("mask", np.concatenate([np.where(query >= key, 0, NEG), np.zeros((P, 4 * P)), np.where(query <= key, 0, NEG)], 1).astype(f))
    cos, sin, perm = _rope(DIFF_ROPE, (0, 64))
    put("cos_d", cos), put("sin_d", sin), put("perm_d", perm)
    cos, sin, perm = _rope(MLA_ROPE, (MLA_NOPE,))
    put("cos_m", cos), put("sin_m", sin), put("perm_m", perm)
    FW, BW, MF, MB = 0, 32, 64, 96
    sel, rs, ig, sp = (np.zeros((P, n), f) for n in (NDEC, NCOL, NCOL, NCOL))
    for r in range(NDEC):
        back = r // SSD_H if r < C_ML else (r - C_ML) // ML_H
        sel[(BW if back else FW) + r, r] = 1.0
        rs[(BW if back else FW) + r, r] = -1.0
        if r >= C_ML:
            sel[(MB if back else MF) + r, r] = -1.0
            ig[r, r] = 1.0
            rs[(MB if back else MF) + r, C_NM + r - C_ML] = -1.0
        else:
            sp[r, C_DT + r] = 1.0
    put("rowsel", sel), put("lin_rs", rs), put("lin_i", ig), put("lin_sp", sp)
    put("sign", np.array([[1.0]] * C_ML + [[-1.0]] * (NDEC - C_ML), f))
    return out


def kernel(**inputs):
    import concourse.bacc as _bacc
    from concourse.bass_utils import run_bass_kernel_spmd as _run

    a = {k: np.asarray(v) for k, v in inputs.items()}
    tokens = np.concatenate([a["meta_tokens"], a["x"][0]], 0)
    stream, heads = _weights(a["w_in"], a["mla_w_uq"], a["mla_w_ukv"], a["w_out"], a["w_ffn_in"], a["w_ffn_out"])
    arrays = {
        "x_t": np.ascontiguousarray(tokens.T.reshape(KD, P, T).transpose(1, 0, 2)),
        "w_stream": stream,
        "w_heads": heads,
        "params": _params(a),
        "consts": _constants(),
    }
    nc = _bacc.Bacc("TRN2", target_bir_lowering=False, num_devices=1, dynamic_dma_scratch_size=1024)
    args = [nc.dram_tensor(n, v.shape, FP32, kind="ExternalInput").ap() for n, v in arrays.items()]
    out = nc.dram_tensor("out_t", (P, KD, SEQ), FP32, kind="ExternalOutput").ap()
    trunk(nc, *args, out)
    r = _run(nc, [arrays], core_ids=[0])
    got = np.asarray(r.results[0]["out_t"])
    return np.ascontiguousarray(got.transpose(2, 1, 0).reshape(1, SEQ, D_MODEL))
```

```python
from contextlib import ExitStack

import numpy as np
import concourse.bass as bass
from concourse import mybir

FP32 = mybir.dt.float32
FP32R = mybir.dt.float32r
ALU = mybir.AluOpType
ACT = mybir.ActivationFunctionType
AX = mybir.AxisListType

DEPTH, D_MODEL, N_META, SEQ = 2, 1024, 16, 512
EPS, NEG = 1e-6, -1e30
P = 128
T = N_META + SEQ
HALF = T // 2
KD = D_MODEL // P
TILES = [(i * P, min(P, T - i * P)) for i in range(-(-T // P))]
NT = len(TILES)
WIDE = NT * P

MLA_H, MLA_NOPE, MLA_ROPE, MLA_V = 8, 64, 32, 64
MLA_QK = MLA_NOPE + MLA_ROPE
MLA_ROWS = MLA_NOPE + 48
Q_RANK, KV_RANK = 384, 256
SSD_H, SSD_P, SSD_G, SSD_N, TAPS = 8, 64, 2, 64, 5
DIFF_H, DIFF_QK, DIFF_V, DIFF_ROPE = 4, 64, 128, 16
ML_H, ML_QK, ML_V = 4, 64, 128
D_FF = 2816
KF = D_FF // P
KM = 16

XS, BM, CM, MISC, ZT, MO, DQ, DK, MQ, MK, MV, CQ, CKV, DV = 0, 4, 5, 6, 7, 11, 15, 19, 23, 25, 27, 31, 34, 36
N_IN = 40
G_SSD, G_ML = 15, 31
SLOT = KD * P
S_OUT1, S_OUT2 = N_IN, N_IN + KD
S_FIN = N_IN + 2 * KD
S_FOUT = S_FIN + 2 * KF
N_SLOT = S_FOUT + 3 * KD
RAW = 2
PARTS = 2
N_RAW = N_SLOT + 1
UQ_HEADS = 3
G_OUT1, G_OUT2, G_FIN, G_FOUT = N_IN, N_IN + KD, N_IN + 2 * KD, N_IN + 2 * KD + 2 * KF
N_GROUP = G_FOUT + KD
CHUNKS_SSD = ((0, 0), (0, 2), (2, 4), (4, 6), (6, 8))
CHUNKS_ML = ((0, 0), (0, 1), (1, 3), (3, 4), (4, 8))
CHUNKS_DIFF = ((0, 2), (2, 4), (4, 6), (6, 7), (7, 8))
LATE_CHUNKS = ((0, 0), (0, 0), (0, 0), (0, 3), (3, 8))

NDEC = 2 * SSD_H + 2 * ML_H
C_ML, C_DT, C_NM = 2 * SSD_H, NDEC, NDEC + 2 * SSD_H
NCOL = C_NM + 2 * ML_H


def layout(fields):
    at, out = 0, {}
    for name, n in fields:
        out[name] = (at, at + n)
        at += n
    return out, at


CONST, N_CONST = layout([("ones", P), ("ident", P), ("mask", 6 * P), ("ones_h", P), ("perm_d", P), ("cos_d", T), ("sin_d", T),
                         ("cos_m", T), ("sin_m", T), ("rowsel", NDEC), ("lin_rs", NCOL), ("lin_i", NCOL), ("lin_sp", NCOL),
                         ("sign", 1)])
PARAM, N_PARAM = layout([("attn_g", KD), ("ffn_g", KD), ("q_g", 3), ("kv_g", 2), ("qh_g", 1), ("kh_g", 1), ("mla_out_g", 4),
                         ("conv_w", 6 * TAPS), ("conv_b", 6), ("ssd_g", 4), ("ssd_d", SSD_H), ("dq_g", 1), ("dk_g", 1),
                         ("diff_out_g", 1), ("ml_out_g", 1), ("bias", 1), ("a_log", 1), ("i_bias", 1), ("lam", 4 * DIFF_QK),
                         ("lambda_init", 2)])

STEPS_SSD, STEPS_ML, STEPS = 2 * SSD_H * NT, 2 * ML_H * NT, 2 * (SSD_H + ML_H) * NT
N_ATT_M = MLA_H * NT
N_ATT = N_ATT_M + 2 * DIFF_H * NT
SQ_D, SQ_S, SQ_C, SQ_M = 0, 8, 12, 17
N_SQ = SQ_M + 2 * MLA_H
RS_A, RS_D, RS_S, RS_C, RS_M, RS_F = 0, 1, 9, 10, 12, 12 + 2 * MLA_H
N_RS = RS_F + 1
JOB_UNITS = {4: (SQ_C, 3, RS_C), 6: (SQ_C + 3, 2, RS_C + 1)}
TR_X, TR_OS, TR_MV, TR_OM, TR_DV, TR_OA, TR_OD = range(0, 7 * NT, NT)


class Signal:

    def __init__(self, sem, per):
        self.sem, self.per = sem, per

    def at(self, layer, k):
        return layer * self.per + k


def trunk(nc, x_t, w_stream, w_heads, params, consts, out):
    ctx = ExitStack()
    with ctx:
        def sb(name, shape, dtype=FP32):
            return ctx.enter_context(nc.sbuf_tensor(name, shape, dtype))

        def overlaid(name, shape, dtype, at):
            return nc.alloc_sbuf_tensor_at(name, shape, dtype, offset=at)

        def signal(name, per):
            return Signal(ctx.enter_context(nc.semaphore(name)), per)

        h = sb("h", [P, KD, T])
        proj_at = nc.sbuf_base
        proj = sb("proj", [P, N_IN * T])
        proj_r = overlaid("proj_r", [P, N_IN * T], FP32R, proj_at)
        mix = sb("mix", [P, KM * T], FP32R)
        raw = sb("raw", [P, RAW, SLOT])
        parts_at = nc.sbuf_base
        parts = sb("parts", [P, PARTS, 2, SLOT], FP32R)
        w_head = overlaid("w_head", [P, 4, SLOT], FP32, parts_at)
        o_at = nc.sbuf_base
        o_tok = sb("o_tok", [P, NT, 512])
        o_tok_r = overlaid("o_tok_r", [P, 4 * T], FP32R, o_at)
        v_tok = sb("v_tok", [P, NT * ML_H * (ML_V + 1)])
        sq = sb("sq", [P, 2, T])
        rstd = sb("rstd", [P, T])
        rstd2 = sb("rstd2", [P, T])
        ebuf = sb("ebuf", [P, 2, T])
        mbuf = sb("mbuf", [P, 2, WIDE])
        qh = sb("qh", [P, 2, WIDE])
        kh = sb("kh", [P, 2, T])
        rows = qh[:, 0, 0:T]
        sel_r = sb("sel_r", [P, NDEC], FP32R)
        cols = sb("cols", [P, NT, NCOL])
        enm = sb("enm", [P, NT, 2 * ML_H])
        con = sb("con", [P, N_CONST])
        par = sb("par", [P, DEPTH, N_PARAM])
        sums = sb("sums", [P, 4])
        negmax = sb("negmax", [P, 2])
        rowmax = sb("rowmax", [P, 2])
        rsum = sb("rsum", [P, 2])
        ea = sb("ea", [P, 1])
        lam_p = sb("lam_p", [P, 2, DIFF_QK])
        lam_s = sb("lam_s", [P, 2])
        lam_e = sb("lam_e", [P, 2])
        neg_lam = sb("neg_lam", [P, 1])
        gain_d = sb("gain_d", [P, 1])
        eps = sb("eps", [P, 1])
        den = sb("den", [P, NT])
        den2 = sb("den2", [P, NT])
        hs = sb("hs", [P, 4 * NT])
        pb = ctx.enter_context(nc.psum_tensor("pb", [P, 8, 512], FP32))

        def C(name, rows_=slice(0, P)):
            return con[rows_, CONST[name][0]:CONST[name][1]]

        def par_at(layer, name, i=0, n=1, rows_=slice(0, P)):
            a = PARAM[name][0] + i
            return par[rows_, layer, a:a + n]

        def tile_of(buf, k, a=0, b=T, rows_=slice(0, P)):
            return buf[rows_, k * T + a:k * T + b]

        def halves(ap):
            return ap.rearrange("p (a b) -> p a b", b=HALF)

        def pair(p, rows_=slice(0, P)):
            return pb[rows_, 2 * p:2 * p + 2, 0:HALF]

        def span(p, width, rows_):
            return pair(p, rows_) if width == T else pb[rows_, 2 * p, 0:width]

        def like(ap, width):
            return halves(ap) if width == T else ap

        def token_major(buf, tile0):
            return buf[:, tile0 * T:tile0 * T + NT * 512].rearrange("p (i f) -> p i f", f=512)

        x_tok = v_tok[:, 0:NT * 512].rearrange("p (i f) -> p i f", f=512)
        v_ml = v_tok[:, :].rearrange("p (i h v) -> p i h v", h=ML_H, v=ML_V + 1)
        o_ml = o_dif = o_tok
        v_mla = v_dif = x_tok

        def cb(g, j, a, b, rows_):
            if j == NT - 1:
                return (qh[rows_, 1, a:b], kh[rows_, 1, a:b])[g]
            return tile_of(proj, (XS, DV)[g] + j, a, b, rows_)

        def xg_parts(k):
            return tile_of(mix, k), tile_of(mix, KD + k)

        def ffn_parts(k):
            return tile_of(proj_r, DQ + k), tile_of(proj_r, DQ + KD + k)

        MIXED = [ZT + f for f in range(4)] + [MO + f for f in range(4)] + [CQ + f for f in range(4)] + [DV + f for f in range(4)]

        def mixed_parts(k):
            return tile_of(mix, k), tile_of(proj_r, MIXED[k])

        def stacked(hd):
            t0 = MQ + 3 * (hd % 2)
            return tile_of(proj_r, t0), tile_of(proj_r, t0 + 1), tile_of(proj_r, t0 + 2)

        def act_parts(k):
            lead = tile_of(proj_r, k if k < DQ else k + KM)
            rest = tile_of(mix, k) if k < KM else tile_of(proj_r, N_IN - 2 + k - KM) if k < KM + 2 else tile_of(o_tok_r, k - KM - 2)
            return lead, rest

        def rng(d, j):
            return (TILES[j][0], T) if d == 0 else (0, TILES[j][0] + TILES[j][1])

        def mask(d, j):
            a = 0 if d == 0 else P + (NT - 1) * P - TILES[j][0]
            lo, hi = rng(d, j)
            c = CONST["mask"][0] + a
            return con[0:TILES[j][1], c:c + hi - lo]

        def unit(u):
            if u < 2 * SSD_H:
                return u // 2, u % 2, (u % 2) * SSD_H + u // 2
            v = u - 2 * SSD_H
            return v // 2, v % 2, 2 * SSD_H + (v % 2) * ML_H + v // 2

        def att(n):
            if n < N_ATT_M:
                hd, i = n // NT, n % NT
                return (qh[0:MLA_ROWS, hd % 2, i * P:(i + 1) * P], kh[0:MLA_ROWS, hd % 2, :],
                        lambda j: v_mla[0:TILES[j][1], j, hd * MLA_V:(hd + 1) * MLA_V], MLA_V, MLA_QK ** -0.5, i, hd)
            hd, i = (n - N_ATT_M) // NT, (n - N_ATT_M) % NT
            r = slice(64 * (hd % 2), 64 * (hd % 2) + 64)
            return (tile_of(proj, DQ + hd // 2, i * P, (i + 1) * P, r), tile_of(proj, DK + hd // 2, rows_=r),
                    lambda j: v_dif[0:TILES[j][1], j, (hd // 2) * DIFF_V:(hd // 2 + 1) * DIFF_V], DIFF_V, DIFF_QK ** -0.5, i, hd)

        def out1_part(n):
            if n < N_ATT_M:
                return (0, n - (N_ATT_M - KD)) if n >= N_ATT_M - KD else None
            return 2 + (n - N_ATT_M) // KD, (n - N_ATT_M) % KD

        def prepare(prep, n, stages=range(5)):
            hd, i = n // NT, n % NT
            stage, ahead = ((3, 1), (4, 1), (0, 2), (1, 2), (2, 2))[i]
            if hd + ahead < MLA_H and stage in stages:
                prep(stage, hd + ahead)

        def opening(value, turned_out, prep):
            order = [value, value, prep, prep, value, value, prep, value, prep, turned_out, turned_out, prep,
                     turned_out, turned_out, prep, prep, turned_out, prep]
            for k, step in enumerate(order):
                c = order[:k].count(step)
                if step == prep:
                    step(c % NT, c // NT)
                else:
                    step(c)

        TURN, TAIL_O = 4, 5
        def bank_pair(g):
            if G_SSD <= g < G_ML:
                return 2
            if G_ML <= g < G_OUT2:
                return 3
            return 1 + g % 3

        def raw_slot(layer, s):
            return (layer * N_RAW + s + (s >= N_IN)) % RAW

        def slot_end(g):
            return g + 1 if g < G_FOUT else S_FOUT + 3 * (g - G_FOUT + 1)

        const_in = signal("const_in", 0)
        table_in = signal("table_in", 0)
        eps_ready = signal("eps_ready", 0)
        par_in = signal("par_in", 0)
        x_in = [signal(f"x_in{k}", 0) for k in range(KD)]
        cleared = signal("cleared", 0)
        loaded = [signal(f"loaded{s}", 0) for s in range(RAW)]
        head_in = [signal(f"head_in{s}", 1) for s in range(4)]
        lead_ready = signal("lead_ready", N_SLOT)
        split = signal("split", N_SLOT)
        mixed_lead = signal("mixed_lead", KD + 4)
        mixed = signal("mixed", KM)
        w_used = signal("w_used", N_SLOT)
        evac = signal("evac", N_GROUP)
        xg_ready = signal("xg_ready", 2 * KD)
        res_sq = signal("res_sq", 2 * KD)
        added = signal("added", 2 * KD)
        res_sum = signal("res_sum", 2)
        sq_ready = signal("sq_ready", N_SQ)
        sq_used = signal("sq_used", N_SQ)
        rs_ready = signal("rs_ready", N_RS)
        rs_used = signal("rs_used", 8 + 1 + 2 + 2 * MLA_H)
        conv_ready = signal("conv_ready", 6)
        conv_act = signal("conv_act", 6)
        z_act = signal("z_act", 4)
        o_tanh = signal("o_tanh", 4)
        o_sig = signal("o_sig", 4)
        dec_u = signal("dec_u", 1)
        dec_ln = signal("dec_ln", 1)
        rows_ready = signal("rows_ready", 1)
        rows_split = signal("rows_split", 2)
        cols_ps = signal("cols_ps", 1)
        cols_ready = signal("cols_ready", 1)
        enm_ready = signal("enm_ready", 1)
        rot_ready = signal("rot_ready", 8)
        rot_used = signal("rot_used", 8)
        roped = signal("roped", 8 + 2 * MLA_H)
        qcos = signal("qcos", 8)
        tr_ready = signal("tr_ready", 7 * NT)
        tr_evac = signal("tr_evac", 7 * NT)
        cb_ps = signal("cb_ps", 2 * NT)
        cb_ready = signal("cb_ready", 2 * NT)
        rowb = signal("rowb", 2 * (SSD_H + ML_H))
        e_raw = signal("e_raw", STEPS)
        e_exp = signal("e_exp", STEPS)
        m_ready = signal("m_ready", STEPS)
        m_used = signal("m_used", STEPS)
        qk_ps = signal("qk_ps", STEPS_ML)
        y_evac = signal("y_evac", SSD_H)
        nd_evac = signal("nd_evac", 2 * ML_H)
        osq = signal("osq", 3 * NT)
        ored = signal("ored", 3 * NT)
        orstd = signal("orstd", 3)
        oscaled = signal("oscaled", 3 * NT)
        v_ps = signal("v_ps", NT)
        v_ready = signal("v_ready", NT)
        p_ps = signal("p_ps", 2 * MLA_H)
        p_copy = signal("p_copy", 2 * MLA_H)
        s_ps = signal("s_ps", N_ATT)
        stacks = signal("stacks", 2 * DIFF_H)
        max_ready = signal("max_ready", N_ATT)
        p_ready = signal("p_ready", N_ATT)
        t_ps = signal("t_ps", N_ATT)
        tail_ps = signal("tail_ps", N_ATT)
        pt_main = signal("pt_main", N_ATT)
        pt_tail = signal("pt_tail", N_ATT)
        o_ps = signal("o_ps", N_ATT)
        o_evac = signal("o_evac", N_ATT)
        lam_sum = signal("lam_sum", 1)
        lam_exp = signal("lam_exp", 1)
        gsilu = signal("gsilu", KF)
        act_ready = signal("act_ready", KF)
        stored = signal("stored", 0)
        dve_chain = signal("dve_chain", 0)
        pool_chain = signal("pool_chain", 0)
        act_chain = signal("act_chain", 0)

        block = ctx.enter_context(nc.Block())

        @block.sync
        def _(sp):
            for k in range(KD):
                if k < RAW:
                    sp.dma_start(raw[:, k, :], w_stream[k, :, :]).then_inc(loaded[k].sem, 16)
                sp.dma_start(h[:, k, :], x_t[:, k, :]).then_inc(x_in[k].sem, 16)
                if k == 0:
                    sp.dma_start(par[:, :, :], params).then_inc(par_in.sem, 16)
            sp.dma_start(con[:, 0:2 * P], consts[:, 0:2 * P]).then_inc(const_in.sem, 16)
            sp.dma_start(con[:, 2 * P:N_CONST], consts[:, 2 * P:N_CONST]).then_inc(table_in.sem, 16)

            def released(r):
                l, s = r // N_RAW, r % N_RAW
                return (v_ps.sem, v_ps.at(l, NT)) if s == N_IN else (split.sem, split.at(l, s + 1 if s < N_IN else s))

            for n in range(DEPTH * N_RAW):
                l, s = n // N_RAW, n % N_RAW
                if n < RAW:
                    continue
                sp.wait_ge(*released(n - RAW))
                sp.dma_start(raw[:, n % RAW, :], w_stream[n, :, :]).then_inc(loaded[n % RAW].sem, 16)
                if s == N_IN:
                    sp.wait_ge(w_used.sem, w_used.at(l, N_IN))
                    for c in range(4):
                        sp.dma_start(w_head[:, c, :], w_heads[4 * l + c, :, :]).then_inc(head_in[c].sem, 16)
            for k in range(KD):
                sp.wait_ge(evac.sem, evac.at(DEPTH - 1, G_FOUT + k + 1))
                sp.dma_start(out[:, k, :], h[:, k, N_META:T]).then_inc(stored.sem, 16)
            sp.wait_ge(stored.sem, 16 * KD)

        @block.gpsimd
        def _(pool):
            nc.gpsimd.memset(v_tok[:, :], 0.0).then_inc(cleared.sem, 1)
            nc.gpsimd.memset(mbuf[:, :, :], 0.0).then_inc(cleared.sem, 1)
            nc.gpsimd.memset(qh[:, :, :], 0.0).then_inc(cleared.sem, 1)
            nc.gpsimd.memset(cols[:, :, :], 0.0).then_inc(cleared.sem, 1)
            nc.gpsimd.memset(o_tok[:, :, :], 0.0).then_inc(cleared.sem, 1)

            def rest(l, s):
                n = l * N_SLOT + s
                w = raw[:, raw_slot(l, s), :]
                pool.wait_ge(lead_ready.sem, n + 1)
                nc.gpsimd.tensor_tensor(parts[:, n % PARTS, 1, :], w, parts[:, n % PARTS, 0, :].bitcast(FP32),
                                        ALU.subtract).then_inc(split.sem, 1)

            chained = [0]

            def link(ins):
                chained[0] += 1
                ins.then_inc(pool_chain.sem, 1)
                pool.wait_ge(pool_chain.sem, chained[0])

            def rotate(l, e):
                buf, half = (qh, kh)[e % 2][:, e // 2 % 2, 0:T], MLA_ROPE // 2
                first, second, both = slice(64, 64 + half), slice(96, 96 + half), slice(MLA_NOPE, MLA_ROWS)
                pool.wait_ge(rs_used.sem, rs_used.at(l, 11 + e + 1))
                link(nc.gpsimd.tensor_tensor(rstd[second, :], buf[first, :], C("sin_m", first), ALU.mult))
                link(nc.gpsimd.tensor_tensor(rstd[first, :], buf[second, :], C("sin_m", second), ALU.mult))
                link(nc.gpsimd.tensor_tensor(buf[both, :], buf[both, :], C("cos_m", both), ALU.mult))
                nc.gpsimd.tensor_tensor(buf[both, :], buf[both, :], rstd[both, :], ALU.add).then_inc(roped.sem, 1)
                pool.wait_ge(roped.sem, roped.at(l, 8 + e + 1))

            def stack(l, hd):
                own = slice(64 * (hd % 2), 64 * (hd % 2) + 64)
                across = slice(64 - 64 * (hd % 2), 128 - 64 * (hd % 2))
                q_parts, k_lead, k_rest = stacked(hd)
                q, k = tile_of(proj, DQ + hd // 2, rows_=own), tile_of(proj, DK + hd // 2, rows_=own)
                pool.wait_ge(s_ps.sem, s_ps.at(l, N_ATT_M + max(hd - 1, 0) * NT))
                link(nc.gpsimd.tensor_scalar(q_parts[own, :], q, 1.0, None, ALU.mult))
                link(nc.gpsimd.tensor_tensor(q_parts[across, :], q, q_parts[own, :].bitcast(FP32), ALU.subtract))
                link(nc.gpsimd.tensor_scalar(k_lead[own, :], k, 1.0, None, ALU.mult))
                link(nc.gpsimd.tensor_scalar(k_lead[across, :], k, 1.0, None, ALU.mult))
                nc.gpsimd.tensor_tensor(k_rest[own, :], k, k_lead[own, :].bitcast(FP32), ALU.subtract).then_inc(stacks.sem, 1)
                pool.wait_ge(stacks.sem, stacks.at(l, hd + 1))

            def mixed_split(l, k):
                lead, other = mixed_parts(k)
                nc.gpsimd.tensor_scalar(lead, tile_of(proj, MIXED[k]), 1.0, None, ALU.mult).then_inc(mixed_lead.sem, 1)
                pool.wait_ge(mixed_lead.sem, mixed_lead.at(l, k + 1))
                nc.gpsimd.tensor_tensor(other, tile_of(proj, MIXED[k]), lead.bitcast(FP32), ALU.subtract).then_inc(mixed.sem, 1)

            for l in range(DEPTH):
                for s in range(N_SLOT):
                    if s != S_OUT1:
                        rest(l, s)
                    for hd in {S_OUT1 + 1: (0, 1), S_OUT1 + 3: (2,), S_OUT1 + 4: (3, 4), S_OUT1 + 5: (5,), S_OUT1 + 6: (6, 7)}.get(s, ()):
                        pool.wait_ge(split.sem, split.at(l, s + 1))
                        stack(l, hd)
                    if s == G_SSD:
                        lead, other = tile_of(proj_r, BM), tile_of(proj_r, CM)
                        if l == 0:
                            pool.wait_ge(table_in.sem, 16)
                            nc.gpsimd.tensor_copy(sel_r[:, :], C("rowsel"))
                        pool.wait_ge(cb_ps.sem, cb_ps.at(l, 2 * NT))
                        nc.gpsimd.tensor_scalar(lead, rows, 1.0, None, ALU.mult).then_inc(rows_split.sem, 1)
                        pool.wait_ge(rows_split.sem, rows_split.at(l, 1))
                        nc.gpsimd.tensor_tensor(other, rows, lead.bitcast(FP32), ALU.subtract).then_inc(rows_split.sem, 1)
                    if s == S_OUT1 + 2:
                        pool.wait_ge(tr_evac.sem, tr_evac.at(l, TR_OA + NT))
                        for k in range(KD, KD + 4):
                            mixed_split(l, k)
                    if MO + 1 <= s < MO + 5:
                        f = s - MO - 1
                        pool.wait_ge(o_tanh.sem, o_tanh.at(l, f + 1))
                        nc.gpsimd.tensor_scalar(tile_of(proj, MO + f), tile_of(proj, MO + f), 0.5, 0.5,
                                                ALU.mult, ALU.add).then_inc(o_sig.sem, 1)
                    if s == N_IN - 1:
                        pool.wait_ge(split.sem, split.at(l, N_IN))
                        pool.wait_ge(evac.sem, evac.at(l, N_IN))
                        link(nc.gpsimd.memset(rstd[64:96, :], 0.0))
                        for e in range(2 * MLA_H):
                            if e == 2 * MLA_H - 1:
                                rest(l, S_OUT1)
                                pool.wait_ge(split.sem, split.at(l, S_OUT1 + 1))
                            rotate(l, e)
                            if e == 1:
                                pool.wait_ge(w_used.sem, w_used.at(l, N_IN))
                                pool.wait_ge(rs_used.sem, rs_used.at(l, 9))
                                pool.wait_ge(tr_evac.sem, tr_evac.at(l, TR_OM + NT))
                            if e % 2 and 1 <= e // 2 <= KD // 2:
                                mixed_split(l, e - 3)
                                mixed_split(l, e - 2)
                                pool.wait_ge(mixed.sem, mixed.at(l, e - 1))
                    t = s - G_SSD - 4
                    if 0 <= t < 8:
                        pool.wait_ge(rs_used.sem, rs_used.at(l, t + 1))
                        pool.wait_ge(rot_ready.sem, rot_ready.at(l, t + 1))
                        nc.gpsimd.tensor_tensor(tile_of(proj, DQ + t), tile_of(proj, DQ + t), C("cos_d"),
                                                ALU.mult).then_inc(qcos.sem, 1)

        @block.tensor
        def _(pe):
            def product(p, lhs_t, rhs, start, stop, rows_=slice(0, P)):
                for a in range(2):
                    last = nc.tensor.matmul(pb[rows_, 2 * p + a, 0:HALF], lhs_t, rhs[:, a * HALF:(a + 1) * HALF],
                                            start=start, stop=stop)
                return last

            def norm_sum(l, s0, n, p, rows_=slice(0, P), ones="ones"):
                for k in range(n):
                    pe.wait_ge(sq_ready.sem, sq_ready.at(l, s0 + k + 1))
                    product(p, C(ones, rows_), sq[rows_, (s0 + k) % 2, :], k == 0, k == n - 1).then_inc(sq_used.sem, 1)

            def residual_sum(l, count):
                pe.wait_ge(added.sem, added.at(l, count * KD))
                product(0, C("ones"), rstd2, True, True).then_inc(res_sum.sem, 1)

            def split_product(l, g, k0, k1, operand):
                p = bank_pair(g)
                k_all = KF if g >= G_FOUT else KD
                for k in range(k0, k1):
                    s = g + k // KD if g < G_FOUT else S_FOUT + 3 * (g - G_FOUT) + k // KD
                    n = l * N_SLOT + s
                    if k % KD == 0:
                        pe.wait_ge(split.sem, n + 1)
                    c = k % KD
                    w_lead = parts[:, n % PARTS, 0, c * P:(c + 1) * P]
                    w_rest = parts[:, n % PARTS, 1, c * P:(c + 1) * P]
                    lead, rest = operand(k)
                    product(p, w_lead, lead, k == 0, False)
                    product(p, w_lead, rest, False, False)
                    last = product(p, w_rest, lead, False, k == k_all - 1)
                    if c == KD - 1 or k == k_all - 1:
                        last.then_inc(w_used.sem, 1)

            def dense(l, g, operand):
                pe.wait_ge(evac.sem, evac.at(l, max(g - 2, 0)))
                split_product(l, g, 0, KF if g >= G_FOUT else KD, operand)

            def beside(l, g, j, operand, chunks):
                if chunks[j][0] == 0 and chunks[j][1] > 0:
                    pe.wait_ge(evac.sem, evac.at(l, g))
                split_product(l, g, *chunks[j], operand)

            def row_bcast(l, u, p):
                pe.wait_ge(e_raw.sem, e_raw.at(l, u * NT))
                r = C("rowsel")[:, unit(u)[2]:unit(u)[2] + 1].to_broadcast([P, P])
                if u == 0:
                    product(p, r, rows, True, True).then_inc(rowb.sem, 1)
                else:
                    pe.wait_ge(rows_split.sem, rows_split.at(l, 2))
                    r = sel_r[:, unit(u)[2]:unit(u)[2] + 1].to_broadcast([P, P])
                    product(p, r, tile_of(proj_r, BM), True, False)
                    product(p, r, tile_of(proj_r, CM), False, True).then_inc(rowb.sem, 1)

            def out_transposes(l, idx, src, i):
                b = 4 + idx % 2
                pe.wait_ge(tr_evac.sem, tr_evac.at(l, max(idx - 1, 0)))
                for f in range(4):
                    last = src(b, f, i)
                last.then_inc(tr_ready.sem, 1)

            def to_tokens(tile0):
                def one(b, f, i):
                    a, w = TILES[i]
                    return nc.tensor.transpose(pb[0:w, b, f * P:(f + 1) * P], tile_of(proj, tile0 + f, a, a + w), C("ident"))
                return one

            def to_features(buf):
                def one(b, f, i):
                    w = TILES[i][1]
                    return nc.tensor.transpose(pb[:, b, f * P:f * P + w], buf[0:w, i, f * P:(f + 1) * P],
                                               C("ident")[0:w, 0:w])
                return one

            for l in range(DEPTH):
                for g in range(G_SSD):
                    if g == 0:
                        for k in range(KD):
                            pe.wait_ge(xg_ready.sem, xg_ready.at(l, k + 1))
                            pe.wait_ge(evac.sem, evac.at(l, 0))
                            split_product(l, 0, k, k + 1, xg_parts)
                    else:
                        dense(l, g, xg_parts)
                    if g == 1:
                        pe.wait_ge(const_in.sem, 16)
                        residual_sum(l, 1)

                pe.wait_ge(evac.sem, evac.at(l, G_SSD))
                pe.wait_ge(rows_ready.sem, rows_ready.at(l, 1))
                pe.wait_ge(cleared.sem, 5)
                for i, (a, w) in enumerate(TILES):
                    o = pb[0:w, 7, i * NCOL:(i + 1) * NCOL]
                    nc.tensor.matmul(o, rows[:, a:a + w], C("lin_rs"), start=True, stop=False)
                    nc.tensor.matmul(o, kh[0:NDEC, 1, a:a + w], C("lin_i", slice(0, NDEC)), start=False, stop=False)
                    last = nc.tensor.matmul(o, mbuf[0:NDEC, 1, a:a + w], C("lin_sp", slice(0, NDEC)), start=False, stop=True)
                last.then_inc(cols_ps.sem, 1)

                pe.wait_ge(conv_act.sem, conv_act.at(l, 6))
                for i in range(NT):
                    out_transposes(l, TR_X + i, to_tokens(XS), i)
                row_bcast(l, 0, 0)
                for g in range(SSD_G):
                    r = slice(64 * g, 64 * g + 64)
                    for j, (a, w) in enumerate(TILES):
                        pe.wait_ge(tr_evac.sem, tr_evac.at(l, TR_X + NT))
                        pe.wait_ge(cb_ready.sem, cb_ready.at(l, max(g * NT + j - 1, 0)))
                        product(1 + (g * NT + j) % 2, tile_of(proj, BM, a, a + w, r), tile_of(proj, CM, rows_=r), True, True,
                                slice(0, w)).then_inc(cb_ps.sem, 1)
                pe.wait_ge(cols_ready.sem, cols_ready.at(l, 1))
                pe.wait_ge(cb_ready.sem, cb_ready.at(l, 2 * NT))
                for u in range(2 * SSD_H):
                    hd, d, _ = unit(u)
                    if d == 0:
                        pe.wait_ge(y_evac.sem, y_evac.at(l, max(hd - 1, 0)))
                    for j, (_, kw) in enumerate(TILES):
                        n = u * NT + j
                        pe.wait_ge(m_ready.sem, m_ready.at(l, n + 1))
                        blocks = range(j, NT) if d == 0 else range(j + 1)
                        lo = rng(d, j)[0]
                        for i in blocks:
                            last = nc.tensor.matmul(pb[:, 6 + hd % 2, i * SSD_P:(i + 1) * SSD_P],
                                                    mbuf[0:kw, n % 2, i * P - lo:i * P - lo + P],
                                                    x_tok[0:kw, j, hd * SSD_P:(hd + 1) * SSD_P],
                                                    start=(d == 0 and j == 0 and i == 0), stop=(d == 1 and j == NT - 1),
                                                    skip_group_check=True)
                        last.then_inc(m_used.sem, 1)
                        if j == NT - 2 and u + 1 < 2 * SSD_H:
                            row_bcast(l, u + 1, 0)
                        beside(l, G_SSD + u, j, xg_parts, CHUNKS_SSD)
                        if j == 0 and 0 <= u - 4 < 8:
                            pe.wait_ge(rs_ready.sem, rs_ready.at(l, RS_D + min(u - 2, 8)))
                            pe.wait_ge(rs_used.sem, rs_used.at(l, u - 3))
                            product(1, C("perm_d"), tile_of(proj, DQ + u - 4), True, True).then_inc(rot_ready.sem, 1)
                        if j == 2 and 0 <= u - 2 < 8:
                            pe.wait_ge(rot_used.sem, rot_used.at(l, max(u - 3, 0)))
                            norm_sum(l, SQ_D + u - 2, 1, 1, ones="ones_h")

                pe.wait_ge(y_evac.sem, y_evac.at(l, SSD_H))
                pe.wait_ge(evac.sem, evac.at(l, G_ML))
                for i in range(NT):
                    out_transposes(l, TR_OS + i, to_features(o_tok), i)
                row_bcast(l, 2 * SSD_H, 0)
                for i in range(NT):
                    out_transposes(l, TR_MV + i, to_tokens(MV), i)
                norm_sum(l, SQ_S, 4, 3)

                def qk(n):
                    u, j = 2 * SSD_H + n // NT, n % NT
                    hd, d, _ = unit(u)
                    a, w = TILES[j]
                    lo, hi = rng(d, j)
                    r = slice(64 * (hd % 2), 64 * (hd % 2) + 64)
                    k_t = tile_of(proj, MK + hd // 2, a, a + w, r)
                    q_t = tile_of(proj, MQ + hd // 2, rows_=r)
                    if hi - lo == T:
                        product(1, k_t, q_t, True, True, slice(0, w)).then_inc(qk_ps.sem, 1)
                    else:
                        nc.tensor.matmul(pb[0:w, 2, 0:hi - lo], k_t, q_t[:, lo:hi], start=True, stop=True).then_inc(qk_ps.sem, 1)

                pe.wait_ge(roped.sem, roped.at(l, 8))
                qk(0)
                pe.wait_ge(tr_evac.sem, tr_evac.at(l, TR_MV + NT))
                pe.wait_ge(rs_ready.sem, rs_ready.at(l, RS_S + 1))
                pe.wait_ge(roped.sem, roped.at(l, 8))
                for n in range(STEPS_ML):
                    v, j = n // NT, n % NT
                    hd, d, _ = unit(2 * SSD_H + v)
                    pe.wait_ge(m_ready.sem, m_ready.at(l, STEPS_SSD + n + 1))
                    if n + 1 < STEPS_ML:
                        qk(n + 1)
                    if j == 0:
                        pe.wait_ge(nd_evac.sem, nd_evac.at(l, v))
                    kw = TILES[j][1]
                    lo = rng(d, j)[0]
                    for i in (range(j, NT) if d == 0 else range(j + 1)):
                        first = (j == 0 and i in (0, 3)) if d == 0 else (i, j) in ((0, 0), (3, 3))
                        c = (i % 3) * (ML_V + 1)
                        last = nc.tensor.matmul(pb[:, 4 + i // 3, c:c + ML_V + 1],
                                                mbuf[0:kw, (STEPS_SSD + n) % 2, i * P - lo:i * P - lo + P],
                                                v_ml[0:kw, j, hd, :], start=first, stop=(j == NT - 1), skip_group_check=True)
                    last.then_inc(m_used.sem, 1)
                    if j == NT - 2 and v + 1 < 2 * ML_H:
                        row_bcast(l, 2 * SSD_H + v + 1, 0)
                    if v in JOB_UNITS and j == 1:
                        pe.wait_ge(evac.sem, evac.at(l, G_ML + v))
                        norm_sum(l, *JOB_UNITS[v][0:2], 3)
                    if v in JOB_UNITS and j == 3:
                        pe.wait_ge(rs_ready.sem, rs_ready.at(l, JOB_UNITS[v][2] + 1))
                    beside(l, G_ML + v, j, xg_parts, LATE_CHUNKS if v in JOB_UNITS else CHUNKS_ML)
                for j in range(NT):
                    beside(l, N_IN - 1, j, xg_parts, CHUNKS_DIFF)

                n_uv = l * N_RAW + N_IN
                pe.wait_ge(loaded[n_uv % RAW].sem, 16 * (n_uv // RAW + 1))
                w_uv = raw[:, n_uv % RAW, :]
                pe.wait_ge(nd_evac.sem, nd_evac.at(l, 2 * ML_H))
                pe.wait_ge(rs_used.sem, rs_used.at(l, 11))
                def v_product(i):
                    a, wd = TILES[i]
                    pe.wait_ge(v_ready.sem, v_ready.at(l, max(i - 1, 0)))
                    for c in range(2):
                        last = nc.tensor.matmul(pb[0:wd, 4 + i % 2, 0:512], tile_of(proj, CKV + c, a, a + wd),
                                                w_uv[:, c * 512:(c + 1) * 512], start=(c == 0), stop=(c == 1))
                    last.then_inc(v_ps.sem, 1)

                def prep(stage, hd):
                    side = stage // 3
                    e = 2 * hd + side
                    rws = slice(0, MLA_ROWS)
                    if stage in (0, 3):
                        pe.wait_ge(rs_ready.sem, rs_ready.at(l, RS_M + e))
                    if stage == 0:
                        pe.wait_ge(head_in[1 + hd // UQ_HEADS].sem, 16 * (l + 1))
                    if stage in (0, 1):
                        w = w_head[:, 1 + hd // UQ_HEADS, :]
                        o = (hd % UQ_HEADS) * 3 * MLA_ROWS
                        for c in ((0,), (1, 2))[stage]:
                            last = product(3, w[:, o + c * MLA_ROWS:o + (c + 1) * MLA_ROWS], tile_of(proj, CQ + c), c == 0, c == 2, rws)
                        if stage == 1:
                            last.then_inc(p_ps.sem, 1)
                    elif stage == 3:
                        pe.wait_ge(head_in[0].sem, 16 * (l + 1))
                        for c in range(2):
                            o = (2 * hd + c) * MLA_NOPE
                            last = product(3, w_head[:, 0, o:o + MLA_NOPE], tile_of(proj, CKV + c), c == 0, c == 1, slice(0, MLA_NOPE))
                        last.then_inc(p_ps.sem, 1)
                    else:
                        pe.wait_ge(p_copy.sem, p_copy.at(l, e + 1))
                        norm_sum(l, SQ_M + e, 1, 3, rws)

                def scores(n):
                    q, k, _, _, _, i, hd = att(n)
                    pe.wait_ge(p_ready.sem, p_ready.at(l, max(n - 1, 0)))
                    if n < N_ATT_M and i == 0:
                        pe.wait_ge(roped.sem, roped.at(l, 8 + 2 * hd + 2))
                    if n < N_ATT_M:
                        product(n % 2, q, k, True, True).then_inc(s_ps.sem, 1)
                        return
                    pe.wait_ge(stacks.sem, stacks.at(l, hd + 1))
                    own = slice(64 * (hd % 2), 64 * (hd % 2) + 64)
                    _, k_lead, k_rest = stacked(hd)
                    c = (MQ + 3 * (hd % 2)) * T + i * P
                    product(n % 2, proj_r[:, c:c + P], k_lead, True, False)
                    product(n % 2, proj_r[own, c:c + P], k_rest[own, :], False, True).then_inc(s_ps.sem, 1)

                def turn(n):
                    pe.wait_ge(p_ready.sem, p_ready.at(l, n + 1))
                    pe.wait_ge(o_evac.sem, o_evac.at(l, max(n - 1, 0)))
                    pe.wait_ge(pt_tail.sem, pt_tail.at(l, n))
                    a, w = TILES[-1]
                    nc.tensor.transpose(pb[0:w, TAIL_O, 0:P], ebuf[:, n % 2, a:a + w], C("ident")).then_inc(tail_ps.sem, 1)
                    pe.wait_ge(pt_main.sem, pt_main.at(l, n))
                    for j, (a, w) in enumerate(TILES[:-1]):
                        last = nc.tensor.transpose(pb[:, TURN, j * P:(j + 1) * P], ebuf[:, n % 2, a:a + w], C("ident"))
                    last.then_inc(t_ps.sem, 1)

                def values(n):
                    _, _, v, dv, _, _, _ = att(n)
                    pe.wait_ge(pt_main.sem, pt_main.at(l, n + 1))
                    pe.wait_ge(pt_tail.sem, pt_tail.at(l, min(n + 2, N_ATT_M if n < N_ATT_M else N_ATT)))
                    pe.wait_ge(o_evac.sem, o_evac.at(l, n))
                    for j, (_, w) in enumerate(TILES):
                        last = nc.tensor.matmul(pb[:, TAIL_O, P:P + dv], mbuf[0:w, n % 2, j * P:(j + 1) * P],
                                                v(j), start=(j == 0), stop=(j == NT - 1))
                    last.then_inc(o_ps.sem, 1)

                def mlstm_turned(i):
                    pe.wait_ge(v_ready.sem, v_ready.at(l, NT))
                    pe.wait_ge(oscaled.sem, oscaled.at(l, i + 1))
                    out_transposes(l, TR_OM + i, to_features(o_ml), i)

                def first_prep(stage, hd):
                    pe.wait_ge(evac.sem, evac.at(l, N_IN))
                    prep(stage, hd)

                opening(v_product, mlstm_turned, first_prep)
                pe.wait_ge(tr_evac.sem, tr_evac.at(l, TR_OM + NT))
                scores(0)
                for n in range(N_ATT_M):
                    hd, i = n // NT, n % NT
                    if n + 1 < N_ATT_M:
                        scores(n + 1)
                    turn(n)
                    prepare(prep, n)
                    if out1_part(n):
                        g, k = out1_part(n)
                        pe.wait_ge(mixed.sem, mixed.at(l, KD))
                        pe.wait_ge(rs_ready.sem, rs_ready.at(l, RS_M + 2 * MLA_H))
                        beside(l, G_OUT1 + g, 0, mixed_parts, ((k, k + 1),))
                    if n >= 1:
                        values(n - 1)
                values(N_ATT_M - 1)

                pe.wait_ge(o_evac.sem, o_evac.at(l, N_ATT_M))
                for i in range(NT):
                    out_transposes(l, TR_DV + i, to_tokens(DV), i)
                beside(l, G_OUT1 + 1, 0, mixed_parts, ((0, KD),))
                for i in range(NT):
                    pe.wait_ge(oscaled.sem, oscaled.at(l, NT + i + 1))
                    out_transposes(l, TR_OA + i, to_features(o_tok), i)
                pe.wait_ge(tr_evac.sem, tr_evac.at(l, TR_OA + NT))
                scores(N_ATT_M)
                for n in range(N_ATT_M, N_ATT):
                    if n + 1 < N_ATT:
                        scores(n + 1)
                    turn(n)
                    g, k = out1_part(n)
                    beside(l, G_OUT1 + g, 0, mixed_parts, ((k, k + 1),))
                    if n > N_ATT_M:
                        values(n - 1)
                values(N_ATT - 1)
                beside(l, G_OUT2 - 1, 0, mixed_parts, ((0, KD),))
                pe.wait_ge(o_evac.sem, o_evac.at(l, N_ATT))
                for i in range(NT):
                    pe.wait_ge(oscaled.sem, oscaled.at(l, 2 * NT + i + 1))
                    out_transposes(l, TR_OD + i, to_features(o_dif), i)

                pe.wait_ge(tr_evac.sem, tr_evac.at(l, TR_OD + NT))
                pe.wait_ge(p_ready.sem, p_ready.at(l, N_ATT))
                pe.wait_ge(evac.sem, evac.at(l, G_OUT2))
                for k in range(KD):
                    pe.wait_ge(mixed.sem, mixed.at(l, KD + k + 1))
                    split_product(l, G_OUT2, k, k + 1, lambda k: mixed_parts(KD + k))
                for g in range(1, KD):
                    dense(l, G_OUT2 + g, lambda k: mixed_parts(KD + k))

                for k in range(KD):
                    pe.wait_ge(xg_ready.sem, xg_ready.at(l, KD + k + 1))
                    if k == 0:
                        pe.wait_ge(evac.sem, evac.at(l, G_FIN - 2))
                    split_product(l, G_FIN, k, k + 1, ffn_parts)
                residual_sum(l, 2)
                for g in range(1, 2 * KF):
                    dense(l, G_FIN + g, ffn_parts)
                for k in range(KF):
                    if k == 0:
                        pe.wait_ge(evac.sem, evac.at(l, G_FOUT - 2))
                    pe.wait_ge(act_ready.sem, act_ready.at(l, k + 1))
                    split_product(l, G_FOUT, k, k + 1, act_parts)
                for g in range(1, KD):
                    dense(l, G_FOUT + g, act_parts)

        @block.scalar
        def _(act):
            chained = [0]

            def link(ins):
                chained[0] += 1
                ins.then_inc(act_chain.sem, 1)
                act.wait_ge(act_chain.sem, chained[0])

            def square(l, s, src, rows_=slice(0, P)):
                act.wait_ge(sq_used.sem, sq_used.at(l, max(s - 1, 0)))
                nc.scalar.activation(halves(sq[rows_, s % 2, :]), src, ACT.Square).then_inc(sq_ready.sem, 1)

            def residual_square(l, s, k):
                n = KD * s + k
                act.wait_ge(added.sem, added.at(l, max(n - 1, 0)))
                nc.scalar.activation(halves(sq[:, k % 2, :]), halves(h[:, k, :]), ACT.Square).then_inc(res_sq.sem, 1)

            def residual_rstd(l, s):
                act.wait_ge(res_sum.sem, res_sum.at(l, s + 1))
                link(nc.scalar.activation(halves(rstd[:, :]), pair(0), ACT.Ln, scale=1.0 / D_MODEL, bias=eps[:, :]))
                nc.scalar.activation(rstd[:, :], rstd[:, :], ACT.Exp, scale=-0.5).then_inc(rs_ready.sem, 1)

            def rsqrt(l, s, p, n, dst, rows_=slice(0, P)):
                act.wait_ge(sq_used.sem, sq_used.at(l, s))
                link(nc.scalar.activation(halves(dst[rows_, :]), pair(p, rows_), ACT.Ln, scale=1.0 / n, bias=eps[rows_, :]))
                nc.scalar.activation(dst[rows_, :], dst[rows_, :], ACT.Exp, scale=-0.5).then_inc(rs_ready.sem, 1)

            def exps(l, n):
                u, j = n // NT, n % NT
                lo, hi = rng(unit(u)[1], j)
                e = ebuf[0:TILES[j][1], n % 2, 0:hi - lo]
                act.wait_ge(e_raw.sem, e_raw.at(l, n + 1))
                nc.scalar.activation(e, e, ACT.Exp).then_inc(e_exp.sem, 1)

            def out_squares(l, base, buf, width_rows=None):
                for i in range(NT):
                    if i >= 2:
                        act.wait_ge(ored.sem, ored.at(l, base + i - 1))
                    nc.scalar.activation(ebuf[:, i % 2, 0:512], buf[:, i, :], ACT.Square).then_inc(osq.sem, 1)

            def out_rstd(l, which, groups):
                act.wait_ge(ored.sem, ored.at(l, (which + 1) * NT))
                link(nc.scalar.activation(hs[:, 0:groups * NT], hs[:, 0:groups * NT], ACT.Ln, scale=groups / 512.0, bias=eps[:, :]))
                nc.scalar.activation(hs[:, 0:groups * NT], hs[:, 0:groups * NT], ACT.Exp, scale=-0.5).then_inc(orstd.sem, 1)

            def softmax(l, n):
                scale = att(n)[4]
                act.wait_ge(max_ready.sem, max_ready.at(l, n + 1))
                act.wait_ge(t_ps.sem, t_ps.at(l, max(n - 1, 0)))
                act.wait_ge(o_evac.sem, o_evac.at(l, max(n - 3, 0)))
                nc.scalar.activation(halves(ebuf[:, n % 2, :]), pair(n % 2), ACT.Exp, scale=scale, bias=negmax[:, n % 2:n % 2 + 1],
                                     accum_out=sums[:, n % 4:n % 4 + 1]).then_inc(p_ready.sem, 1)

            def turned(l, n):
                act.wait_ge(t_ps.sem, t_ps.at(l, n + 1))
                act.wait_ge(o_ps.sem, o_ps.at(l, max(n - 1, 0)))
                nc.scalar.activation(mbuf[:, n % 2, 0:512], pb[:, TURN, 0:512], ACT.Copy).then_inc(pt_main.sem, 1)

            def lead(l, s):
                l, s = l + s // N_SLOT, s % N_SLOT
                if l == DEPTH:
                    return
                n, r = l * N_SLOT + s, l * N_RAW + s + (s >= N_IN)
                act.wait_ge(loaded[r % RAW].sem, 16 * (r // RAW + 1))
                if n >= PARTS:
                    act.wait_ge(w_used.sem, n - PARTS + 1)
                if s == N_IN:
                    act.wait_ge(p_ps.sem, p_ps.at(l, 2 * MLA_H))
                nc.scalar.activation(parts[:, n % PARTS, 0, :], raw[:, r % RAW, :], ACT.Copy).then_inc(lead_ready.sem, 1)

            act.wait_ge(par_in.sem, 16)
            act.wait_ge(eps_ready.sem, 1)
            for l in range(DEPTH):
                if l == 0:
                    nc.scalar.preload_act_table_set("natural_log_exp_and_others")
                    for k in range(KD):
                        act.wait_ge(x_in[k].sem, 16)
                        residual_square(l, 0, k)
                        if k < PARTS:
                            lead(l, k)
                lead(l, 2)
                residual_rstd(l, 0)

                nc.scalar.preload_act_table_set("silu_and_others")
                for g in range(1, G_SSD + 1):
                    if 1 < g < G_SSD:
                        lead(l, g + 1)
                    if 0 <= g - 2 < 6:
                        f = g - 2
                        act.wait_ge(conv_ready.sem, conv_ready.at(l, f + 1))
                        nc.scalar.activation(tile_of(proj, f), kh[:, f % 2, :], ACT.Silu).then_inc(conv_act.sem, 1)
                    if g == ZT + 1:
                        nc.scalar.preload_act_table_set("natural_log_exp_and_others")
                        d24 = slice(0, NDEC)
                        act.wait_ge(dec_u.sem, dec_u.at(l, 1))
                        link(nc.scalar.activation(ebuf[d24, 1, :], ebuf[d24, 0, :], ACT.Abs))
                        link(nc.scalar.activation(ebuf[d24, 1, :], ebuf[d24, 1, :], ACT.Exp, scale=-1.0))
                        link(nc.scalar.activation(ea[d24, :], par_at(l, "a_log", rows_=d24), ACT.Exp))
                        nc.scalar.activation(ebuf[d24, 1, :], ebuf[d24, 1, :], ACT.Ln, bias=1.0).then_inc(dec_ln.sem, 1)
                        act.wait_ge(lam_sum.sem, lam_sum.at(l, 1))
                        nc.scalar.activation(lam_e[:, :], lam_s[:, :], ACT.Exp).then_inc(lam_exp.sem, 1)
                        nc.scalar.preload_act_table_set("silu_and_others")
                    if g > MISC + 1:
                        act.wait_ge(evac.sem, evac.at(l, g))
                        t = tile_of(proj, g - 1)
                        if g - 1 < MO:
                            nc.scalar.activation(t, t, ACT.Silu).then_inc(z_act.sem, 1)
                        else:
                            nc.scalar.activation(t, t, ACT.Tanh, scale=0.5).then_inc(o_tanh.sem, 1)
                nc.scalar.preload_act_table_set("natural_log_exp_and_others")

                for n in range(STEPS_SSD):
                    u, j = n // NT, n % NT
                    exps(l, n)
                    if j == 1:
                        lead(l, G_SSD + u + 1)
                    if j == 2 and 0 <= u - 1 < 8:
                        act.wait_ge(evac.sem, evac.at(l, DQ + u))
                        square(l, SQ_D + u - 1, halves(tile_of(proj, DQ + u - 1)))
                    if j == NT - 1 and 0 <= u - 2 < 8:
                        act.wait_ge(rs_used.sem, rs_used.at(l, u - 2))
                        rsqrt(l, SQ_D + u - 1, 1, DIFF_QK, rstd2)
                act.wait_ge(cols_ready.sem, cols_ready.at(l, 1))
                nc.scalar.activation(enm[:, :, :], cols[:, :, C_NM:NCOL], ACT.Exp).then_inc(enm_ready.sem, 1)
                act.wait_ge(tr_evac.sem, tr_evac.at(l, TR_OS + NT))
                for f in range(4):
                    square(l, SQ_S + f, halves(tile_of(proj, ZT + f)))
                exps(l, STEPS_SSD)
                act.wait_ge(rs_used.sem, rs_used.at(l, 8))
                rsqrt(l, SQ_S + 4, 3, 512, rstd2)
                def tile_square(s, g):
                    act.wait_ge(evac.sem, evac.at(l, g + 1))
                    square(l, SQ_C + s, halves(tile_of(proj, g)))

                for n in range(STEPS_SSD, STEPS):
                    v, j = (n - STEPS_SSD) // NT, n % NT
                    if n > STEPS_SSD:
                        exps(l, n)
                    if (v, j) in ((3, 2), (3, 3), (4, 1)):
                        s = j - 2 if v == 3 else 2
                        tile_square(s, CQ + s)
                    if (v, j) in ((5, 2), (5, 3)):
                        tile_square(3 + j - 2, CKV + j - 2)
                    if (v, j) == (4, 2):
                        act.wait_ge(rs_used.sem, rs_used.at(l, 9))
                        rsqrt(l, SQ_C + 3, 3, Q_RANK, rstd2)
                    if (v, j) == (6, 2):
                        act.wait_ge(rs_used.sem, rs_used.at(l, 10))
                        rsqrt(l, SQ_C + 5, 3, KV_RANK, rstd2)
                    if j == 1:
                        lead(l, G_ML + v + 1)
                act.wait_ge(nd_evac.sem, nd_evac.at(l, 2 * ML_H))
                out_squares(l, 0, o_ml)
                out_rstd(l, 0, ML_H)

                rws = slice(0, MLA_ROWS)

                def prep(stage, hd):
                    side = stage // 3
                    e = 2 * hd + side
                    if stage in (1, 3):
                        act.wait_ge(p_copy.sem, p_copy.at(l, e + 1))
                        act.wait_ge(sq_used.sem, sq_used.at(l, SQ_M + e - 1))
                        nc.scalar.activation(sq[rws, (SQ_M + e) % 2, :], (qh, kh)[side][rws, hd % 2, 0:T],
                                             ACT.Square).then_inc(sq_ready.sem, 1)
                    elif stage in (2, 4):
                        act.wait_ge(rs_used.sem, rs_used.at(l, 11 + e))
                        rsqrt(l, SQ_M + e + 1, 3, MLA_QK, rstd2, rws)

                for s in range(NT + 3):
                    prep(s % NT, s // NT)
                softmax(l, 0)
                for n in range(N_ATT_M):
                    hd, i = n // NT, n % NT
                    if n + 1 < N_ATT_M:
                        softmax(l, n + 1)
                    turned(l, n)
                    prepare(prep, n)
                    if n in (N_ATT_M - KD - 2, N_ATT_M - KD - 1):
                        lead(l, S_OUT1 + n - (N_ATT_M - KD - 2))
                act.wait_ge(o_evac.sem, o_evac.at(l, N_ATT_M))
                out_squares(l, NT, o_tok)
                out_rstd(l, 1, 1)
                lead(l, S_OUT1 + 2)
                softmax(l, N_ATT_M)
                for n in range(N_ATT_M, N_ATT):
                    if n + 1 < N_ATT:
                        softmax(l, n + 1)
                    turned(l, n)
                    g, k = out1_part(n)
                    if k == 0:
                        lead(l, S_OUT1 + g + 1)
                lead(l, S_OUT2)
                act.wait_ge(o_evac.sem, o_evac.at(l, N_ATT))
                out_squares(l, 2 * NT, o_dif)
                out_rstd(l, 2, DIFF_H)
                lead(l, S_OUT2 + 1)

                for k in range(KD):
                    lead(l, S_OUT2 + k + 2)
                    act.wait_ge(evac.sem, evac.at(l, G_OUT2 + k + 1))
                    residual_square(l, 1, k)
                residual_rstd(l, 1)
                nc.scalar.preload_act_table_set("silu_and_others")
                for j in range(KF):
                    lead(l, S_FIN + 2 * j + 2)
                    act.wait_ge(evac.sem, evac.at(l, G_FIN + 2 * j + 1))
                    nc.scalar.activation(ebuf[:, j % 2, :], ebuf[:, j % 2, :], ACT.Silu).then_inc(gsilu.sem, 1)
                    lead(l, S_FIN + 2 * j + 3)
                if l + 1 < DEPTH:
                    nc.scalar.preload_act_table_set("natural_log_exp_and_others")
                for s in range(S_FOUT + 2, N_SLOT + 2):
                    lead(l, s)
                    k = s - S_FOUT - 4
                    if k >= 0 and k % 3 == 0 and l + 1 < DEPTH:
                        act.wait_ge(evac.sem, evac.at(l, G_FOUT + k // 3 + 1))
                        residual_square(l + 1, 0, k // 3)

        @block.vector
        def _(dve):
            chained = [0]

            def link(ins):
                chained[0] += 1
                ins.then_inc(dve_chain.sem, 1)
                dve.wait_ge(dve_chain.sem, chained[0])

            def gains(l, k, name, dst):
                lead, rest = dst(k)
                g = par_at(l, name, k)
                link(nc.vector.tensor_scalar(lead, h[:, k, :], g, None, ALU.mult))
                nc.vector.scalar_tensor_tensor(out=rest, in0=h[:, k, :], scalar=g, in1=lead.bitcast(FP32), op0=ALU.mult,
                                               op1=ALU.subtract).then_inc(xg_ready.sem, 1)

            def add_square(l, s, k):
                n = KD * s + k
                dve.wait_ge(res_sq.sem, res_sq.at(l, n + 1))
                if k:
                    dve.wait_ge(added.sem, added.at(l, n))
                    nc.vector.tensor_tensor(rstd2[:, :], rstd2[:, :], sq[:, k % 2, :], ALU.add).then_inc(added.sem, 1)
                else:
                    nc.vector.tensor_copy(rstd2[:, :], sq[:, 0, :]).then_inc(added.sem, 1)

            def mixed_split(l, k):
                lead, rest = mixed_parts(k)
                link(nc.vector.tensor_copy(lead, tile_of(proj, MIXED[k])))
                nc.vector.tensor_tensor(rest, tile_of(proj, MIXED[k]), lead.bitcast(FP32), ALU.subtract).then_inc(mixed.sem, 1)

            def scale_out(l, g, dst):
                dve.wait_ge(w_used.sem, w_used.at(l, slot_end(g)))
                nc.vector.tensor_tensor(halves(dst), pair(bank_pair(g)), halves(rstd[:, :]), ALU.mult).then_inc(evac.sem, 1)

            def residual(l, g, k):
                dve.wait_ge(w_used.sem, w_used.at(l, slot_end(g)))
                nc.vector.tensor_tensor(halves(h[:, k, :]), halves(h[:, k, :]), pair(bank_pair(g)), ALU.add).then_inc(evac.sem, 1)

            def conv(l, f):
                if f >= 2:
                    dve.wait_ge(conv_act.sem, conv_act.at(l, f - 1))
                mid = TAPS // 2
                acc, src = kh[:, f % 2, :], tile_of(proj, f)
                link(nc.vector.tensor_scalar(acc, src, par_at(l, "conv_w", f * TAPS + mid), par_at(l, "conv_b", f), ALU.mult, ALU.add))
                shifts = [s for s in range(-mid, mid + 1) if s]
                for s in shifts:
                    a, b = max(0, -s), T - max(0, s)
                    ins = nc.vector.scalar_tensor_tensor(out=acc[:, a:b], in0=src[:, a + s:b + s],
                                                         scalar=par_at(l, "conv_w", f * TAPS + mid + s), in1=acc[:, a:b],
                                                         op0=ALU.mult, op1=ALU.add)
                    if s == shifts[-1]:
                        ins.then_inc(conv_ready.sem, 1)
                    else:
                        link(ins)

            def normed(l, src, gain, rows_=slice(0, P), count=True):
                ins = nc.vector.scalar_tensor_tensor(out=src, in0=src, scalar=gain, in1=rstd2[rows_, :], op0=ALU.mult, op1=ALU.mult)
                return ins.then_inc(rs_used.sem, 1) if count else ins

            def from_transposes(l, idx, dst, i, f_major=False, op=None):
                dve.wait_ge(tr_ready.sem, tr_ready.at(l, idx + 1))
                w = TILES[i][1]
                b = 4 + idx % 2
                src = pb[:, b, :].rearrange("p (f t) -> p f t", f=4)[:, :, 0:w] if f_major else pb[0:w, b, 0:512]
                op(dst, src).then_inc(tr_evac.sem, 1)

            def copy(dst, src):
                return nc.vector.tensor_copy(dst, src)

            def feature_block(buf, tile0, i):
                a, w = TILES[i]
                return buf[:, tile0 * T:(tile0 + 4) * T].rearrange("p (f t) -> p f t", t=T)[:, :, a:a + w]

            def exponents(l, n):
                u, j = n // NT, n % NT
                _, d, r = unit(u)
                lo, hi = rng(d, j)
                w = TILES[j][1]
                rw = slice(0, w)
                if j == 0:
                    dve.wait_ge(rowb.sem, rowb.at(l, u + 1))
                dve.wait_ge(m_ready.sem, m_ready.at(l, max(n - 1, 0)))
                e = ebuf[rw, n % 2, :]
                m = mask(d, j)
                runs = [(lo, hi)] if hi <= HALF or lo >= HALF else [(lo, HALF), (HALF, hi)]
                if (lo, hi) == (0, T):
                    ins = nc.vector.scalar_tensor_tensor(out=halves(e[:, 0:T]), in0=pair(0, rw), scalar=cols[rw, j, r:r + 1],
                                                         in1=halves(m), op0=ALU.add, op1=ALU.min)
                else:
                    for a, b in runs:
                        ins = nc.vector.scalar_tensor_tensor(out=e[:, a - lo:b - lo],
                                                             in0=pb[rw, a // HALF, a % HALF:a % HALF + b - a],
                                                             scalar=cols[rw, j, r:r + 1], in1=m[:, a - lo:b - lo],
                                                             op0=ALU.add, op1=ALU.min)
                ins.then_inc(e_raw.sem, 1)

            def weights(l, n):
                u, j = n // NT, n % NT
                hd, d, r = unit(u)
                lo, hi = rng(d, j)
                rw = slice(0, TILES[j][1])
                e, m = ebuf[rw, n % 2, 0:hi - lo], mbuf[rw, n % 2, 0:hi - lo]
                dve.wait_ge(e_exp.sem, e_exp.at(l, n + 1))
                dve.wait_ge(m_used.sem, m_used.at(l, max(n - 1, 0)))
                if u < 2 * SSD_H:
                    nc.vector.scalar_tensor_tensor(out=m, in0=e, scalar=cols[rw, j, C_DT + r:C_DT + r + 1],
                                                   in1=cb(hd // (SSD_H // SSD_G), j, lo, hi, rw), op0=ALU.mult,
                                                   op1=ALU.mult).then_inc(m_ready.sem, 1)
                else:
                    dve.wait_ge(qk_ps.sem, qk_ps.at(l, n - STEPS_SSD + 1))
                    nc.vector.scalar_tensor_tensor(out=like(m, hi - lo), in0=like(e, hi - lo), scalar=ML_QK ** -0.5,
                                                   in1=span(1, hi - lo, rw), op0=ALU.mult, op1=ALU.mult).then_inc(m_ready.sem, 1)

            def ssd_head(l, hd):
                dve.wait_ge(m_used.sem, m_used.at(l, (hd + 1) * 2 * NT))
                c = slice(hd * SSD_P, (hd + 1) * SSD_P)
                nc.vector.scalar_tensor_tensor(out=o_tok[:, :, c], in0=x_tok[:, :, c], scalar=par_at(l, "ssd_d", hd),
                                               in1=pb[:, 6 + hd % 2, 0:NT * SSD_P].rearrange("p (i v) -> p i v", v=SSD_P),
                                               op0=ALU.mult, op1=ALU.add).then_inc(y_evac.sem, 1)

            def ml_unit(l, v):
                hd, d, _ = unit(2 * SSD_H + v)
                dve.wait_ge(m_used.sem, m_used.at(l, STEPS_SSD + (v + 1) * NT))
                b = 4
                nc.vector.tensor_copy(den[:, 0:3], pb[:, b, ML_V:3 * (ML_V + 1):ML_V + 1])
                link(nc.vector.tensor_copy(den[:, 3:5], pb[:, b + 1, ML_V:2 * (ML_V + 1):ML_V + 1]))
                link(nc.vector.scalar_tensor_tensor(out=den2[:, :], in0=den[:, :], scalar=-1.0, in1=den[:, :], op0=ALU.mult, op1=ALU.max))
                link(nc.vector.tensor_tensor(den[:, :], den2[:, :], enm[:, :, d * ML_H + hd], ALU.max))
                link(nc.vector.reciprocal(den2[:, :], den[:, :]))
                for i in range(NT):
                    num = pb[:, b + i // 3, (i % 3) * (ML_V + 1):(i % 3) * (ML_V + 1) + ML_V]
                    o = o_ml[:, i, hd * ML_V:(hd + 1) * ML_V]
                    if d == 0:
                        ins = nc.vector.tensor_scalar(o, num, den2[:, i:i + 1], None, ALU.mult)
                    else:
                        ins = nc.vector.scalar_tensor_tensor(out=o, in0=num, scalar=den2[:, i:i + 1], in1=o, op0=ALU.mult, op1=ALU.add)
                ins.then_inc(nd_evac.sem, 1)
                dve.wait_ge(nd_evac.sem, nd_evac.at(l, v + 1))

            def out_sums(l, which, groups):
                for i in range(NT):
                    dve.wait_ge(osq.sem, osq.at(l, which * NT + i + 1))
                    nc.vector.reduce_sum(hs[:, i * groups:(i + 1) * groups],
                                         ebuf[:, i % 2, 0:512].rearrange("p (g v) -> p g v", g=groups), axis=AX.X).then_inc(ored.sem, 1)

            def out_scales(l, which, groups, buf):
                dve.wait_ge(orstd.sem, orstd.at(l, which + 1))
                for i in range(NT):
                    o = buf[:, i, :].rearrange("p (g v) -> p g v", g=groups)
                    if groups == 1:
                        nc.vector.tensor_scalar(buf[:, i, :], buf[:, i, :], hs[:, i:i + 1], None, ALU.mult).then_inc(oscaled.sem, 1)
                    else:
                        nc.vector.tensor_tensor(o, o, hs[:, i * groups:(i + 1) * groups].unsqueeze(2).to_broadcast([P, groups, 512 // groups]),
                                                ALU.mult).then_inc(oscaled.sem, 1)

            def row_max(l, n):
                scale = att(n)[4]
                dve.wait_ge(s_ps.sem, s_ps.at(l, n + 1))
                dve.wait_ge(p_ready.sem, p_ready.at(l, max(n - 1, 0)))
                link(nc.vector.tensor_reduce(rowmax[:, n % 2:n % 2 + 1], pair(n % 2), AX.XY, ALU.max))
                nc.vector.tensor_scalar(negmax[:, n % 2:n % 2 + 1], rowmax[:, n % 2:n % 2 + 1], -scale, None,
                                        ALU.mult).then_inc(max_ready.sem, 1)

            def turned_tail(l, n):
                dve.wait_ge(tail_ps.sem, tail_ps.at(l, n + 1))
                dve.wait_ge(o_ps.sem, o_ps.at(l, max(n - 1, 0)))
                w = TILES[-1][1]
                nc.vector.tensor_copy(mbuf[0:w, n % 2, 512:WIDE], pb[0:w, TAIL_O, 0:P]).then_inc(pt_tail.sem, 1)

            def att_out(l, n):
                _, _, _, dv, _, i, hd = att(n)
                r = rsum[:, n % 2:n % 2 + 1]
                dve.wait_ge(p_ready.sem, p_ready.at(l, n + 1))
                link(nc.vector.reciprocal(r, sums[:, n % 4:n % 4 + 1]))
                src = pb[:, TAIL_O, P:P + dv]
                if n < N_ATT_M:
                    dve.wait_ge(o_ps.sem, o_ps.at(l, n + 1))
                    nc.vector.tensor_scalar(o_tok[:, i, hd * dv:(hd + 1) * dv], src, r, None, ALU.mult).then_inc(o_evac.sem, 1)
                else:
                    o = o_dif[:, i, (hd // 2) * dv:(hd // 2 + 1) * dv]
                    if hd % 2 == 0:
                        dve.wait_ge(o_ps.sem, o_ps.at(l, n + 1))
                        nc.vector.tensor_scalar(o, src, r, None, ALU.mult).then_inc(o_evac.sem, 1)
                    else:
                        link(nc.vector.tensor_tensor(r, r, neg_lam[:, :], ALU.mult))
                        dve.wait_ge(o_evac.sem, o_evac.at(l, n - NT + 1))
                        dve.wait_ge(o_ps.sem, o_ps.at(l, n + 1))
                        nc.vector.scalar_tensor_tensor(out=o, in0=src, scalar=r, in1=o, op0=ALU.mult, op1=ALU.add).then_inc(o_evac.sem, 1)

            nc.vector.memset(eps[:, :], EPS).then_inc(eps_ready.sem, 1)
            dve.wait_ge(par_in.sem, 16)
            for l in range(DEPTH):
                if l:
                    dve.wait_ge(w_used.sem, w_used.at(l, 0))
                for k in range(KD):
                    if l == 0:
                        dve.wait_ge(x_in[k].sem, 16)
                    else:
                        dve.wait_ge(evac.sem, evac.at(l - 1, G_FOUT + k + 1))
                    gains(l, k, "attn_g", xg_parts)
                    if l and k == 1:
                        add_square(l, 0, KD - 1)
                if l == 0:
                    for k in range(KD):
                        add_square(l, 0, k)
                dve.wait_ge(rs_ready.sem, rs_ready.at(l, RS_A + 1))
                d24 = slice(0, NDEC)
                for g in range(G_SSD):
                    scale_out(l, g, tile_of(proj, g))
                    if g < 6:
                        dve.wait_ge(evac.sem, evac.at(l, g + 1))
                        conv(l, g)
                    if g == MISC:
                        dve.wait_ge(table_in.sem, 16)
                        dve.wait_ge(evac.sem, evac.at(l, MISC + 1))
                        nc.vector.tensor_scalar(ebuf[d24, 0, :], tile_of(proj, MISC, rows_=d24), par_at(l, "bias", rows_=d24),
                                                C("sign", d24), ALU.add, ALU.mult).then_inc(dec_u.sem, 1)
                        lam = par_at(l, "lam", 0, 4 * DIFF_QK).rearrange("p (a b) -> p a b", b=DIFF_QK)
                        link(nc.vector.tensor_tensor(lam_p[:, :, :], lam[:, 0:4:2, :], lam[:, 1:4:2, :], ALU.mult))
                        nc.vector.reduce_sum(lam_s[:, :], lam_p[:, :, :], axis=AX.X).then_inc(lam_sum.sem, 1)
                    if g == MISC + 3:
                        dve.wait_ge(conv_act.sem, conv_act.at(l, 6))
                        dve.wait_ge(cleared.sem, 5)
                        dve.wait_ge(dec_ln.sem, dec_ln.at(l, 1))
                        u, ln = ebuf[d24, 0, :], ebuf[d24, 1, :]
                        dec, sp, ig = kh[d24, 0, :], mbuf[d24, 1, 0:T], kh[d24, 1, :]
                        link(nc.vector.scalar_tensor_tensor(out=sp, in0=u, scalar=0.0, in1=ln, op0=ALU.max, op1=ALU.add))
                        link(nc.vector.tensor_scalar(dec, sp, ea[d24, :], -1.0, ALU.mult, ALU.mult))
                        link(nc.vector.tensor_copy(ig, tile_of(proj, MISC, rows_=slice(32, 32 + NDEC))))
                        link(nc.vector.tensor_scalar(ig, ig, par_at(l, "i_bias", rows_=d24), None, ALU.add))
                        link(nc.vector.memset(ebuf[d24, 0, :], 0.0))
                        zero = ebuf[d24, 0, :]
                        link(nc.vector.tensor_tensor_scan(rows[0:NDEC, :], dec, zero, 0.0, ALU.add, ALU.add))
                        link(nc.vector.tensor_tensor_scan(rows[32:32 + NDEC, ::-1], dec[:, ::-1], zero, 0.0, ALU.add, ALU.add))
                        link(nc.vector.tensor_tensor_scan(rows[64:64 + NDEC, :], dec, ig, NEG, ALU.add, ALU.max))
                        nc.vector.tensor_tensor_scan(rows[96:96 + NDEC, ::-1], dec[:, ::-1], ig[:, ::-1], NEG, ALU.add,
                                                     ALU.max).then_inc(rows_ready.sem, 1)
                        dve.wait_ge(rows_ready.sem, rows_ready.at(l, 1))
                        dve.wait_ge(lam_exp.sem, lam_exp.at(l, 1))
                        link(nc.vector.scalar_tensor_tensor(out=neg_lam[:, :], in0=lam_e[:, 0:1], scalar=-1.0, in1=lam_e[:, 1:2],
                                                            op0=ALU.mult, op1=ALU.add))
                        link(nc.vector.tensor_tensor(neg_lam[:, :], neg_lam[:, :], par_at(l, "lambda_init", 0), ALU.subtract))
                        link(nc.vector.tensor_tensor(gain_d[:, :], par_at(l, "diff_out_g"), par_at(l, "lambda_init", 1), ALU.mult))

                dve.wait_ge(cols_ps.sem, cols_ps.at(l, 1))
                nc.vector.tensor_copy(cols[:, 0:NT - 1, :], pb[:, 7, 0:(NT - 1) * NCOL].rearrange("p (i c) -> p i c", c=NCOL))
                nc.vector.tensor_copy(cols[0:TILES[-1][1], NT - 1, :], pb[0:TILES[-1][1], 7, (NT - 1) * NCOL:NT * NCOL]).then_inc(cols_ready.sem, 1)
                dve.wait_ge(cols_ready.sem, cols_ready.at(l, 1))
                for i in range(NT):
                    from_transposes(l, TR_X + i, x_tok[0:TILES[i][1], i, :], i, op=copy)
                exponents(l, 0)
                for g in range(SSD_G):
                    for j, (_, w) in enumerate(TILES):
                        dve.wait_ge(cb_ps.sem, cb_ps.at(l, g * NT + j + 1))
                        nc.vector.tensor_copy(halves(cb(g, j, 0, T, slice(0, w))), pair(1 + (g * NT + j) % 2, slice(0, w))).then_inc(cb_ready.sem, 1)
                dve.wait_ge(cb_ready.sem, cb_ready.at(l, 2 * NT))
                sines = kh[:, 0, :]
                for n in range(STEPS_SSD):
                    u, j = n // NT, n % NT
                    if n + 1 < STEPS_SSD:
                        exponents(l, n + 1)
                    weights(l, n)
                    if j == 1 and u >= 1:
                        scale_out(l, DQ + u - 1, tile_of(proj, DQ + u - 1))
                    if j == 2 and u % 2 == 0 and u:
                        ssd_head(l, u // 2 - 1)
                    if j == 0 and 0 <= u - 3 < 8:
                        t = u - 3
                        dve.wait_ge(rs_ready.sem, rs_ready.at(l, RS_D + t + 1))
                        normed(l, tile_of(proj, DQ + t), par_at(l, "dq_g" if t < 4 else "dk_g"))
                    if j == 1 and 0 <= u - 4 < 8:
                        t = u - 4
                        dve.wait_ge(rot_ready.sem, rot_ready.at(l, t + 1))
                        nc.vector.tensor_tensor(halves(sines), pair(1), halves(C("sin_d")), ALU.mult).then_inc(rot_used.sem, 1)
                    if j == 2 and 0 <= u - 4 < 8:
                        t = u - 4
                        dve.wait_ge(rot_used.sem, rot_used.at(l, t + 1))
                        dve.wait_ge(qcos.sem, qcos.at(l, t + 1))
                        nc.vector.tensor_tensor(tile_of(proj, DQ + t), tile_of(proj, DQ + t), sines, ALU.add).then_inc(roped.sem, 1)
                scale_out(l, G_ML - 1, tile_of(proj, G_ML - 1))
                ssd_head(l, SSD_H - 1)
                dve.wait_ge(z_act.sem, z_act.at(l, 4))
                dve.wait_ge(m_ready.sem, m_ready.at(l, STEPS_SSD))
                for i in range(NT):
                    def gated(dst, src):
                        return nc.vector.tensor_tensor(dst, src, dst, ALU.mult)
                    from_transposes(l, TR_OS + i, feature_block(proj, ZT, i), i, True, gated)
                nc.vector.memset(v_ml[:, :, :, ML_V], 1.0)
                for i in range(NT):
                    def by_head(dst, src):
                        return nc.vector.tensor_copy(dst, src.rearrange("p (h v) -> p h v", v=ML_V))
                    from_transposes(l, TR_MV + i, v_ml[0:TILES[i][1], i, :, 0:ML_V], i, op=by_head)

                dve.wait_ge(enm_ready.sem, enm_ready.at(l, 1))
                exponents(l, STEPS_SSD)
                for n in range(STEPS_SSD, STEPS):
                    if n + 1 < STEPS:
                        exponents(l, n + 1)
                    weights(l, n)
                    v, j = (n - STEPS_SSD) // NT, n % NT
                    if n == STEPS_SSD:
                        dve.wait_ge(rs_ready.sem, rs_ready.at(l, RS_S + 1))
                        for f in range(4):
                            normed(l, tile_of(proj, ZT + f), par_at(l, "ssd_g", f), count=(f == 3))
                    if j == 0 and v >= 1:
                        ml_unit(l, v - 1)
                    if j == 1 and v >= 1:
                        scale_out(l, G_ML + v - 1, tile_of(proj, G_ML + v - 1))
                    if v - 1 in JOB_UNITS and j == 1:
                        s0, tiles, norm = JOB_UNITS[v - 1]
                        dve.wait_ge(rs_ready.sem, rs_ready.at(l, norm + 1))
                        t0, gain = (CQ, "q_g") if norm == RS_C else (CKV, "kv_g")
                        for c in range(tiles):
                            normed(l, tile_of(proj, t0 + c), par_at(l, gain, c), count=(c == tiles - 1))
                ml_unit(l, 2 * ML_H - 1)
                scale_out(l, N_IN - 2, tile_of(proj, N_IN - 2))
                out_sums(l, 0, ML_H)
                scale_out(l, N_IN - 1, tile_of(proj, N_IN - 1))
                def value(i):
                    w = TILES[i][1]
                    dve.wait_ge(v_ps.sem, v_ps.at(l, i + 1))
                    nc.vector.tensor_copy(v_mla[0:w, i, :], pb[0:w, 4 + i % 2, :]).then_inc(v_ready.sem, 1)

                rws, kr = slice(0, MLA_ROWS), slice(MLA_NOPE, MLA_ROWS)

                def prep(stage, hd):
                    side = stage // 3
                    e = 2 * hd + side
                    buf = (qh, kh)[side]
                    if stage in (1, 3):
                        dve.wait_ge(s_ps.sem, s_ps.at(l, max(hd - 1, 0) * NT))
                        dve.wait_ge(p_ps.sem, p_ps.at(l, e + 1))
                        if side == 1:
                            nc.vector.tensor_copy(buf[kr, hd % 2, 0:T], tile_of(proj, MISC, rows_=kr))
                        m = slice(0, MLA_ROWS if side == 0 else MLA_NOPE)
                        nc.vector.tensor_copy(halves(buf[m, hd % 2, 0:T]), pair(3, m)).then_inc(p_copy.sem, 1)
                        dve.wait_ge(p_copy.sem, p_copy.at(l, e + 1))
                    elif stage in (2, 4):
                        dve.wait_ge(rs_ready.sem, rs_ready.at(l, RS_M + e + 1))
                        normed(l, buf[rws, hd % 2, 0:T], par_at(l, ("qh_g", "kh_g")[side], rows_=rws), rws)

                def mlstm_turned(i):
                    def gate(dst, src):
                        return nc.vector.scalar_tensor_tensor(out=dst, in0=src, scalar=par_at(l, "ml_out_g"), in1=dst,
                                                              op0=ALU.mult, op1=ALU.mult)
                    if i == 0:
                        dve.wait_ge(o_sig.sem, o_sig.at(l, 4))
                    from_transposes(l, TR_OM + i, feature_block(proj, MO, i), i, True, gate)

                def value_and_scales(i):
                    value(i)
                    if i == 1:
                        out_scales(l, 0, ML_H, o_ml)
                opening(value_and_scales, mlstm_turned, prep)
                row_max(l, 0)
                for n in range(N_ATT_M):
                    hd, i = n // NT, n % NT
                    if n + 1 < N_ATT_M:
                        row_max(l, n + 1)
                    turned_tail(l, n)
                    prepare(prep, n, (1, 3))
                    if n >= 1:
                        att_out(l, n - 1)
                    prepare(prep, n, (2, 4))
                att_out(l, N_ATT_M - 1)
                residual(l, G_OUT1, 0)
                for i in range(NT):
                    from_transposes(l, TR_DV + i, v_dif[0:TILES[i][1], i, :], i, op=copy)
                out_sums(l, 1, 1)
                out_scales(l, 1, 1, o_tok)
                residual(l, G_OUT1 + 1, 1)
                for i in range(NT):
                    def by_gain(dst, src, i=i):
                        return nc.vector.tensor_tensor(dst, src, par_at(l, "mla_out_g", 0, 4).unsqueeze(2).to_broadcast([P, 4, TILES[i][1]]), ALU.mult)
                    from_transposes(l, TR_OA + i, feature_block(proj, CQ, i), i, True, by_gain)

                row_max(l, N_ATT_M)
                for n in range(N_ATT_M, N_ATT):
                    if n + 1 < N_ATT:
                        row_max(l, n + 1)
                    turned_tail(l, n)
                    g, k = out1_part(n)
                    if k == KD - 1:
                        residual(l, G_OUT1 + g, g)
                    if n > N_ATT_M:
                        att_out(l, n - 1)
                att_out(l, N_ATT - 1)
                out_sums(l, 2, DIFF_H)
                out_scales(l, 2, DIFF_H, o_dif)
                residual(l, G_OUT2 - 1, KD - 1)
                for i in range(NT):
                    def scaled(dst, src):
                        return nc.vector.tensor_scalar(dst, src, gain_d[:, :], None, ALU.mult)
                    from_transposes(l, TR_OD + i, feature_block(proj, DV, i), i, True, scaled)
                dve.wait_ge(tr_evac.sem, tr_evac.at(l, TR_OD + NT))
                dve.wait_ge(mixed.sem, mixed.at(l, KD + 4))
                for k in range(KD + 4, KM):
                    mixed_split(l, k)

                for k in range(KD):
                    residual(l, G_OUT2 + k, k)
                    dve.wait_ge(evac.sem, evac.at(l, G_OUT2 + k + 1))
                    gains(l, k, "ffn_g", ffn_parts)
                    add_square(l, 1, k)

                dve.wait_ge(rs_ready.sem, rs_ready.at(l, RS_F + 1))
                for j in range(KF):
                    if j >= 2:
                        dve.wait_ge(act_ready.sem, act_ready.at(l, j - 1))
                    scale_out(l, G_FIN + 2 * j, ebuf[:, j % 2, :])
                    scale_out(l, G_FIN + 2 * j + 1, mbuf[:, j % 2, 0:T])
                    dve.wait_ge(gsilu.sem, gsilu.at(l, j + 1))
                    dve.wait_ge(evac.sem, evac.at(l, G_FIN + 2 * j + 2))
                    prod = ebuf[:, j % 2, :]
                    link(nc.vector.tensor_tensor(prod, prod, mbuf[:, j % 2, 0:T], ALU.mult))
                    lead, rest = act_parts(j)
                    link(nc.vector.tensor_copy(lead, prod))
                    nc.vector.tensor_tensor(rest, prod, lead.bitcast(FP32), ALU.subtract).then_inc(act_ready.sem, 1)
                for k in range(KD):
                    residual(l, G_FOUT + k, k)
                    if l + 1 < DEPTH and k:
                        add_square(l + 1, 0, k - 1)


def _columns():
    cq, ckv, kr, z = 0, 384, 640, 672
    xbc, dt, dq = 1184, 1952, 1968
    dk, dv, mq, mk, mv, mo, mi, mf = 2480, 2992, 3504, 3760, 4016, 4528, 5040, 5048
    run = lambda a, n: list(range(a, a + n))
    misc = run(dt, 16) + run(mf, 8) + [-1] * 8 + [-1] * 16 + run(mi, 8) + [-1] * 8 + run(kr, 16) + [-1] * 16 + run(kr + 16, 16) + [-1] * 16
    return np.array(run(xbc, 768) + misc + run(z, 512) + run(mo, 512) + run(dq, 512) + run(dk, 512) + run(mq, 256)
                    + run(mk, 256) + run(mv, 512) + run(cq, 384) + run(ckv, 256) + run(dv, 512))


_HALF = MLA_ROPE // 2
_HEAD = np.array(list(range(MLA_ROPE, MLA_QK)) + list(range(_HALF)) + [MLA_QK] * 16 + list(range(_HALF, MLA_ROPE)))


def _padded(x):
    return np.concatenate([x, np.zeros(x.shape[:-1] + (1,), x.dtype)], -1)[..., _HEAD]


def _weights(w_in, w_uq, w_ukv, w_out, w_fi, w_fo):
    f = np.float32
    ws = np.zeros((DEPTH, N_RAW, P, SLOT), f)
    heads = np.zeros((DEPTH, 4, P, SLOT), f)
    cols = _columns()
    v_at = N_IN
    order = np.r_[4:8, 12:16, 0:4, 8:12]
    for l in range(DEPTH):
        wi = np.concatenate([w_in[l], np.zeros((D_MODEL, 1), f)], 1)[:, cols]
        tiles = lambda w, kt: w.reshape(kt, P, -1, P).transpose(2, 1, 0, 3)
        ws[l, 0:N_IN] = tiles(wi, KD).reshape(N_IN, P, SLOT)
        kv = w_ukv[l].reshape(2, P, MLA_H, MLA_NOPE + MLA_V)
        ws[l, v_at] = kv[..., MLA_NOPE:].transpose(1, 0, 2, 3).reshape(P, SLOT)
        heads[l, 0] = kv[..., :MLA_NOPE].transpose(1, 2, 0, 3).reshape(P, SLOT)
        uq = _padded(w_uq[l].reshape(3, P, MLA_H, MLA_QK)).transpose(2, 1, 0, 3).reshape(MLA_H, P, 3 * MLA_ROWS)
        for hd in range(MLA_H):
            o = (hd % UQ_HEADS) * 3 * MLA_ROWS
            heads[l, 1 + hd // UQ_HEADS, :, o:o + 3 * MLA_ROWS] = uq[hd]
        dense = ws[l, v_at + 1 - N_IN:]
        wo = tiles(w_out[l], KM)[:, :, order].reshape(KD, P, 2, SLOT)
        dense[S_OUT1:S_OUT2], dense[S_OUT2:S_FIN] = wo[:, :, 0], wo[:, :, 1]
        fi = tiles(w_fi[l], KD).reshape(2, KF, P, SLOT)
        dense[S_FIN:S_FOUT] = fi.transpose(1, 0, 2, 3).reshape(2 * KF, P, SLOT)
        fo = tiles(w_fo[l], KF).reshape(KD, P, KF * P)
        pad = np.zeros((KD, P, 3 * SLOT), f)
        pad[:, :, :KF * P] = fo
        dense[S_FOUT:] = pad.reshape(KD, P, 3, SLOT).transpose(0, 2, 1, 3).reshape(3 * KD, P, SLOT)
    return ws.reshape(DEPTH * N_RAW, P, SLOT), heads.reshape(DEPTH * 4, P, SLOT)


def _params(a):
    f = np.float32
    out = np.zeros((P, DEPTH, N_PARAM), f)

    def put(name, v, rows_=P):
        s, e = PARAM[name]
        for l in range(DEPTH):
            out[0:rows_, l, s:e] = v(l)

    tiled = lambda x, n: x.reshape(n, P).T
    put("attn_g", lambda l: tiled(a["attn_norm_g"][l], KD))
    put("ffn_g", lambda l: tiled(a["ffn_norm_g"][l], KD))
    put("q_g", lambda l: tiled(a["mla_q_norm_g"][l], 3))
    put("kv_g", lambda l: tiled(a["mla_kv_norm_g"][l], 2))
    put("qh_g", lambda l: _padded(a["mla_q_head_g"][l])[:, None], MLA_ROWS)
    put("kh_g", lambda l: _padded(a["mla_k_head_g"][l])[:, None], MLA_ROWS)
    put("mla_out_g", lambda l: tiled(a["mla_out_g"][l], 4))
    put("conv_w", lambda l: a["ssd_conv_w"][l].reshape(TAPS, 6, P).transpose(2, 1, 0).reshape(P, 6 * TAPS))
    put("conv_b", lambda l: tiled(a["ssd_conv_b"][l], 6))
    put("ssd_g", lambda l: tiled(a["ssd_norm_g"][l], 4))
    put("ssd_d", lambda l: np.broadcast_to(a["ssd_d"][l][None], (P, SSD_H)))
    put("dq_g", lambda l: np.concatenate([a["diff_q_head_g"][l]] * 2)[:, None])
    put("dk_g", lambda l: np.concatenate([a["diff_k_head_g"][l]] * 2)[:, None])
    put("diff_out_g", lambda l: a["diff_out_g"][l][:, None])
    put("ml_out_g", lambda l: a["mlstm_out_g"][l][:, None])
    z8, z16 = np.zeros(8, f), np.zeros(16, f)
    put("bias", lambda l: np.concatenate([a["ssd_dt_bias"][l].ravel(), a["mlstm_f_bias"][l].ravel()])[:, None], NDEC)
    put("a_log", lambda l: np.concatenate([a["ssd_a_log"][l].ravel(), z8])[:, None], NDEC)
    put("i_bias", lambda l: np.concatenate([z16, a["mlstm_i_bias"][l].ravel()])[:, None], NDEC)
    put("lam", lambda l: np.broadcast_to(a["diff_lambda"][l].reshape(1, -1), (P, 4 * DIFF_QK)))
    init = [0.8 - 0.6 * float(np.exp(-0.3 * l)) for l in range(DEPTH)]
    put("lambda_init", lambda l: np.array([[init[l], 1.0 - init[l]]], f))
    return out


def _rope(rot, starts):
    f = np.float32
    r = rot // 2
    inv = (1.0 / (f(500000.0) ** (np.arange(0, rot, 2, dtype=f) / f(rot)))).astype(f)
    ang = (np.arange(T, dtype=f)[:, None] * inv[None, :]).astype(f)
    c, s = np.cos(ang).astype(f).T, np.sin(ang).astype(f).T
    cos, sin, perm = np.ones((P, T), f), np.zeros((P, T), f), np.zeros((P, P), f)
    for a in starts:
        cos[a:a + r], cos[a + r:a + rot] = c, c
        sin[a:a + r], sin[a + r:a + rot] = s, s
        for k in range(r):
            perm[a + r + k, a + k] = -1.0
            perm[a + k, a + r + k] = 1.0
    return cos, sin, perm


def _constants():
    f = np.float32
    out = np.zeros((P, N_CONST), f)

    def put(name, v):
        s, e = CONST[name]
        out[0:v.shape[0], s:e] = v

    put("ones", np.ones((P, P), f))
    put("ident", np.eye(P, dtype=f))
    put("ones_h", np.kron(np.eye(2, dtype=f), np.ones((64, 64), f)))
    key, query = np.arange(P)[:, None], np.arange(P)[None, :]
    put("mask", np.concatenate([np.where(query >= key, 0, NEG), np.zeros((P, 4 * P)), np.where(query <= key, 0, NEG)], 1).astype(f))
    cos, sin, perm = _rope(DIFF_ROPE, (0, 64))
    put("cos_d", cos), put("sin_d", sin), put("perm_d", perm)
    cos, sin, _ = _rope(MLA_ROPE, (MLA_NOPE,))
    for a, b, t in ((64, 64, 1.0), (96, 80, -1.0)):
        out[a:a + 16, slice(*CONST["cos_m"])] = cos[b:b + 16]
        out[a:a + 16, slice(*CONST["sin_m"])] = sin[b:b + 16] if t > 0 else np.negative(sin[b:b + 16])
    FW, BW, MF, MB = 0, 32, 64, 96
    sel, rs, ig, sp = (np.zeros((P, n), f) for n in (NDEC, NCOL, NCOL, NCOL))
    for r in range(NDEC):
        back = r // SSD_H if r < C_ML else (r - C_ML) // ML_H
        sel[(BW if back else FW) + r, r] = 1.0
        rs[(BW if back else FW) + r, r] = -1.0
        if r >= C_ML:
            sel[(MB if back else MF) + r, r] = -1.0
            ig[r, r] = 1.0
            rs[(MB if back else MF) + r, C_NM + r - C_ML] = -1.0
        else:
            sp[r, C_DT + r] = 1.0
    put("rowsel", sel), put("lin_rs", rs), put("lin_i", ig), put("lin_sp", sp)
    put("sign", np.array([[1.0]] * C_ML + [[-1.0]] * (NDEC - C_ML), f))
    return out


def kernel(**inputs):
    import concourse.bacc as _bacc
    from concourse.bass_utils import run_bass_kernel_spmd as _run

    a = {k: np.asarray(v) for k, v in inputs.items()}
    tokens = np.concatenate([a["meta_tokens"], a["x"][0]], 0)
    stream, heads = _weights(a["w_in"], a["mla_w_uq"], a["mla_w_ukv"], a["w_out"], a["w_ffn_in"], a["w_ffn_out"])
    arrays = {
        "x_t": np.ascontiguousarray(tokens.T.reshape(KD, P, T).transpose(1, 0, 2)),
        "w_stream": stream,
        "w_heads": heads,
        "params": _params(a),
        "consts": _constants(),
    }
    nc = _bacc.Bacc("TRN2", target_bir_lowering=False, num_devices=1, dynamic_dma_scratch_size=1024)
    args = [nc.dram_tensor(n, v.shape, FP32, kind="ExternalInput").ap() for n, v in arrays.items()]
    out = nc.dram_tensor("out_t", (P, KD, SEQ), FP32, kind="ExternalOutput").ap()
    trunk(nc, *args, out)
    r = _run(nc, [arrays], core_ids=[0])
    got = np.asarray(r.results[0]["out_t"])
    return np.ascontiguousarray(got.transpose(2, 1, 0).reshape(1, SEQ, D_MODEL))
```
